# Optimizing a Trainium2 kernel written in Bass

```python
import math
import jax, jax.numpy as jnp
from jax import lax
import numpy as np

D_MODEL = 1024
BATCH = 1
SEQ = 256
DEPTH = 2

N_BRANCH = 4
D_BRANCH = 256
S5_GROUP = 16
S5_GROUPS = D_BRANCH // S5_GROUP
S5_STATE = 64
HEAD_DIM = 64
FOX_HEADS = D_BRANCH // HEAD_DIM
SB_HEADS = D_BRANCH // HEAD_DIM
Q_BLOCK = 128
CONV_WIDTH = 31
D_FF = 2816
N_EXPERTS = 8
TOP_K = 2
D_FF_EXPERT = 2816
N_DENSE = (DEPTH + 1) // 2
N_MOE = DEPTH // 2
EPS = 1e-6

N_S5_IN = D_BRANCH
N_FOX_QKV = 3 * D_BRANCH
N_FOX_F = FOX_HEADS
N_CONV_IN = 2 * D_BRANCH
N_SB_QKV = 3 * D_BRANCH
N_GATES = N_BRANCH * D_MODEL
D_PROJ = N_S5_IN + N_FOX_QKV + N_FOX_F + N_CONV_IN + N_SB_QKV + N_GATES
SPLIT_POINTS = [N_S5_IN,
                N_S5_IN + N_FOX_QKV,
                N_S5_IN + N_FOX_QKV + N_FOX_F,
                N_S5_IN + N_FOX_QKV + N_FOX_F + N_CONV_IN,
                N_S5_IN + N_FOX_QKV + N_FOX_F + N_CONV_IN + N_SB_QKV]

kernel_name = "hybrid_s5_fox_conformer_stickbreak_moe"

def rms_norm(x, g):
    xf = x.astype(jnp.float32)
    y = xf * lax.rsqrt(jnp.mean(xf * xf, axis=-1, keepdims=True) + EPS)
    return (y * g.astype(jnp.float32)).astype(x.dtype)

def layer_norm(x, g, b):
    xf = x.astype(jnp.float32)
    mu = jnp.mean(xf, axis=-1, keepdims=True)
    var = jnp.mean(jnp.square(xf - mu), axis=-1, keepdims=True)
    y = (xf - mu) * lax.rsqrt(var + EPS)
    return (y * g.astype(jnp.float32) + b.astype(jnp.float32)).astype(x.dtype)

def split_heads(t, n_heads):
    b, l, _ = t.shape
    return t.reshape(b, l, n_heads, HEAD_DIM).transpose(0, 2, 1, 3)

def merge_blocks(o):
    nb, b, h, qb, dh = o.shape
    return o.transpose(1, 0, 3, 2, 4).reshape(b, nb * qb, h * dh)

def forgetting_attention(q, k, v, log_f):
    seq = q.shape[2]
    scale = 1.0 / math.sqrt(HEAD_DIM)
    cum = jnp.cumsum(log_f, axis=-1)
    kpos = jnp.arange(seq)

    def block(i):
        start = i * Q_BLOCK
        qb = lax.dynamic_slice_in_dim(q, start, Q_BLOCK, axis=2)
        cq = lax.dynamic_slice_in_dim(cum, start, Q_BLOCK, axis=2)
        qpos = start + jnp.arange(Q_BLOCK)
        s = jnp.einsum("bhqd,bhkd->bhqk", qb, k).astype(jnp.float32) * scale
        s = s + cq[..., :, None] - cum[..., None, :]
        causal = kpos[None, :] <= qpos[:, None]
        s = jnp.where(causal, s, -jnp.inf)
        p = jax.nn.softmax(s, axis=-1)
        return jnp.einsum("bhqk,bhkd->bhqd", p.astype(v.dtype), v)

    return merge_blocks(lax.map(block, jnp.arange(seq // Q_BLOCK)))

def stick_breaking_attention(q, k, v):
    seq = q.shape[2]
    scale = 1.0 / math.sqrt(HEAD_DIM)
    kpos = jnp.arange(seq)

    def block(i):
        start = i * Q_BLOCK
        qb = lax.dynamic_slice_in_dim(q, start, Q_BLOCK, axis=2)
        qpos = start + jnp.arange(Q_BLOCK)
        z = jnp.einsum("bhqd,bhkd->bhqk", qb, k).astype(jnp.float32) * scale
        past = kpos[None, :] < qpos[:, None]
        log_beta = jax.nn.log_sigmoid(z)
        log_keep = jnp.where(past, jax.nn.log_sigmoid(-z), 0.0)
        after = lax.cumsum(log_keep, axis=3, reverse=True) - log_keep
        a = jnp.where(past, jnp.exp(log_beta + after), 0.0)
        return jnp.einsum("bhqk,bhkd->bhqd", a.astype(v.dtype), v)

    return merge_blocks(lax.map(block, jnp.arange(seq // Q_BLOCK)))

def _s5_combine(e1, e2):
    a1r, a1i, b1r, b1i = e1
    a2r, a2i, b2r, b2i = e2
    return (a2r * a1r - a2i * a1i,
            a2r * a1i + a2i * a1r,
            a2r * b1r - a2i * b1i + b2r,
            a2r * b1i + a2i * b1r + b2i)

def s5_ssm(u, lam_re, lam_im, log_dt, b_re, b_im, c_re, c_im, d_skip):
    bsz, seq, _ = u.shape
    f32 = jnp.float32
    uf = u.astype(f32)
    ug = uf.reshape(bsz, seq, S5_GROUPS, S5_GROUP)
    lam_re, lam_im = lam_re.astype(f32), lam_im.astype(f32)
    dt = jnp.exp(log_dt.astype(f32))[:, None]
    mag = jnp.exp(lam_re * dt)
    ab_re = mag * jnp.cos(lam_im * dt)
    ab_im = mag * jnp.sin(lam_im * dt)
    nr, ni = ab_re - 1.0, ab_im
    den = lam_re * lam_re + lam_im * lam_im
    k_re = (nr * lam_re + ni * lam_im) / den
    k_im = (ni * lam_re - nr * lam_im) / den
    b_re, b_im = b_re.astype(f32), b_im.astype(f32)
    bb_re = k_re[..., None] * b_re - k_im[..., None] * b_im
    bb_im = k_re[..., None] * b_im + k_im[..., None] * b_re
    bu_re = jnp.einsum("blgh,gph->blgp", ug, bb_re)
    bu_im = jnp.einsum("blgh,gph->blgp", ug, bb_im)
    a_re = jnp.broadcast_to(ab_re, bu_re.shape)
    a_im = jnp.broadcast_to(ab_im, bu_im.shape)
    _, _, s_re, s_im = lax.associative_scan(_s5_combine, (a_re, a_im, bu_re, bu_im), axis=1)
    y = (jnp.einsum("blgp,ghp->blgh", s_re, c_re.astype(f32))
         - jnp.einsum("blgp,ghp->blgh", s_im, c_im.astype(f32)))
    y = y.reshape(bsz, seq, D_BRANCH) + d_skip.astype(f32) * uf
    return y.astype(u.dtype)

def conformer_conv(ab, w_dw, b_dw, ln_g, ln_b):
    a, b = jnp.split(ab, 2, axis=-1)
    u = a * jax.nn.sigmoid(b)
    u = lax.conv_general_dilated(u, w_dw[:, None, :], window_strides=(1,),
                                 padding=[(CONV_WIDTH - 1, 0)],
                                 dimension_numbers=("NWC", "WIO", "NWC"),
                                 feature_group_count=D_BRANCH) + b_dw
    u = layer_norm(u, ln_g, ln_b)
    return jax.nn.silu(u)

def swiglu(h, w1, w3, w2):
    return (jax.nn.silu(h @ w1) * (h @ w3)) @ w2

def moe_ffn(h, w_router, b_router, w1, w3, w2):
    bsz, seq, d = h.shape
    ht = h.reshape(bsz * seq, d)
    logits = ht.astype(jnp.float32) @ w_router.astype(jnp.float32) + b_router.astype(jnp.float32)
    top_val, top_idx = lax.top_k(logits, TOP_K)
    top_w = jax.nn.softmax(top_val, axis=-1)
    combine = jnp.sum(jax.nn.one_hot(top_idx, N_EXPERTS, dtype=jnp.float32) * top_w[..., None], axis=1)
    combine = combine.astype(h.dtype)
    y = jnp.zeros_like(ht)
    for e in range(N_EXPERTS):
        y = y + combine[:, e:e + 1] * swiglu(ht, w1[e], w3[e], w2[e])
    return y.reshape(bsz, seq, d)

def setup_inputs(seed: int = 0) -> dict:
    key = jax.random.key(seed)
    ks = jax.random.split(key, 40)
    f32 = jnp.float32

    def nrm(k, shape, scale):
        return jax.random.normal(k, shape, f32) * scale

    def gain(k, shape):
        return 1.0 + nrm(k, shape, 0.02)

    G, P, H = S5_GROUPS, S5_STATE, S5_GROUP
    lam_im_init = jnp.pi * jnp.arange(P, dtype=f32)
    return {
        "x": nrm(ks[0], (BATCH, SEQ, D_MODEL), 1.0),
        "g_mix": gain(ks[1], (DEPTH, D_MODEL)),
        "w_in": nrm(ks[2], (DEPTH, D_MODEL, D_PROJ), D_MODEL ** -0.5),
        "b_forget": jax.random.uniform(ks[3], (DEPTH, FOX_HEADS), f32, 1.0, 4.0),
        "fox_q_gain": gain(ks[4], (DEPTH, HEAD_DIM)),
        "fox_k_gain": gain(ks[5], (DEPTH, HEAD_DIM)),
        "sb_q_gain": gain(ks[6], (DEPTH, HEAD_DIM)),
        "sb_k_gain": gain(ks[7], (DEPTH, HEAD_DIM)),
        "s5_lam_re": -0.5 + nrm(ks[8], (DEPTH, G, P), 0.01),
        "s5_lam_im": lam_im_init + nrm(ks[9], (DEPTH, G, P), 0.01),
        "s5_log_dt": jax.random.uniform(ks[10], (DEPTH, G), f32, math.log(1e-3), math.log(1e-1)),
        "s5_b_re": nrm(ks[11], (DEPTH, G, P, H), (2 * H) ** -0.5),
        "s5_b_im": nrm(ks[12], (DEPTH, G, P, H), (2 * H) ** -0.5),
        "s5_c_re": nrm(ks[13], (DEPTH, G, H, P), P ** -0.5),
        "s5_c_im": nrm(ks[14], (DEPTH, G, H, P), P ** -0.5),
        "s5_d": nrm(ks[15], (DEPTH, D_BRANCH), 1.0),
        "s5_w_glu": nrm(ks[16], (DEPTH, D_BRANCH, D_BRANCH), D_BRANCH ** -0.5),
        "conv_w": nrm(ks[17], (DEPTH, CONV_WIDTH, D_BRANCH), CONV_WIDTH ** -0.5),
        "conv_b": nrm(ks[18], (DEPTH, D_BRANCH), 0.02),
        "conv_ln_g": gain(ks[19], (DEPTH, D_BRANCH)),
        "conv_ln_b": nrm(ks[20], (DEPTH, D_BRANCH), 0.02),
        "w_branch": nrm(ks[21], (DEPTH, N_BRANCH, D_BRANCH, D_MODEL), D_BRANCH ** -0.5),
        "w_out": nrm(ks[22], (DEPTH, D_MODEL, D_MODEL), D_MODEL ** -0.5),
        "g_ffn": gain(ks[23], (DEPTH, D_MODEL)),
        "ffn_w1": nrm(ks[24], (N_DENSE, D_MODEL, D_FF), D_MODEL ** -0.5),
        "ffn_w3": nrm(ks[25], (N_DENSE, D_MODEL, D_FF), D_MODEL ** -0.5),
        "ffn_w2": nrm(ks[26], (N_DENSE, D_FF, D_MODEL), D_FF ** -0.5),
        "router_w": nrm(ks[27], (N_MOE, D_MODEL, N_EXPERTS), D_MODEL ** -0.5),
        "router_b": nrm(ks[28], (N_MOE, N_EXPERTS), 0.01),
        "moe_w1": nrm(ks[29], (N_MOE, N_EXPERTS, D_MODEL, D_FF_EXPERT), D_MODEL ** -0.5),
        "moe_w3": nrm(ks[30], (N_MOE, N_EXPERTS, D_MODEL, D_FF_EXPERT), D_MODEL ** -0.5),
        "moe_w2": nrm(ks[31], (N_MOE, N_EXPERTS, D_FF_EXPERT, D_MODEL), D_FF_EXPERT ** -0.5),
    }

def reference(x, g_mix, w_in, b_forget, fox_q_gain, fox_k_gain, sb_q_gain, sb_k_gain,
              s5_lam_re, s5_lam_im, s5_log_dt, s5_b_re, s5_b_im, s5_c_re, s5_c_im, s5_d, s5_w_glu,
              conv_w, conv_b, conv_ln_g, conv_ln_b, w_branch, w_out, g_ffn,
              ffn_w1, ffn_w3, ffn_w2, router_w, router_b, moe_w1, moe_w3, moe_w2):
    bsz, seq = x.shape[0], x.shape[1]
    for i in range(DEPTH):
        h = rms_norm(x, g_mix[i])
        proj = h @ w_in[i]
        u_s5, qkv_f, f_logit, conv_ab, qkv_sb, gate_logit = jnp.split(proj, SPLIT_POINTS, axis=-1)

        y_s5 = s5_ssm(u_s5, s5_lam_re[i], s5_lam_im[i], s5_log_dt[i], s5_b_re[i], s5_b_im[i],
                      s5_c_re[i], s5_c_im[i], s5_d[i])
        y_s5 = jax.nn.gelu(y_s5)
        y_s5 = y_s5 * jax.nn.sigmoid(y_s5 @ s5_w_glu[i])

        qf, kf, vf = [split_heads(t, FOX_HEADS) for t in jnp.split(qkv_f, 3, axis=-1)]
        qf, kf = rms_norm(qf, fox_q_gain[i]), rms_norm(kf, fox_k_gain[i])
        log_f = jax.nn.log_sigmoid(f_logit.astype(jnp.float32) + b_forget[i].astype(jnp.float32))
        y_fox = forgetting_attention(qf, kf, vf, log_f.transpose(0, 2, 1))

        y_conv = conformer_conv(conv_ab, conv_w[i], conv_b[i], conv_ln_g[i], conv_ln_b[i])

        qs, ks_, vs = [split_heads(t, SB_HEADS) for t in jnp.split(qkv_sb, 3, axis=-1)]
        qs, ks_ = rms_norm(qs, sb_q_gain[i]), rms_norm(ks_, sb_k_gain[i])
        y_sb = stick_breaking_attention(qs, ks_, vs)

        ys = jnp.stack([y_s5.astype(x.dtype), y_fox.astype(x.dtype),
                        y_conv.astype(x.dtype), y_sb.astype(x.dtype)], axis=2)
        gates = jax.nn.sigmoid(gate_logit.reshape(bsz, seq, N_BRANCH, D_MODEL))
        merged = jnp.sum(gates * jnp.einsum("blnc,ncd->blnd", ys, w_branch[i]), axis=2)
        x = x + merged @ w_out[i]

        h = rms_norm(x, g_ffn[i])
        j = i // 2
        if i % 2 == 0:
            ffn = swiglu(h, ffn_w1[j], ffn_w3[j], ffn_w2[j])
        else:
            ffn = moe_ffn(h, router_w[j], router_b[j], moe_w1[j], moe_w3[j], moe_w2[j])
        x = x + ffn
    return x


_drawn_inputs = setup_inputs


def setup_inputs(seed=0):
    import zlib

    import numpy as np

    out = dict(_drawn_inputs(seed))
    spreads = {}
    factors = {'fox_q_gain': 8.0,
     'fox_k_gain': 4.346,
     'sb_q_gain': 8.0,
     'sb_k_gain': 8.0,
     's5_lam_re': 8.0,
     's5_c_im': 3.423,
     'router_b': 4.114}
    for name, (base, spread) in spreads.items():
        noise = np.random.default_rng([zlib.crc32(name.encode()), seed]).standard_normal(out[name].shape)
        drawn = base * np.exp(spread * noise) if base else spread * noise
        out[name] = __import__('jax').numpy.asarray(drawn.astype(out[name].dtype))
    for name, factor in factors.items():
        out[name] = (out[name] * factor).astype(out[name].dtype)
    return out
```

```python
from contextlib import ExitStack

import numpy as np

import concourse.bass as bass
from concourse import mybir

ALU = mybir.AluOpType
ACT = mybir.ActivationFunctionType
AX_X = mybir.AxisListType.X
F32 = mybir.dt.float32
F32R = mybir.dt.float32r
I32 = mybir.dt.int32
U32 = mybir.dt.uint32

P = 128
D = 1024
KT = D // P
SEQ = 256
NB = SEQ // P
DB = 256
CT = DB // P
HD = 64
NH = DB // HD
CONVW = 31
PAD = CONVW - 1
DFF = 2816
CH = 256
NCH = DFF // CH
NE = 8
EPS = 1e-6
BIG = 1e30
NG, GP, GH = 16, 64, 16
ST = NG // 2

IN_S5, IN_FOX, IN_F = 0, DB, 4 * DB
IN_CONV = IN_F + NH
IN_SB = IN_CONV + 2 * DB
IN_GATE = IN_SB + 3 * DB
D_PROJ = IN_GATE + 4 * D

UNIT = 2048
RING = 3
MIX_UNITS = 33
FFN_UNITS = 3 * NCH
assert MIX_UNITS % RING == 0 and FFN_UNITS % RING == 0

CONST = {}
_at = 0
for _name, _n in (("ident", P), ("tri", P), ("tri_strict", P), ("ones", P), ("later", P), ("suffix", P),
                  ("minus", P), ("mean", P), ("causal", P), ("past", P), ("keep", 3 * P), ("iota", P),
                  ("parity", 2), ("side", 2), ("iota8", NE)):
    CONST[_name] = (_at, _at + _n)
    _at += _n
N_CONST = _at

PARAM = {}
_at = 0
for _name, _n in (("g_mix", KT), ("g_ffn", KT), ("b_forget", NH), ("fox_q", 1), ("fox_k", 1), ("sb_q", 1),
                  ("sb_k", 1), ("lam_re", ST), ("lam_im", ST), ("log_dt", ST), ("b_re", ST * GH),
                  ("b_im", ST * GH), ("c_re", CT * GP), ("c_im", CT * GP), ("s5_d", CT),
                  ("conv_w", CT * CONVW), ("conv_b", CT), ("ln_g", CT), ("ln_b", CT), ("w_glu", CT * DB),
                  ("w_forget", KT * NH)):
    PARAM[_name] = (_at, _at + _n)
    _at += _n
N_PARAM = _at
N_ROUTER = KT * NE + NE

TWO_PI_1, TWO_PI_2 = 6.28125, 0.0019340515136719
TWO_PI_3 = 2 * np.pi - TWO_PI_1 - TWO_PI_2
ROUND = 1.5 * 2.0 ** 23
PI_F32 = 3.1415925


class Units:

    def __init__(self, base, steps=0):
        assert base % RING == 0
        self.base, self.steps = base // RING, steps

    def slot(self, j):
        return j % RING

    def earlier(self, j):
        return self.base + self.steps + j // RING

    def is_first(self, j):
        return isinstance(self.steps, int) and self.earlier(j) == 0


class Chain:

    def __init__(self, eng, sem):
        self.eng, self.sem, self.n, self.more = eng, sem, 0, 0

    def __call__(self, ins):
        self.n += 1
        ins.then_inc(self.sem, 1)
        self.eng.wait_ge(self.sem, self.more + self.n)

    def mark(self, ins):
        self.n += 1
        ins.then_inc(self.sem, 1)

    def settle(self):
        self.eng.wait_ge(self.sem, self.more + self.n)


def build(nc, x, consts, params, router, w_in, w_branch, w_out, ffn_w1, ffn_w3, ffn_w2, moe_w1, moe_w3, moe_w2,
          out, upto=99):
    with ExitStack() as ctx:
        def sb(name, shape, dt=F32):
            return ctx.enter_context(nc.sbuf_tensor(name, shape, dt))

        def sem(name):
            return ctx.enter_context(nc.semaphore(name))

        bank = [ctx.enter_context(nc.psum_tensor(f"bank{i}", [P, 512], F32)) for i in range(8)]

        raw = sb("raw", [P, RING, UNIT])
        high = sb("high", [P, RING, UNIT], F32R)
        low = sb("low", [P, RING, UNIT], F32R)
        X = sb("X", [P, NB, D])
        H = sb("H", [P, NB, D])
        G2 = sb("G2", [P, NB, D])
        M = sb("M", [P, NB, D])
        hT_hi = sb("hT_hi", [P, KT, SEQ], F32R)
        hT_lo = sb("hT_lo", [P, KT, SEQ], F32R)
        C = sb("C", [P, N_CONST])
        PR = sb("PR", [P, 2, N_PARAM])
        RT = sb("RT", [P, N_ROUTER])
        smallw_hi = sb("smallw_hi", [P, 2 * KT * NH + KT * NE], F32R)
        smallw_lo = sb("smallw_lo", [P, 2 * KT * NH + KT * NE], F32R)
        stat = sb("stat", [P, 8])
        rot_c = sb("rot_c", [P, ST, SEQ])
        rot_s = sb("rot_s", [P, ST, SEQ])
        s5p = sb("s5p", [P, 20, ST])
        s5b = sb("s5b", [P, 2, ST, 2, GH])
        s5c = sb("s5c", [P, 2, CT, 2, GP])
        BT = sb("BT", [P, 2, CT, P])
        CTt = sb("CTt", [P, 2, DB])
        uT = sb("uT", [P, CT, SEQ])
        bu = sb("bu", [P, ST, 2, SEQ])
        tmp = sb("tmp", [P, 4, 2 * SEQ])
        silu = bu[:, 0:2, :, :]
        gated_h = bu[:, 2:4, :, :]
        upad = G2[:, 0, 0:CT * (PAD + SEQ)].rearrange("p (a c) -> p a c", a=CT)
        ca = sb("ca", [P, CT, SEQ])
        cs = sb("cs", [P, CT, SEQ])
        lnv = sb("lnv", [P, 3, SEQ])
        qk = H[:, 0, :].rearrange("p (w b c) -> p w b c", w=2, b=NB)
        sq = G2[:, 1, :].rearrange("p (w b c) -> p w b c", w=2, b=NB)
        nrm = sb("nrm", [P, 2, 2, NB * NH])
        V = sb("V", [P, 2, NB, DB])
        qT = sb("qT", [P, 2, 2, CT, SEQ])
        lf = sb("lf", [P, 4, NB * NH])
        TL = M[:, :, :].rearrange("p a c -> p (a c)")[:, 0:NH * 3 * P].rearrange("p (h i c) -> p h i c", h=NH, i=3)
        sc = sb("sc", [P, 2, 3 * P])
        pT = sb("pT", [P, 2, 3 * P])
        mx = sb("mx", [P, 2, NH, 2])
        rs = sb("rs", [P, 2, NH, 2])
        route = sb("route", [P, 12, NB, NE])
        top_at = sb("top_at", [P, NB, NE], U32)
        spill = sb("spill", [P, 4, NE])
        spill_i = sb("spill_i", [1, 4], I32)
        ys_hi = sb("ys_hi", [P, 2, CT, SEQ], F32R)
        ys_lo = sb("ys_lo", [P, 2, CT, SEQ], F32R)

        def const(name, a=0, b=None, rows=P):
            lo_, hi_ = CONST[name]
            return C[0:rows, lo_ + a:(hi_ if b is None else lo_ + b)]

        def par(l, name, a=0, b=None):
            lo_, hi_ = PARAM[name]
            return PR[:, l, lo_ + a:(hi_ if b is None else lo_ + b)]

        ident = const("ident")

        raw_ready = [sem(f"raw_ready{s}") for s in range(RING)]
        hi_ready = [sem(f"hi_ready{s}") for s in range(RING)]
        lo_ready = [sem(f"lo_ready{s}") for s in range(RING)]
        used = [sem(f"used{s}") for s in range(RING)]
        loaded = sem("loaded")
        stored = sem("stored")
        act_step = sem("act_step")
        dve_step = sem("dve_step")
        small_hi = sem("small_hi")
        small_lo = sem("small_lo")
        squared = sem("squared")
        mean_sq = sem("mean_sq")
        rms_root = sem("rms_root")
        normed = sem("normed")
        turned = sem("turned")
        turned_hi = sem("turned_hi")
        turned_lo = sem("turned_lo")
        s5_exp = sem("s5_exp")
        s5_arg = sem("s5_arg")
        s5_sin = sem("s5_sin")
        s5_spread = sem("s5_spread")
        s5_turned = sem("s5_turned")
        s5_lhs = sem("s5_lhs")
        s5_rot = sem("s5_rot")
        forget_ready = sem("forget_ready")
        forget_in = sem("forget_in")
        forget_ln = sem("forget_ln")
        forget_tri = sem("forget_tri")
        taken = sem("taken")
        bu_ready = sem("bu_ready")
        bu_taken = sem("bu_taken")
        conv_sum = sem("conv_sum")
        conv_mean = sem("conv_mean")
        conv_cent = sem("conv_cent")
        conv_sq = sem("conv_sq")
        conv_var = sem("conv_var")
        conv_vare = sem("conv_vare")
        conv_root = sem("conv_root")
        conv_lin = sem("conv_lin")
        conv_tanh = sem("conv_tanh")
        conv_out = sem("conv_out")
        qk_mean = sem("qk_mean")
        qk_root = sem("qk_root")
        qk_normed = sem("qk_normed")
        qk_turned = sem("qk_turned")
        qk_gained = sem("qk_gained")
        score = sem("score")
        row_max = sem("row_max")
        p_exp = sem("p_exp")
        p_norm = sem("p_norm")
        p_turned = sem("p_turned")
        p_taken = sem("p_taken")
        fox_out = sem("fox_out")
        z_ready = sem("z_ready")
        z_ln = sem("z_ln")
        z_soft = sem("z_soft")
        z_cum = sem("z_cum")
        a_exp = sem("a_exp")
        sb_out = sem("sb_out")
        s5_state = sem("s5_state")
        s5_y = sem("s5_y")
        gelu_in = sem("gelu_in")
        gelu_tanh = sem("gelu_tanh")
        gelu_out = sem("gelu_out")
        glu_ready = sem("glu_ready")
        glu_tanh = sem("glu_tanh")
        glu_out = sem("glu_out")
        ys_high = sem("ys_high")
        ys_low = sem("ys_low")
        gate_ready = sem("gate_ready")
        gate_tanh = sem("gate_tanh")
        branch = sem("branch")
        gated = sem("gated")
        merged = sem("merged")
        silu_ready = sem("silu_ready")
        g_ready = sem("g_ready")
        g_turned = sem("g_turned")
        g_hi = sem("g_hi")
        g_lo = sem("g_lo")
        logits = sem("logits")
        top_gap = sem("top_gap")
        top_exp = sem("top_exp")
        chosen = sem("chosen")
        places = sem("places")
        routed = sem("routed")
        spill_known = sem("spill_known")
        picked = sem("picked")
        gathered = sem("gathered")
        pick_turned = sem("pick_turned")
        gather_hi = sem("gather_hi")
        gather_lo = sem("gather_lo")
        pick_taken = sem("pick_taken")
        y_taken = sem("y_taken")
        spread = sem("spread")
        added = sem("added")
        finished = sem("finished")
        x_mixed = sem("x_mixed")
        block = ctx.enter_context(nc.Block())

        ORDER = (2, 1, 3, 0)
        COLS = [IN_CONV, IN_CONV + DB, IN_S5] + [IN_FOX + DB * i for i in range(3)] + [IN_SB + DB * i for i in range(3)]
        mix_src = []

        def k_rows(w, k0, nk, c0, n):
            return w.rearrange("(k p) c -> p k c", p=P)[:, k0:k0 + nk, c0:c0 + n]

        for l in range(2):
            src = [k_rows(w_in[l], 0, KT, c, DB) for c in COLS]
            for n in ORDER:
                for half in range(2):
                    for kh in range(2):
                        src.append(k_rows(w_in[l], 4 * kh, 4, IN_GATE + n * D + half * 512, 512))
                src.append(k_rows(w_branch[l, n], 0, CT, 0, D))
            src += [k_rows(w_out[l], 2 * i, 2, 0, D) for i in range(4)]
            assert len(src) == MIX_UNITS
            mix_src.append(src)

        def unit_view(t, s, nk):
            return t[:, s, :].rearrange("p (k c) -> p k c", k=nk)

        BASE = [0, MIX_UNITS + FFN_UNITS]
        DENSE0 = MIX_UNITS
        MOE0 = 2 * MIX_UNITS + FFN_UNITS

        PAIRS = (NCH - 1) // 2
        N_SPILL = 2 * SEQ // (P + 1)
        expert_gain = (1, "g_ffn")

        def wait_products(eng, u, j):
            eng.wait_ge(used[u.slot(j)], u.earlier(j) + 1)

        @block.sync
        def _(sp):
            sp.dma_start(C[:, :], consts).then_inc(loaded, 16)
            sp.dma_start(PR[:, :, :], params.rearrange("p (l n) -> p l n", l=2)).then_inc(loaded, 16)
            sp.dma_start(RT[:, :], router).then_inc(loaded, 16)
            sp.dma_start(X[:, :, :], x.rearrange("a (b p) d -> p (a b) d", p=P)).then_inc(loaded, 16)

            def load(u, j, src):
                s = u.slot(j)
                if not u.is_first(j):
                    sp.wait_ge(lo_ready[s], u.earlier(j))
                sp.dma_start(unit_view(raw, s, src.shape[1]), src).then_inc(raw_ready[s], 16)

            def load_ffn(base, steps, w1, w3, w2):
                w1, w3 = (w.rearrange("(k p) n -> p k n", p=P) for w in (w1, w3))
                w2 = w2.rearrange("(c p) n -> p c n", p=P)
                u = Units(base, steps)
                load(u, 0, w1[:, :, 0:CH])
                load(u, 1, w3[:, :, 0:CH])
                with sp.Fori(0, PAIRS) as i:
                    u = Units(base, steps + i * 2)
                    for m in range(2):
                        load(u, 2 + 3 * m, w1[:, :, bass.ds(i * (2 * CH) + (1 + m) * CH, CH)])
                        load(u, 3 + 3 * m, w3[:, :, bass.ds(i * (2 * CH) + (1 + m) * CH, CH)])
                        load(u, 4 + 3 * m, w2[:, bass.ds(i * 4 + 2 * m, 2), :])
                load(Units(base, steps), FFN_UNITS - 1, w2[:, 2 * NCH - 2:2 * NCH, :])

            def load_expert(e, n):
                load_ffn(MOE0, n * NCH, moe_w1[0, e], moe_w3[0, e], moe_w2[0, e])

            for l in range(2):
                u = Units(BASE[l])
                for j, src in enumerate(mix_src[l]):
                    load(u, j, src)
                if l == 0 and upto > 1:
                    load_ffn(DENSE0, 0, ffn_w1[0], ffn_w3[0], ffn_w2[0])
                if upto <= 2 * l + 2:
                    break
            if upto >= 4:
                with sp.Fori(0, NE) as e:
                    load_expert(e, e)
                sp.wait_ge(spill_known, 1)
                n_spill = sp.value_load(spill_i[0:1, 0:1], min_val=0, max_val=N_SPILL)
                for t in range(N_SPILL):
                    with sp.If(n_spill > t):
                        load_expert(sp.value_load(spill_i[0:1, 1 + t:2 + t], min_val=0, max_val=NE - 1), NE + t)
                sp.wait_ge(finished, 1)
            else:
                sp.wait_ge(x_mixed, 4 * upto)
            sp.dma_start(out.rearrange("a (b p) d -> p (a b) d", p=P), X[:, :, :]).then_inc(stored, 16)
            sp.wait_ge(stored, 16)

        @block.gpsimd
        def _(pool):
            def split_low(u, j):
                s = u.slot(j)
                pool.wait_ge(hi_ready[s], u.earlier(j) + 1)
                pool.tensor_tensor(low[:, s, :], raw[:, s, :], high[:, s, :].bitcast(F32),
                                   ALU.subtract).then_inc(lo_ready[s], 1)

            for l in range(2):
                with pool.Fori(0, MIX_UNITS // RING) as i:
                    for j in range(RING):
                        split_low(Units(BASE[l], i), j)
                if l == 0 and upto > 1:
                    with pool.Fori(0, FFN_UNITS // RING) as i:
                        for j in range(RING):
                            split_low(Units(DENSE0, i), j)
                if upto <= 2 * l + 2:
                    break
            if upto >= 4:
                with pool.Fori(0, NE * NCH) as i:
                    split_low(Units(MOE0, i), 2)
                pool.wait_ge(spill_known, 1)
                n_spill = pool.value_load(spill_i[0:1, 0:1], min_val=0, max_val=N_SPILL)
                for t in range(N_SPILL):
                    with pool.If(n_spill > t):
                        with pool.Fori(0, NCH) as i:
                            split_low(Units(MOE0, (NE + t) * NCH + i), 2)

        @block.scalar
        def _(act):
            step = Chain(act, act_step)

            def split_high(u, j):
                s = u.slot(j)
                act.wait_ge(raw_ready[s], u.earlier(j) * 16 + 16)
                if not u.is_first(j):
                    act.wait_ge(used[s], u.earlier(j))
                act.activation(high[:, s, :], raw[:, s, :], ACT.Copy).then_inc(hi_ready[s], 1)

            def norm_rows(r):
                if r:
                    act.wait_ge(x_mixed, 4 * r)
                for b in range(NB):
                    act.activation(H[:, b, :], X[:, b, :], ACT.Square, accum_out=stat[:, b:b + 1]).then_inc(squared, 1)
                act.wait_ge(mean_sq, r + 1)
                act.activation(stat[:, 4:6], stat[:, 2:4], ACT.Sqrt).then_inc(rms_root, 1)

            def turn_high(t, base, gain):
                for k in range(KT):
                    if k % 2 == 0:
                        act.wait_ge(turned, 4 * t + k // 2 + 1)
                    act.activation(hT_hi[:, k, :], bank[base + k // 2][:, (k % 2) * SEQ:(k % 2 + 1) * SEQ], ACT.Copy,
                                   scale=0.5 if gain is None else gain[:, k:k + 1]).then_inc(turned_hi, 1)

            def s5_angles(l):
                a = [s5p[:, i, :] for i in range(20)]
                act.activation(a[0], par(l, "log_dt"), ACT.Exp).then_inc(s5_exp, 1)
                act.wait_ge(s5_arg, 2 * l + 1)
                act.activation(a[1], a[1], ACT.Exp).then_inc(s5_exp, 1)
                act.wait_ge(s5_arg, 2 * l + 2)
                act.activation(a[4], a[3], ACT.Sin).then_inc(s5_sin, 1)
                act.activation(a[5], a[3], ACT.Sin, scale=0.5).then_inc(s5_sin, 1)

            def s5_operands(l):
                act.wait_ge(s5_turned, 2 * l + 1)
                act.activation(BT[:, :, :, :].rearrange("p a b c -> p (a b c)"), bank[6][:, :],
                               ACT.Copy).then_inc(s5_lhs, 1)
                act.wait_ge(s5_turned, 2 * l + 2)
                act.activation(CTt[:, 0, :], bank[7][:, 0:DB], ACT.Copy).then_inc(s5_lhs, 1)
                act.activation(CTt[:, 1, :], bank[7][:, DB:2 * DB], ACT.Copy, scale=-1.0).then_inc(s5_lhs, 1)

            act.wait_ge(loaded, 64)
            nf = KT * NH
            for l in range(2):
                act.activation(smallw_hi[:, l * nf:(l + 1) * nf], par(l, "w_forget"), ACT.Copy).then_inc(small_hi, 1)
            act.activation(smallw_hi[:, 2 * nf:], RT[:, 0:KT * NE], ACT.Copy).then_inc(small_hi, 1)

            for l in range(2):
                mix = Units(BASE[l])
                after = None if upto <= 2 * l + 1 else Units(BASE[l] + MIX_UNITS)
                if l == 0:
                    for j in range(RING):
                        split_high(mix, j)
                norm_rows(2 * l)
                if l == 0:
                    s5_angles(0)
                turn_high(3 * l, 0, par(l, "g_mix"))

                act.wait_ge(forget_in, l + 1)
                step(act.activation(lf[:, 1, :], lf[:, 0, :], ACT.Abs))
                step(act.activation(lf[:, 2, :], lf[:, 1, :], ACT.Exp, scale=-1.0))
                act.activation(lf[:, 3, :], lf[:, 2, :], ACT.Ln, bias=1.0).then_inc(forget_ln, 1)

                def halves(b):
                    return b[:, :].rearrange("p (a c) -> p a c", a=2)

                def take(i, dst, func=ACT.Copy, scale=1.0):
                    wait_products(act, mix, i)
                    act.activation(dst, halves(bank[i % 4]), func, scale=scale).then_inc(taken, 1)

                def take_bu(t):
                    act.wait_ge(bu_ready, ST * l + t + 1)
                    act.activation(bu[:, t, :, :], halves(bank[6 + t % 2]), ACT.Copy).then_inc(bu_taken, 1)

                def take_qk(kind, which):
                    if kind or l:
                        act.wait_ge(qk_turned, 2 * (2 * l + kind))
                        act.wait_ge(qk_mean, 2 * (2 * l + kind))
                    take(3 + 3 * kind + which, qk[:, which, :, :])
                    take(3 + 3 * kind + which, sq[:, which, :, :], ACT.Square)

                def root_qk(kind):
                    act.wait_ge(qk_mean, 2 * (2 * l + kind + 1))
                    act.activation(nrm[:, 1, :, :], nrm[:, 0, :, :], ACT.Sqrt).then_inc(qk_root, 1)

                def gain_qk(kind):
                    for which in range(2):
                        act.wait_ge(qk_turned, 2 * (2 * l + kind) + which + 1)
                        b = bank[(6, 7, 5, 4)[2 * kind + which]]
                        g = par(l, ("fox_q", "fox_k", "sb_q", "sb_k")[2 * kind + which])
                        act.activation(qT[:, kind, which, :, :], halves(b), ACT.Copy, scale=g).then_inc(qk_gained, 1)

                def gates(i):
                    n, half = i // 2, i % 2
                    buf = (G2, H)[n % 2]
                    if n >= 2 and half == 0:
                        if n == 2:
                            act.wait_ge(gated, 16 * l + 4)
                        else:
                            act.wait_ge(merged, 12 * l + 4)
                    for b in range(NB):
                        if b == 0:
                            act.wait_ge(gate_ready, 8 * l + i + 1)
                        else:
                            wait_products(act, mix, 10 + 5 * n + 2 * half)
                        act.activation(buf[:, b, half * 512:(half + 1) * 512], bank[2 * half + b][:, :], ACT.Tanh,
                                       scale=0.5).then_inc(gate_tanh, 1)

                def row_exp(h):
                    act.wait_ge(row_max, NH * l + h + 1)
                    if h >= 2:
                        act.wait_ge(p_turned, NH * l + h - 1)
                    act.activation(sc[:, h % 2, 0:P], bank[6 + h % 2][:, 0:P], ACT.Exp, bias=mx[:, 0, h, 0:1],
                                   accum_out=rs[:, 0, h, 0:1]).then_inc(p_exp, 1)
                    act.activation(sc[:, h % 2, P:3 * P], bank[6 + h % 2][:, P:3 * P], ACT.Exp, bias=mx[:, 0, h, 1:2],
                                   accum_out=rs[:, 0, h, 1:2]).then_inc(p_exp, 1)

                def take_p(h):
                    act.wait_ge(p_turned, NH * l + h + 1)
                    if h >= 2:
                        act.wait_ge(fox_out, NH * l + h - 1)
                    act.activation(pT[:, h % 2, :], bank[4][:, 0:3 * P], ACT.Copy).then_inc(p_taken, 1)

                def soft_ln(pair):
                    act.wait_ge(z_ready, NH * l + 2 * pair + 2)
                    for i in range(2):
                        step.mark(act.activation(sc[:, i, :], bank[6 + i][:, 0:3 * P], ACT.Abs))
                    step.settle()
                    step(act.activation(sc[:, :, :], sc[:, :, :], ACT.Exp, scale=-1.0))
                    act.activation(sc[:, :, :], sc[:, :, :], ACT.Ln, bias=1.0).then_inc(z_ln, 1)

                def a_weights(pair):
                    for i in range(2):
                        act.wait_ge(z_cum, NH * l + 2 * pair + i + 1)
                        if pair:
                            act.wait_ge(sb_out, NH * l + 2 * pair)
                        act.activation(pT[:, i, :], bank[6 + i][:, 0:3 * P], ACT.Exp).then_inc(a_exp, 1)

                def ys_split(n, src, ready, count, scale):
                    act.wait_ge(ready, count)
                    if n >= 2:
                        wait_products(act, mix, 13 + 5 * (n - 2))
                    act.activation(ys_hi[:, n % 2, :, :], src, ACT.Copy, scale=scale).then_inc(ys_high, 1)

                for u in range(MIX_UNITS):
                    if u + RING < MIX_UNITS:
                        split_high(mix, u + RING)
                    elif after:
                        split_high(after, u + RING - MIX_UNITS)
                    if u == 0:
                        if l:
                            act.wait_ge(ys_low, 4 * l)
                        take(0, ca[:, :, :])
                    if u == 1:
                        take(1, cs[:, :, :], ACT.Tanh, 0.5)
                        s5_operands(l)
                    if u == 2:
                        take(2, uT[:, :, :])
                    if u in (3, 4):
                        take_qk(0, u - 3)
                    if u == 5:
                        take(5, V[:, 0, :, :])
                        root_qk(0)
                    if u in (3, 4, 5, 6):
                        take_bu(2 * (u - 3))
                        take_bu(2 * (u - 3) + 1)
                    if u == 7:
                        gain_qk(0)
                        take_qk(1, 0)
                        take_qk(1, 1)
                    if u == 8:
                        take(8, V[:, 1, :, :])
                        root_qk(1)
                        act.wait_ge(conv_cent, l + 1)
                        act.activation(cs[:, :, :], ca[:, :, :], ACT.Square).then_inc(conv_sq, 1)
                    if u == 9:
                        act.wait_ge(conv_vare, l + 1)
                        act.activation(lnv[:, 1, :], lnv[:, 0, :], ACT.Sqrt).then_inc(conv_root, 1)
                        row_exp(0)
                    if u == 10:
                        gates(0)
                        gain_qk(1)
                        row_exp(1)
                        act.wait_ge(conv_lin, l + 1)
                        act.activation(cs[:, :, :], ca[:, :, :], ACT.Tanh, scale=0.5).then_inc(conv_tanh, 1)
                        ys_split(0, ca[:, :, :], conv_out, l + 1, 0.5)
                    if u == 11:
                        row_exp(2)
                        take_p(0)
                    if u == 12:
                        gates(1)
                        row_exp(3)
                        take_p(1)
                    if u == 13:
                        take_p(2)
                    if u == 14:
                        take_p(3)
                        soft_ln(0)
                    if u == 15:
                        gates(2)
                        ys_split(1, halves(bank[5]), fox_out, NH * (l + 1), 1.0)
                    if u == 16:
                        a_weights(0)
                    if u == 17:
                        gates(3)
                        soft_ln(1)
                    if u == 19:
                        a_weights(1)
                    if u == 20:
                        gates(4)
                        ys_split(2, halves(bank[5]), sb_out, NH * (l + 1), 1.0)
                    if u == 22:
                        gates(5)
                    if u == 25:
                        gates(6)
                        act.wait_ge(gelu_in, l + 1)
                        act.activation(cs[:, :, :], halves(tmp[:, 1, :]), ACT.Tanh,
                                       scale=0.7978845608028654).then_inc(gelu_tanh, 1)
                    if u == 26:
                        act.wait_ge(glu_ready, l + 1)
                        act.activation(cs[:, :, :], halves(bank[6]), ACT.Tanh, scale=0.25).then_inc(glu_tanh, 1)
                        ys_split(3, ca[:, :, :], glu_out, l + 1, 0.25)
                    if u == 27:
                        gates(7)
                    if u == MIX_UNITS - 5:
                        turn_high(3 * l + 1, 4, None)
                if upto <= 2 * l + 1:
                    break
                norm_rows(2 * l + 1)
                turn_high(3 * l + 2, 0, par(l, "g_ffn"))

                if l == 0:
                    s5_angles(1)

                    def hidden(u, j, odd):
                        wait_products(act, u, j)
                        act.activation(silu[:, odd, :, :], halves(bank[2 * odd]), ACT.Silu).then_inc(silu_ready, 1)

                    def hidden_high(c, odd):
                        act.wait_ge(g_ready, c + 1)
                        act.activation(ys_hi[:, odd, :, :], gated_h[:, odd, :, :],
                                       ACT.Copy).then_inc(g_hi, 1)

                    split_high(Units(DENSE0), 3)
                    hidden(Units(DENSE0), 0, 0)
                    split_high(Units(DENSE0), 4)
                    hidden_high(0, 0)

                    def pair(i, last):
                        u = Units(DENSE0, i * 2)
                        for m in range(2):
                            split_high(u, 5 + 3 * m)
                            hidden(u, 2 + 3 * m, 1 - m)
                            if not last or m == 0 or upto > 2:
                                split_high(u, 6 + 3 * m)
                            hidden_high(i * 2 + 1 + m, 1 - m)
                            if not last or m == 0 or upto > 2:
                                split_high(u, 7 + 3 * m)

                    with act.Fori(0, PAIRS - 1) as i:
                        pair(i, False)
                    pair(PAIRS - 1, True)
                    if upto > 2:
                        split_high(Units(BASE[1]), 2)
                if upto <= 2 * l + 2:
                    break

            if upto >= 4:
                act.wait_ge(top_gap, 1)
                act.activation(route[:, 10, :, 0:1], route[:, 9, :, 0:1], ACT.Exp).then_inc(top_exp, 1)

                def expert(n, first):
                    u = Units(MOE0, n * NCH)
                    if not first:
                        split_high(u, 0)
                    act.wait_ge(pick_turned, n + 1)
                    act.activation(pT[:, 0, 0:NB * P], bank[2][:, 0:NB * P], ACT.Copy).then_inc(pick_taken, 1)
                    for k in range(KT):
                        act.wait_ge(gathered, n * 2 + k // 4 + 1)
                        act.activation(hT_hi[:, k, 0:P], bank[6 + k // 4][:, (k % 4) * P:(k % 4 + 1) * P], ACT.Copy,
                                       scale=par(1, "g_ffn", k, k + 1)).then_inc(gather_hi, 1)
                    if not first:
                        split_high(u, 1)
                        split_high(u, 2)

                    def hidden(v, j, odd):
                        wait_products(act, v, j)
                        act.activation(silu[:, odd, 0, :], bank[2 * odd][:, 0:CH], ACT.Silu).then_inc(silu_ready, 1)

                    def hidden_high(c, odd):
                        act.wait_ge(g_turned, n * NCH + c + 1)
                        act.activation(ys_hi[:, odd, 0, :], bank[6][:, 0:CH], ACT.Copy).then_inc(g_hi, 1)

                    def pair(i, last):
                        u = Units(MOE0, n * NCH + i * 2)
                        for m in range(2):
                            hidden_high(i * 2 + m, m)
                            split_high(u, 5 + 3 * m)
                            hidden(u, 2 + 3 * m, 1 - m)
                            if not last or m == 0:
                                split_high(u, 6 + 3 * m)
                                split_high(u, 7 + 3 * m)

                    split_high(u, 3)
                    hidden(u, 0, 0)
                    split_high(u, 4)
                    with act.Fori(0, PAIRS - 1) as i:
                        pair(i, False)
                    pair(PAIRS - 1, True)
                    hidden_high(NCH - 1, 0)
                    wait_products(act, u, FFN_UNITS - 1)
                    for half in range(2):
                        act.activation(M[:, 0, half * 512:(half + 1) * 512], bank[4 + half][:, :],
                                       ACT.Copy).then_inc(y_taken, 1)

                expert(0, True)
                with act.Fori(1, NE) as e:
                    expert(e, False)
                act.wait_ge(spill_known, 1)
                n_spill = act.value_load(spill_i[0:1, 0:1], min_val=0, max_val=N_SPILL)
                for t in range(N_SPILL):
                    with act.If(n_spill > t):
                        expert(NE + t, False)

        @block.vector
        def _(dve):
            step = Chain(dve, dve_step)
            tt, ts, stt = dve.tensor_tensor, dve.tensor_scalar, dve.scalar_tensor_tensor

            def norm_rows(r):
                dve.wait_ge(squared, 2 * r + 2)
                ts(stat[:, 2:4], stat[:, 0:2], 1.0 / D, EPS, ALU.mult, ALU.add).then_inc(mean_sq, 1)
                dve.wait_ge(rms_root, r + 1)
                step(dve.reciprocal(stat[:, 6:8], stat[:, 4:6]))
                for b in range(NB):
                    ts(H[:, b, :], X[:, b, :], stat[:, 6 + b:7 + b], None, ALU.mult).then_inc(normed, 1)

            def turn_low(t, base, gain):
                for k in range(KT):
                    dve.wait_ge(turned_hi, KT * t + k // 2 * 2 + 2)
                    stt(hT_lo[:, k, :], bank[base + k // 2][:, (k % 2) * SEQ:(k % 2 + 1) * SEQ],
                        0.5 if gain is None else gain[:, k:k + 1], hT_hi[:, k, :].bitcast(F32), ALU.mult,
                        ALU.subtract).then_inc(turned_lo, 1)

            s5a = [s5p[:, i, :] for i in range(20)]
            dt, mag, turn, arg, sin, hsin, t6, _, cos, are, aim, nre, den, kre, kim, t14, t15, t16, pc, ps = s5a

            def s5_angles(l):
                lre, lim = par(l, "lam_re"), par(l, "lam_im")
                dve.wait_ge(s5_exp, 2 * l + 1)
                tt(mag, lre, dt, ALU.mult).then_inc(s5_arg, 1)
                step(tt(turn, lim, dt, ALU.mult))
                step(ts(t6, turn, 1.0 / (2 * np.pi), ROUND, ALU.mult, ALU.add))
                step(ts(t6, t6, ROUND, None, ALU.subtract))
                step(stt(arg, t6, -TWO_PI_1, turn, ALU.mult, ALU.add))
                step(stt(arg, t6, -TWO_PI_2, arg, ALU.mult, ALU.add))
                step(stt(arg, t6, -TWO_PI_3, arg, ALU.mult, ALU.add))
                ts(arg, arg, PI_F32, -PI_F32, ALU.min, ALU.max).then_inc(s5_arg, 1)

            def s5_spread_of(l):
                lre, lim = par(l, "lam_re"), par(l, "lam_im")
                dve.wait_ge(s5_sin, 2 * l + 2)
                step(tt(cos, hsin, hsin, ALU.mult))
                step(ts(cos, cos, -2.0, 1.0, ALU.mult, ALU.add))
                step.mark(tt(are, mag, cos, ALU.mult))
                step.mark(tt(aim, mag, sin, ALU.mult))
                step.mark(tt(den, lre, lre, ALU.mult))
                step(tt(t14, lim, lim, ALU.mult))
                step.mark(ts(nre, are, 1.0, None, ALU.subtract))
                step(tt(den, den, t14, ALU.add))
                step.mark(dve.reciprocal(den, den))
                step.mark(tt(t14, nre, lre, ALU.mult))
                step.mark(tt(t15, aim, lim, ALU.mult))
                step.mark(tt(t16, aim, lre, ALU.mult))
                step(tt(kim, nre, lim, ALU.mult))
                step.mark(tt(t14, t14, t15, ALU.add))
                step(tt(t16, t16, kim, ALU.subtract))
                step.mark(tt(kre, t14, den, ALU.mult))
                step(tt(kim, t16, den, ALU.mult))
                b3 = [tmp[:, i, 0:ST * GH].rearrange("p (t h) -> p t h", h=GH) for i in range(4)]
                bre, bim = (par(l, n).rearrange("p (t h) -> p t h", h=GH) for n in ("b_re", "b_im"))
                kre3, kim3 = (k.unsqueeze(2).to_broadcast([P, ST, GH]) for k in (kre, kim))
                step.mark(tt(b3[0], bre, kre3, ALU.mult))
                step.mark(tt(b3[1], bim, kim3, ALU.mult))
                step.mark(tt(b3[2], bim, kre3, ALU.mult))
                step(tt(b3[3], bre, kim3, ALU.mult))
                step.mark(tt(b3[0], b3[0], b3[1], ALU.subtract))
                step(tt(b3[2], b3[2], b3[3], ALU.add))
                for ri in range(2):
                    for side in range(2):
                        step.mark(ts(s5b[:, ri, :, side, :], b3[2 * ri], const("side", side, side + 1), None, ALU.mult))
                    for side in range(2):
                        c3 = par(l, ("c_re", "c_im")[ri]).rearrange("p (a c) -> p a c", a=CT)
                        ins = ts(s5c[:, ri, :, side, :], c3, const("parity", side, side + 1), None, ALU.mult)
                        if ri == 0 or side == 0:
                            step.mark(ins)
                ins.then_inc(s5_spread, 1)
                step.settle()

            def s5_table(l, n, end):
                step.settle()
                if n == 1:
                    step.mark(dve.memset(rot_c[:, :, 0:1], 1.0))
                    step.mark(dve.memset(rot_s[:, :, 0:1], 0.0))
                    step.mark(dve.tensor_copy(pc, cos))
                    step(dve.tensor_copy(ps, sin))
                ta = tmp[:, 0:2, :].rearrange("p a c -> p (a c)")
                tb = tmp[:, 2:4, :].rearrange("p a c -> p (a c)")
                while n < end:
                    c0, s0, c1, s1 = rot_c[:, :, 0:n], rot_s[:, :, 0:n], rot_c[:, :, n:2 * n], rot_s[:, :, n:2 * n]
                    pcb, psb = (v.unsqueeze(2).to_broadcast([P, ST, n]) for v in (pc, ps))
                    t0, t1 = (t[:, 0:ST * n].rearrange("p (t n) -> p t n", t=ST) for t in (ta, tb))
                    step.mark(tt(t0, s0, psb, ALU.mult))
                    step.mark(tt(t1, c0, psb, ALU.mult))
                    step.mark(tt(c1, c0, pcb, ALU.mult))
                    step(tt(s1, s0, pcb, ALU.mult))
                    step.mark(tt(c1, c1, t0, ALU.subtract))
                    step.mark(tt(s1, s1, t1, ALU.add))
                    step.mark(tt(t14, pc, pc, ALU.mult))
                    step.mark(tt(t15, ps, ps, ALU.mult))
                    step(tt(t16, pc, ps, ALU.mult))
                    step.mark(tt(pc, t14, t15, ALU.subtract))
                    step(ts(ps, t16, 2.0, None, ALU.mult))
                    n *= 2

            def s5_scan(l, pair):
                t0 = 2 * pair
                dve.wait_ge(bu_taken, ST * l + t0 + 2)
                step.settle()
                if l or pair:
                    dve.wait_ge(s5_state, ST // 2 * l + pair)
                re, im = bu[:, t0:t0 + 2, 0, :], bu[:, t0:t0 + 2, 1, :]
                c, s = rot_c[:, t0:t0 + 2, :], rot_s[:, t0:t0 + 2, :]
                q = [tmp[:, i, :].rearrange("p (a c) -> p a c", a=2) for i in range(4)]
                step.mark(tt(q[0], c, re, ALU.mult))
                step.mark(tt(q[1], s, im, ALU.mult))
                step.mark(tt(q[2], c, im, ALU.mult))
                step(tt(q[3], s, re, ALU.mult))
                step.mark(tt(q[0], q[0], q[1], ALU.add))
                step(tt(q[2], q[2], q[3], ALU.subtract))
                for a in range(2):
                    mag = s5p[:, 1, t0 + a:t0 + a + 1].to_broadcast([P, SEQ])
                    for ri in range(2):
                        ins = dve.tensor_tensor_scan(bu[:, t0 + a, ri, :], mag, q[2 * ri][:, a, :], 0.0, ALU.mult, ALU.add)
                        step.mark(ins)
                step.settle()
                step.mark(tt(q[0], c, re, ALU.mult))
                step.mark(tt(q[1], s, im, ALU.mult))
                step.mark(tt(q[2], c, im, ALU.mult))
                step(tt(q[3], s, re, ALU.mult))
                step.mark(tt(re, q[0], q[1], ALU.subtract))
                tt(im, q[2], q[3], ALU.add).then_inc(s5_state, 1)

            def halves(b):
                return b[:, :].rearrange("p (a c) -> p a c", a=2)

            dve.wait_ge(loaded, 64)
            nf = KT * NH
            for l in range(2):
                dve.wait_ge(small_hi, l + 1)
                tt(smallw_lo[:, l * nf:(l + 1) * nf], par(l, "w_forget"), smallw_hi[:, l * nf:(l + 1) * nf].bitcast(F32),
                   ALU.subtract).then_inc(small_lo, 1)
            dve.wait_ge(small_hi, 3)
            tt(smallw_lo[:, 2 * nf:], RT[:, 0:KT * NE], smallw_hi[:, 2 * nf:].bitcast(F32), ALU.subtract).then_inc(small_lo, 1)

            for l in range(2):
                mix = Units(BASE[l])
                norm_rows(2 * l)
                if l == 0:
                    s5_angles(0)
                turn_low(3 * l, 0, par(l, "g_mix"))
                if l == 0:
                    s5_spread_of(0)

                dve.wait_ge(forget_ready, l + 1)
                f3 = lf[:, 0, :].rearrange("p (b h) -> p b h", b=NB)
                tt(f3, bank[4][:, 0:NB * NH].rearrange("p (b h) -> p b h", b=NB),
                   par(l, "b_forget").unsqueeze(1).to_broadcast([P, NB, NH]), ALU.add).then_inc(forget_in, 1)
                dve.wait_ge(forget_ln, l + 1)
                dve.wait_ge(forget_in, l + 1)
                step(stt(lf[:, 1, :], lf[:, 0, :], 0.0, lf[:, 3, :], ALU.min, ALU.subtract))
                for h in range(NH):
                    for i, (tab, b) in enumerate((("tri", 0), ("ones", 0), ("tri", 1))):
                        ins = ts(TL[:, h, i, :], const(tab), lf[:, 1, b * NH + h:b * NH + h + 1], None, ALU.mult)
                ins.then_inc(forget_tri, 1)

                dve.wait_ge(taken, 13 * l + 2)
                step.mark(dve.memset(upad[:, :, 0:PAD], 0.0))
                step(stt(upad[:, :, PAD:], cs[:, :, :], 1.0, ca[:, :, :], ALU.add, ALU.mult))
                for tap in range(CONVW):
                    for c in range(CT):
                        w = par(l, "conv_w", c * CONVW + tap, c * CONVW + tap + 1)
                        src = upad[:, c, tap:tap + SEQ]
                        if tap == 0:
                            step.mark(ts(ca[:, c, :], src, w, None, ALU.mult))
                        else:
                            step.mark(stt(ca[:, c, :], src, w, ca[:, c, :], ALU.mult, ALU.add))
                    step.settle()
                for c in range(CT):
                    ts(ca[:, c, :], ca[:, c, :], 0.5, par(l, "conv_b", c, c + 1), ALU.mult, ALU.add).then_inc(conv_sum, 1)

                def norm_qk(kind):
                    for which in range(2):
                        i = 3 + 3 * kind + which
                        dve.wait_ge(taken, 13 * l + (5, 7, 10, 12)[2 * kind + which])
                        step(dve.tensor_reduce(nrm[:, 0, which, :],
                                               sq[:, which, :, :].rearrange("p b (h d) -> p (b h) d", d=HD), AX_X, ALU.add))
                        f = 1.0 if which == 0 else 1.0 / HD
                        ts(nrm[:, 0, which, :], nrm[:, 0, which, :], f, f * HD * EPS, ALU.mult, ALU.add).then_inc(qk_mean, 1)
                    dve.wait_ge(qk_root, 2 * l + kind + 1)
                    dve.wait_ge(qk_mean, 2 * (2 * l + kind + 1))
                    step(dve.reciprocal(nrm[:, 0, :, :], nrm[:, 1, :, :]))
                    for which in range(2):
                        v = qk[:, which, :, :].rearrange("p b (h d) -> p (b h) d", d=HD)
                        tt(v, v, nrm[:, 0, which, :].unsqueeze(2).to_broadcast([P, NB * NH, HD]),
                           ALU.mult).then_inc(qk_normed, 1)

                def ys_split(n, src, scale):
                    dve.wait_ge(ys_high, 4 * l + n + 1)
                    stt(ys_lo[:, n % 2, :, :], src, scale, ys_hi[:, n % 2, :, :].bitcast(F32), ALU.mult,
                        ALU.subtract).then_inc(ys_low, 1)

                def row_max_of(h):
                    dve.wait_ge(score, NH * l + h + 1)
                    b = bank[6 + h % 2]
                    step.mark(dve.tensor_reduce(mx[:, 0, h, 0:1], b[:, 0:P], AX_X, ALU.max, negate=True))
                    dve.tensor_reduce(mx[:, 0, h, 1:2], b[:, P:3 * P], AX_X, ALU.max, negate=True).then_inc(row_max, 1)

                def row_norm(h):
                    dve.wait_ge(p_exp, 2 * (NH * l + h + 1))
                    step(dve.reciprocal(rs[:, 1, h, :], rs[:, 0, h, :]))
                    step.mark(ts(sc[:, h % 2, 0:P], sc[:, h % 2, 0:P], rs[:, 1, h, 0:1], None, ALU.mult))
                    ts(sc[:, h % 2, P:3 * P], sc[:, h % 2, P:3 * P], rs[:, 1, h, 1:2], None, ALU.mult).then_inc(p_norm, 1)

                def soft(pair):
                    dve.wait_ge(z_ln, 2 * l + pair + 1)
                    for i in range(2):
                        step(stt(sc[:, i, :], bank[6 + i][:, 0:3 * P], 0.0, sc[:, i, :], ALU.max, ALU.add))
                        tt(sc[:, i, :], sc[:, i, :], const("keep"), ALU.mult).then_inc(z_soft, 1)

                def apply_gates(n, half):
                    buf = (G2, H)[n % 2]
                    for b in range(NB):
                        cols = slice(half * 512, (half + 1) * 512)
                        if half and b:
                            wait_products(dve, mix, 13 + 5 * n)
                        else:
                            dve.wait_ge(branch, 12 * l + 3 * n + 2 * half + b + 1)
                        dve.wait_ge(gate_tanh, 16 * l + 4 * n + 2 * half + b + 1)
                        if n == 0:
                            stt(M[:, b, cols], buf[:, b, cols], 1.0, bank[2 * half + b][:, :], ALU.add,
                                ALU.mult).then_inc(gated, 1)
                        else:
                            stt(buf[:, b, cols], buf[:, b, cols], 1.0, bank[2 * half + b][:, :], ALU.add,
                                ALU.mult).then_inc(gated, 1)
                            dve.wait_ge(gated, 16 * l + 4 * n + 2 * half + b + 1)
                            if n >= 2:
                                dve.wait_ge(merged, 12 * l + 4 * (n - 2) + 2 * half + b + 1)
                            tt(M[:, b, cols], M[:, b, cols], buf[:, b, cols], ALU.add).then_inc(merged, 1)

                norm_qk(0)
                if l == 0:
                    s5_table(0, 1, SEQ)
                s5_scan(l, 0)
                dve.wait_ge(conv_mean, l + 1)
                dve.wait_ge(conv_sum, 2 * l + 2)
                tt(ca[:, :, :], ca[:, :, :], bank[4][:, 0:SEQ].unsqueeze(1).to_broadcast([P, CT, SEQ]),
                   ALU.subtract).then_inc(conv_cent, 1)
                norm_qk(1)
                dve.wait_ge(conv_var, l + 1)
                ts(lnv[:, 0, :], bank[4][:, SEQ:2 * SEQ], EPS, None, ALU.add).then_inc(conv_vare, 1)
                row_max_of(0)
                dve.wait_ge(conv_root, l + 1)
                step(dve.reciprocal(lnv[:, 2, :], lnv[:, 1, :]))
                dve.wait_ge(conv_cent, l + 1)
                step(tt(ca[:, :, :], ca[:, :, :], lnv[:, 2, :].unsqueeze(1).to_broadcast([P, CT, SEQ]), ALU.mult))
                for c in range(CT):
                    ins = ts(ca[:, c, :], ca[:, c, :], par(l, "ln_g", c, c + 1), par(l, "ln_b", c, c + 1), ALU.mult, ALU.add)
                    if c < CT - 1:
                        step.mark(ins)
                ins.then_inc(conv_lin, 1)
                row_norm(0)
                row_max_of(1)
                dve.wait_ge(conv_tanh, l + 1)
                stt(ca[:, :, :], cs[:, :, :], 1.0, ca[:, :, :], ALU.add, ALU.mult).then_inc(conv_out, 1)
                ys_split(0, ca[:, :, :], 0.5)
                row_norm(1)
                row_max_of(2)
                row_norm(2)
                row_max_of(3)
                row_norm(3)
                apply_gates(0, 0)
                apply_gates(0, 1)
                soft(0)
                ys_split(1, halves(bank[5]), 1.0)
                s5_scan(l, 1)
                soft(1)
                apply_gates(1, 0)
                apply_gates(1, 1)
                s5_scan(l, 2)
                ys_split(2, halves(bank[5]), 1.0)
                s5_scan(l, 3)
                apply_gates(2, 0)
                apply_gates(2, 1)
                dve.wait_ge(s5_y, l + 1)
                y3, g3, q3 = (halves(tmp[:, i, :]) for i in (0, 1, 2))
                dve.wait_ge(s5_state, ST // 2 * (l + 1))
                for c in range(CT):
                    step.mark(stt(y3[:, c, :], uT[:, c, :], par(l, "s5_d", c, c + 1), halves(bank[4])[:, c, :],
                                  ALU.mult, ALU.add))
                step.settle()
                step(tt(q3, y3, y3, ALU.mult))
                step(ts(q3, q3, 0.044715, 1.0, ALU.mult, ALU.add))
                tt(g3, q3, y3, ALU.mult).then_inc(gelu_in, 1)
                dve.wait_ge(gelu_tanh, l + 1)
                stt(q3, cs[:, :, :], 1.0, y3, ALU.add, ALU.mult).then_inc(gelu_out, 1)
                dve.wait_ge(glu_tanh, l + 1)
                dve.wait_ge(gelu_out, l + 1)
                stt(ca[:, :, :], cs[:, :, :], 1.0, q3, ALU.add, ALU.mult).then_inc(glu_out, 1)
                ys_split(3, ca[:, :, :], 0.25)
                apply_gates(3, 0)
                apply_gates(3, 1)
                turn_low(3 * l + 1, 4, None)

                def add_to_x(u, base):
                    wait_products(dve, u, MIX_UNITS - 1)
                    for half in range(2):
                        for b in range(NB):
                            xs = X[:, b, half * 512:(half + 1) * 512]
                            tt(xs, xs, bank[base + 2 * half + b][:, :], ALU.add).then_inc(x_mixed, 1)

                add_to_x(mix, 0)
                if upto <= 2 * l + 1:
                    break
                dve.wait_ge(x_mixed, 4 * (2 * l + 1))
                norm_rows(2 * l + 1)
                turn_low(3 * l + 2, 0, par(l, "g_ffn"))
                if l == 0:
                    def hidden(u, j, c, odd):
                        wait_products(dve, u, j)
                        dve.wait_ge(silu_ready, c + 1)
                        tt(gated_h[:, odd, :, :], silu[:, odd, :, :], halves(bank[2 * odd + 1]), ALU.mult).then_inc(g_ready, 1)
                        dve.wait_ge(g_hi, c + 1)
                        tt(ys_lo[:, odd, :, :], gated_h[:, odd, :, :], ys_hi[:, odd, :, :].bitcast(F32),
                           ALU.subtract).then_inc(g_lo, 1)

                    s5_angles(1)
                    hidden(Units(DENSE0), 1, 0, 0)
                    s5_spread_of(1)
                    s5_table(1, 1, 32)
                    hidden(Units(DENSE0), 3, 1, 1)
                    s5_table(1, 32, 128)
                    hidden(Units(DENSE0), 6, 2, 0)
                    s5_table(1, 128, SEQ)
                    with dve.Fori(1, PAIRS) as i:
                        for m in range(2):
                            hidden(Units(DENSE0, i * 2), 3 + 3 * m, i * 2 + 1 + m, 1 - m)
                    add_to_x(Units(DENSE0), 4)
                    dve.wait_ge(x_mixed, 8)
                if upto <= 2 * l + 2:
                    break

            if upto >= 4:
                r = [route[:, i, :, :] for i in range(12)]
                lg, top, at, one, two, sel, comb, place, w1, gap, e, spare = r
                dve.wait_ge(logits, 1)
                step(tt(lg, bank[4][:, 0:NB * NE].rearrange("p (b e) -> p b e", b=NB),
                        RT[:, KT * NE:].unsqueeze(1).to_broadcast([P, NB, NE]), ALU.add))
                for b in range(NB):
                    step.mark(dve.max(top[:, b, :], lg[:, b, :]))
                step.settle()
                for b in range(NB):
                    step.mark(dve.max_index(top_at[:, b, :], top[:, b, :], lg[:, b, :]))
                ts_ = tt(gap[:, :, 0:1], top[:, :, 1:2], top[:, :, 0:1], ALU.subtract)
                ts_.then_inc(top_gap, 1)
                step.settle()
                step(dve.tensor_copy(at, top_at[:, :, :]))
                for b in range(NB):
                    step.mark(ts(one[:, b, :], const("iota8"), at[:, b, 0:1], None, ALU.is_equal))
                    step.mark(ts(two[:, b, :], const("iota8"), at[:, b, 1:2], None, ALU.is_equal))
                step.settle()
                tt(sel, one, two, ALU.add).then_inc(chosen, 1)
                dve.wait_ge(top_exp, 1)
                step(ts(w1[:, :, 0:1], e[:, :, 0:1], 1.0, None, ALU.add))
                step(dve.reciprocal(w1[:, :, 0:1], w1[:, :, 0:1]))
                step(tt(w1[:, :, 1:2], w1[:, :, 0:1], e[:, :, 0:1], ALU.mult))
                for b in range(NB):
                    step(ts(comb[:, b, :], one[:, b, :], w1[:, b, 0:1], None, ALU.mult))
                    step(stt(comb[:, b, :], two[:, b, :], w1[:, b, 1:2], comb[:, b, :], ALU.mult, ALU.add))
                dve.wait_ge(places, 1)
                dve.wait_ge(chosen, 1)
                pb3 = bank[5][:, 0:NB * NE].rearrange("p (b e) -> p b e", b=NB)
                step(stt(place, pb3, 1.0, sel, ALU.add, ALU.mult))
                step(ts(place, place, 1.0, None, ALU.subtract))
                step(ts(spare, place, float(P), None, ALU.subtract))
                s = [spill[0:1, i, :] for i in range(4)]
                step(ts(s[0], bank[5][0:1, NB * NE:(NB + 1) * NE], float(P), None, ALU.is_gt))
                step(dve.tensor_tensor_scan(s[1], const("ones", 0, NE, rows=1), s[0], 0.0, ALU.mult, ALU.add))
                step(dve.tensor_copy(spill_i[0:1, 0:1], s[1][:, NE - 1:NE]))
                for t in range(N_SPILL):
                    step(stt(s[2], s[1], float(t + 1), s[0], ALU.is_equal, ALU.mult))
                    step(tt(s[2], s[2], const("iota8", rows=1), ALU.mult))
                    step(dve.tensor_reduce(s[3][:, t:t + 1], s[2], AX_X, ALU.add))
                dve.tensor_copy(spill_i[0:1, 1:1 + N_SPILL], s[3][:, 0:N_SPILL]).then_inc(spill_known, 1)

                def split_low(u, j):
                    s_ = u.slot(j)
                    if s_ == 2:
                        return
                    dve.wait_ge(hi_ready[s_], u.earlier(j) + 1)
                    tt(low[:, s_, :], raw[:, s_, :], high[:, s_, :].bitcast(F32), ALU.subtract).then_inc(lo_ready[s_], 1)

                def expert(e_, n, where):
                    u = Units(MOE0, n * NCH)
                    for b in range(NB):
                        ts(G2[:, 0, b * P:(b + 1) * P], const("iota"), route[:, where, b, bass.ds(e_, 1)], None,
                           ALU.is_equal).then_inc(picked, 1)
                    split_low(u, 0)
                    for k in range(KT):
                        dve.wait_ge(gather_hi, n * KT + k // 4 * 4 + 4)
                        stt(hT_lo[:, k, 0:P], bank[6 + k // 4][:, (k % 4) * P:(k % 4 + 1) * P], par(1, "g_ffn", k, k + 1),
                            hT_hi[:, k, 0:P].bitcast(F32), ALU.mult, ALU.subtract).then_inc(gather_lo, 1)
                    split_low(u, 1)

                    def hidden(v, j, c, odd):
                        wait_products(dve, v, j)
                        dve.wait_ge(silu_ready, n * NCH + NCH + c + 1)
                        tt(gated_h[:, odd, 0, :], silu[:, odd, 0, :], bank[2 * odd + 1][:, 0:CH], ALU.mult).then_inc(g_ready, 1)

                    def hidden_low(c, odd):
                        dve.wait_ge(g_hi, n * NCH + NCH + c + 1)
                        tt(ys_lo[:, odd, 0, :], bank[6][:, 0:CH], ys_hi[:, odd, 0, :].bitcast(F32),
                           ALU.subtract).then_inc(g_lo, 1)

                    def pair(i, last):
                        v = Units(MOE0, n * NCH + i * 2)
                        for m in range(2):
                            hidden_low(i * 2 + m, m)
                            split_low(v, 5 + 3 * m)
                            if not last or m == 0:
                                split_low(v, 6 + 3 * m)
                            hidden(v, 3 + 3 * m, i * 2 + 1 + m, 1 - m)
                            if not last or m == 0:
                                split_low(v, 7 + 3 * m)

                    split_low(u, 3)
                    hidden(u, 1, 0, 0)
                    split_low(u, 4)
                    with dve.Fori(0, PAIRS - 1) as i:
                        pair(i, False)
                    pair(PAIRS - 1, True)
                    hidden_low(NCH - 1, 0)
                    for b in range(NB):
                        for half in range(2):
                            i = 2 * b + half
                            dve.wait_ge(spread, n * 4 + i + 1)
                            xs = X[:, b, half * 512:(half + 1) * 512]
                            stt(xs, bank[6 + i % 2][:, :], route[:, 6, b, bass.ds(e_, 1)], xs, ALU.mult,
                                ALU.add).then_inc(added, 1)

                step.settle()
                dve.wait_ge(spill_known, 1)
                with dve.Fori(0, NE) as e_:
                    expert(e_, e_, 7)
                n_spill = dve.value_load(spill_i[0:1, 0:1], min_val=0, max_val=N_SPILL)
                for t in range(N_SPILL):
                    with dve.If(n_spill > t):
                        expert(dve.value_load(spill_i[0:1, 1 + t:2 + t], min_val=0, max_val=NE - 1), NE + t, 11)
                dve.memset(stat[:, 0:1], 0.0).then_inc(finished, 1)

        @block.tensor
        def _(pe):
            def product(dst, w, m, start, stop):
                pe.matmul(dst, w[0], m[0], start=start, stop=False, skip_group_check=True)
                pe.matmul(dst, w[1], m[0], start=False, stop=False, skip_group_check=True)
                return pe.matmul(dst, w[0], m[1], start=False, stop=stop, skip_group_check=True)

            def parts(s, nk):
                return unit_view(high, s, nk), unit_view(low, s, nk)

            def cut(pair_, *ix):
                return tuple(t[ix] for t in pair_)

            def arrive(u, j):
                s = u.slot(j)
                pe.wait_ge(lo_ready[s], u.earlier(j) + 1)
                return s

            hT = (hT_hi, hT_lo)
            everything = slice(None)

            def turn(t, src, base):
                for i in range(KT // 2):
                    for kk in range(2):
                        for b in range(NB):
                            k = 2 * i + kk
                            ins = pe.transpose(bank[base + i][:, kk * SEQ + b * P:kk * SEQ + (b + 1) * P],
                                               src[:, b, k * P:(k + 1) * P], ident)
                    ins.then_inc(turned, 1)

            def channel_rows(u, j, dst):
                s = arrive(u, j)
                w = parts(s, KT)
                for c in range(2):
                    for k in range(KT):
                        ins = product(dst[:, c * SEQ:(c + 1) * SEQ], cut(w, everything, k, slice(c * P, (c + 1) * P)),
                                      cut(hT, everything, k, everything), k == 0, k == KT - 1)
                return ins, s

            def token_rows(u, j, dst):
                s = arrive(u, j)
                w = parts(s, KT)
                for b in range(NB):
                    for k in range(KT):
                        ins = product(dst[:, b * DB:(b + 1) * DB], cut(hT, everything, k, slice(b * P, (b + 1) * P)),
                                      cut(w, everything, k, everything), k == 0, k == KT - 1)
                return ins, s

            def wide_rows(u, j, nk, k0, last_k, lhs, dst, events=None, free=None):
                s = arrive(u, j)
                n = UNIT // nk // 512
                w = parts(s, nk)
                for half in range(n):
                    for b in range(NB):
                        if free:
                            free(half, b)
                        for k in range(nk):
                            ins = product(dst(half, b), cut(lhs, everything, k0 + k, slice(b * P, (b + 1) * P)),
                                          cut(w, everything, k, slice(half * 512, (half + 1) * 512)),
                                          k0 + k == 0, k0 + k == last_k)
                        last = half == n - 1 and b == NB - 1
                        if events and not last:
                            ins.then_inc(events, 1)
                return ins, s


            pe.wait_ge(loaded, 64)
            for l in range(2):
                U = Units(BASE[l])
                pe.wait_ge(normed, NB * (2 * l + 1))
                turn(3 * l, H, 0)
                pe.wait_ge(small_lo, l + 1)
                for b in range(NB):
                    for k in range(KT):
                        if b == 0:
                            pe.wait_ge(turned_lo, KT * 3 * l + k + 1)
                        cols = slice(l * KT * NH + k * NH, l * KT * NH + (k + 1) * NH)
                        ins = product(bank[4][:, b * NH:(b + 1) * NH], cut(hT, everything, k, slice(b * P, (b + 1) * P)),
                                      cut((smallw_hi, smallw_lo), everything, cols), k == 0, k == KT - 1)
                ins.then_inc(forget_ready, 1)

                def project(u):
                    if u >= 4:
                        pe.wait_ge(taken, 13 * l + (1, 2, 3, 5, 7)[u - 4])
                    ins, s = (channel_rows if u < 3 else token_rows)(U, u, bank[u % 4])
                    ins.then_inc(used[s], 1)

                def s5_operands():
                    pe.wait_ge(s5_spread, l + 1)
                    for ri in range(2):
                        for th in range(CT):
                            ins = pe.transpose(bank[6][:, (2 * ri + th) * P:(2 * ri + th + 1) * P],
                                               s5b[:, ri, 4 * th:4 * th + 4, :, :].rearrange("p t s h -> p (t s h)"), ident)
                    ins.then_inc(s5_turned, 1)
                    for ri in range(2):
                        for th in range(CT):
                            ins = pe.transpose(bank[7][:, (2 * ri + th) * P:(2 * ri + th + 1) * P],
                                               s5c[:, ri, th, :, :].rearrange("p s n -> p (s n)"), ident)
                    ins.then_inc(s5_turned, 1)

                def bu_of(t):
                    n, jj, th = ST * l + t, t % 4, t // 4
                    if t == 0:
                        pe.wait_ge(taken, 13 * l + 3)
                        pe.wait_ge(s5_lhs, 3 * (l + 1))
                    if t >= 2:
                        pe.wait_ge(bu_taken, n - 1)
                    rows = slice(32 * jj, 32 * jj + 32)
                    for ri in range(2):
                        ins = pe.matmul(bank[6 + t % 2][:, ri * SEQ:(ri + 1) * SEQ], BT[rows, ri, th, :], uT[rows, th, :],
                                        start=True, stop=True)
                    ins.then_inc(bu_ready, 1)

                def turn_qk(kind, which):
                    pe.wait_ge(qk_normed, 2 * (2 * l + kind) + which + 1)
                    i = 2 * kind + which
                    if i == 0:
                        pe.wait_ge(bu_taken, ST * (l + 1))
                    if i == 3:
                        pe.wait_ge(conv_vare, l + 1)
                    b5 = bank[(6, 7, 5, 4)[i]]
                    for hp in range(CT):
                        for b in range(NB):
                            ins = pe.transpose(b5[:, hp * SEQ + b * P:hp * SEQ + (b + 1) * P],
                                               qk[:, which, b, hp * P:(hp + 1) * P], ident)
                    ins.then_inc(qk_turned, 1)

                def qk_of(kind, h):
                    r0 = HD * (h % 2)
                    q, k = (qT[r0:r0 + HD, kind, which, h // 2, :] for which in range(2))
                    return q, k

                def fox_scores(h):
                    if h == 0:
                        pe.wait_ge(forget_tri, l + 1)
                        pe.wait_ge(qk_gained, 4 * l + 2)
                    if h >= 2:
                        pe.wait_ge(p_exp, 2 * (NH * l + h - 1))
                    q, k = qk_of(0, h)
                    b = bank[6 + h % 2]
                    mm = lambda o, a, c, st, sp_: pe.matmul(o, a, c, start=st, stop=sp_, skip_group_check=True)
                    mm(b[:, 0:P], q[:, 0:P], k[:, 0:P], True, False)
                    mm(b[:, 0:P], TL[:, h, 0, :], const("later"), False, False)
                    mm(b[:, 0:P], ident, const("causal"), False, True)
                    mm(b[:, P:3 * P], q[:, P:2 * P], k, True, False)
                    mm(b[:, P:2 * P], TL[:, h, 1, :], const("later"), False, False)
                    both = C[:, CONST["ones"][0]:CONST["later"][1]]
                    mm(b[:, P:3 * P], TL[:, h, 2, :], both, False, False)
                    mm(b[:, 2 * P:3 * P], ident, const("causal"), False, True).then_inc(score, 1)

                def turn_p(h):
                    pe.wait_ge(p_norm, NH * l + h + 1)
                    if h == 0:
                        pe.wait_ge(qk_gained, 4 * l + 4)
                    else:
                        pe.wait_ge(p_taken, NH * l + h)
                    for i in range(3):
                        ins = pe.transpose(bank[4][:, i * P:(i + 1) * P], sc[:, h % 2, i * P:(i + 1) * P], ident)
                    ins.then_inc(p_turned, 1)

                def attend(kind, h, ready, count, ev):
                    pe.wait_ge(ready, count)
                    if h == 0:
                        if kind == 0:
                            pe.wait_ge(qk_gained, 4 * l + 3)
                        else:
                            pe.wait_ge(ys_low, 4 * l + 2)
                    r0, hp = HD * (h % 2), h // 2
                    o = bank[5][r0:r0 + HD, hp * SEQ:(hp + 1) * SEQ]
                    v = [V[:, kind, b, h * HD:(h + 1) * HD] for b in range(NB)]
                    pe.matmul(o, v[0], pT[:, h % 2, 0:2 * P], start=True, stop=False, skip_group_check=True)
                    pe.matmul(o[:, P:2 * P], v[1], pT[:, h % 2, 2 * P:3 * P], start=False, stop=True,
                              skip_group_check=True).then_inc(ev, 1)

                def fox_attend(h):
                    attend(0, h, p_taken, NH * l + h + 1, fox_out)

                def sb_attend(h):
                    attend(1, h, a_exp, NH * l + h + 1, sb_out)

                def sb_scores(pair):
                    for i in range(2):
                        h = 2 * pair + i
                        if pair == 0:
                            pe.wait_ge(qk_gained, 4 * l + 4)
                            pe.wait_ge(p_exp, 2 * (NH * l + 3 + i))
                        else:
                            pe.wait_ge(a_exp, NH * l + i + 1)
                        q, k = qk_of(1, h)
                        pe.matmul(bank[6 + i][:, 0:2 * P], k[:, 0:P], q, start=True, stop=False, skip_group_check=True)
                        pe.matmul(bank[6 + i][:, 2 * P:3 * P], k[:, P:2 * P], q[:, P:2 * P], start=False, stop=True,
                                  skip_group_check=True).then_inc(z_ready, 1)

                def sb_sums(pair):
                    for i in range(2):
                        pe.wait_ge(z_soft, NH * l + 2 * pair + i + 1)
                        b, s = bank[6 + i], sc[:, i, :]
                        mm = lambda o, a, c: pe.matmul(o, a, c, start=False, stop=False, skip_group_check=True)
                        mm(b[:, 0:2 * P], const("suffix"), s[:, 0:2 * P])
                        mm(b[:, P:2 * P], const("minus"), s[:, 2 * P:3 * P])
                        mm(b[:, 2 * P:3 * P], const("suffix"), s[:, 2 * P:3 * P])
                        mm(b[:, 0:P], ident, const("past"))
                        mm(b[:, 2 * P:3 * P], ident, const("past")).then_inc(z_cum, 1)

                def conv_stat(which):
                    if which == 0:
                        pe.wait_ge(conv_sum, 2 * l + 2)
                        pe.wait_ge(forget_in, l + 1)
                    else:
                        pe.wait_ge(conv_sq, l + 1)
                    for c in range(CT):
                        ins = pe.matmul(bank[4][:, which * SEQ:(which + 1) * SEQ], const("mean"),
                                        (ca if which == 0 else cs)[:, c, :], start=(c == 0), stop=(c == CT - 1),
                                        skip_group_check=True)
                    ins.then_inc((conv_mean, conv_var)[which], 1)

                def s5_out(pair):
                    pe.wait_ge(s5_state, ST // 2 * l + pair + 1)
                    if pair == 0:
                        pe.wait_ge(p_taken, NH * (l + 1))
                    for t in (2 * pair, 2 * pair + 1):
                        jj, th = t % 4, t // 4
                        o = bank[4][32 * jj:32 * jj + 32, th * SEQ:(th + 1) * SEQ]
                        for ri in range(2):
                            ins = pe.matmul(o, CTt[:, ri, 32 * t:32 * t + 32], bu[:, t, ri, :], start=(ri == 0),
                                            stop=(ri == 1), skip_group_check=True)
                    if pair == 3:
                        ins.then_inc(s5_y, 1)

                def glu():
                    pe.wait_ge(gelu_out, l + 1)
                    pe.wait_ge(a_exp, NH * l + 3)
                    w = par(l, "w_glu").rearrange("p (k c) -> p k c", k=CT)
                    g = tmp[:, 2, :].rearrange("p (a c) -> p a c", a=CT)
                    for c in range(CT):
                        for k in range(CT):
                            ins = pe.matmul(bank[6][:, c * SEQ:(c + 1) * SEQ], w[:, k, c * P:(c + 1) * P], g[:, k, :],
                                            start=(k == 0), stop=(k == CT - 1), skip_group_check=True)
                    ins.then_inc(glu_ready, 1)

                def gates(n, half, kh):
                    if kh == 0:
                        if n == 0:
                            pe.wait_ge(taken, 13 * l + (13, 12)[half])
                    j = 9 + 5 * n + 2 * half + kh

                    def free(_, b):
                        if kh == 0 and n:
                            pe.wait_ge(gated, 16 * l + 4 * (n - 1) + 2 * half + b + 1)

                    ins, s = wide_rows(U, j, 4, 4 * kh, KT - 1, hT, lambda _, b: bank[2 * half + b][:, :],
                                       gate_ready if kh else None, free)
                    ins.then_inc(used[s], 1)

                def branch_rows(n):
                    pe.wait_ge(ys_low, 4 * l + n + 1)
                    ys = (ys_hi[:, n % 2, :, :], ys_lo[:, n % 2, :, :])
                    ins, s = wide_rows(U, 13 + 5 * n, CT, 0, CT - 1, ys, lambda half, b: bank[2 * half + b][:, :], branch,
                                       lambda half, b: pe.wait_ge(gate_tanh, 16 * l + 4 * n + 2 * half + b + 1))
                    ins.then_inc(used[s], 1)

                for u in range(9):
                    project(u)
                    if u == 1:
                        s5_operands()
                    if 3 <= u <= 6:
                        bu_of(2 * (u - 3))
                        bu_of(2 * (u - 3) + 1)
                    if u == 7:
                        turn_qk(0, 0)
                        turn_qk(0, 1)
                        conv_stat(0)
                gates(0, 0, 0)
                conv_stat(1)
                fox_scores(0)
                gates(0, 0, 1)
                turn_qk(1, 0)
                turn_qk(1, 1)
                fox_scores(1)
                gates(0, 1, 0)
                turn_p(0)
                fox_scores(2)
                gates(0, 1, 1)
                fox_attend(0)
                turn_p(1)
                fox_scores(3)
                branch_rows(0)
                fox_attend(1)
                turn_p(2)
                gates(1, 0, 0)
                fox_attend(2)
                turn_p(3)
                sb_scores(0)
                gates(1, 0, 1)
                fox_attend(3)
                gates(1, 1, 0)
                sb_sums(0)
                gates(1, 1, 1)
                sb_attend(0)
                sb_attend(1)
                sb_scores(1)
                branch_rows(1)
                gates(2, 0, 0)
                sb_sums(1)
                gates(2, 0, 1)
                sb_attend(2)
                sb_attend(3)
                gates(2, 1, 0)
                s5_out(0)
                gates(2, 1, 1)
                s5_out(1)
                branch_rows(2)
                gates(3, 0, 0)
                s5_out(2)
                s5_out(3)
                gates(3, 0, 1)
                gates(3, 1, 0)
                glu()
                gates(3, 1, 1)
                branch_rows(3)

                pe.wait_ge(merged, 12 * (l + 1))
                pe.wait_ge(glu_tanh, l + 1)
                turn(3 * l + 1, M, 4)
                for i in range(4):
                    def free(half, b, i=i):
                        if i == 0 and half == 0 and b == 0:
                            pe.wait_ge(turned_lo, KT * (3 * l + 2))
                    ins, s = wide_rows(U, 29 + i, 2, 2 * i, KT - 1, hT, lambda half, b: bank[2 * half + b][:, :], None, free)
                    ins.then_inc(used[s], 1)
                if upto <= 2 * l + 1:
                    break

                pe.wait_ge(normed, NB * (2 * l + 2))
                turn(3 * l + 2, H, 0)
                pe.wait_ge(turned_lo, KT * (3 * l + 3))
                if l == 0:
                    def hidden(u, j, c, odd, which):
                        ins, s = channel_rows(u, j, bank[2 * odd + which])
                        ins.then_inc(used[s], 1)

                    def down(u, j, c, odd, first, last):
                        pe.wait_ge(g_lo, c + 1)
                        s = arrive(u, j)
                        w = parts(s, 2)
                        g = (ys_hi[:, odd, :, :], ys_lo[:, odd, :, :])
                        for half in range(2):
                            for b in range(NB):
                                for f in range(2):
                                    ins = product(bank[4 + 2 * half + b][:, :], cut(g, everything, f, slice(b * P, (b + 1) * P)),
                                                  cut(w, everything, f, slice(half * 512, (half + 1) * 512)),
                                                  first and f == 0, last and f == 1)
                        ins.then_inc(used[s], 1)

                    u = Units(DENSE0)
                    hidden(u, 0, 0, 0, 0)
                    hidden(u, 1, 0, 0, 1)

                    def pair(i, first):
                        u = Units(DENSE0, i * 2)
                        for m in range(2):
                            c, odd = i * 2 + 1 + m, 1 - m
                            if not (first and m == 0):
                                pe.wait_ge(g_ready, c - 1)
                            hidden(u, 2 + 3 * m, c, odd, 0)
                            hidden(u, 3 + 3 * m, c, odd, 1)
                            down(u, 4 + 3 * m, i * 2 + m, m, first and m == 0, False)

                    pair(0, True)
                    with pe.Fori(1, PAIRS) as i:
                        pair(i, False)
                    down(Units(DENSE0), FFN_UNITS - 1, NCH - 1, 0, False, True)
                if upto <= 2 * l + 2:
                    break

            if upto >= 4:
                pe.wait_ge(small_lo, 3)
                for b in range(NB):
                    for k in range(KT):
                        cols = slice(2 * KT * NH + k * NE, 2 * KT * NH + (k + 1) * NE)
                        ins = product(bank[4][:, b * NE:(b + 1) * NE], cut(hT, everything, k, slice(b * P, (b + 1) * P)),
                                      cut((smallw_hi, smallw_lo), everything, cols), k == 0, k == KT - 1)
                ins.then_inc(logits, 1)
                pe.wait_ge(chosen, 1)
                sel = route[:, 5, :, :]
                pe.matmul(bank[5][:, 0:NE], const("tri_strict"), sel[:, 0, :], start=True, stop=True)
                pe.matmul(bank[5][:, NE:2 * NE], const("tri_strict"), sel[:, 1, :], start=True, stop=False,
                          skip_group_check=True)
                pe.matmul(bank[5][:, NE:2 * NE], const("ones"), sel[:, 0, :], start=False, stop=True, skip_group_check=True)
                pe.matmul(bank[5][:, 2 * NE:3 * NE], const("ones"), sel[:, 0, :], start=True, stop=False,
                          skip_group_check=True)
                pe.matmul(bank[5][:, 2 * NE:3 * NE], const("ones"), sel[:, 1, :], start=False, stop=True,
                          skip_group_check=True).then_inc(places, 1)

                def expert(n, first):
                    pe.wait_ge(picked, n * NB + NB)
                    for b in range(NB):
                        ins = pe.transpose(bank[2][:, b * P:(b + 1) * P], G2[:, 0, b * P:(b + 1) * P], ident)
                    ins.then_inc(pick_turned, 1)
                    if not first:
                        pe.wait_ge(added, n * 4)
                    for k in range(KT):
                        for b in range(NB):
                            ins = pe.matmul(bank[6 + k // 4][:, (k % 4) * P:(k % 4 + 1) * P], H[:, b, k * P:(k + 1) * P],
                                            G2[:, 0, b * P:(b + 1) * P], start=(b == 0), stop=(b == NB - 1),
                                            skip_group_check=True)
                        if k % 4 == 3:
                            ins.then_inc(gathered, 1)

                    def hidden(u, j, c, odd, which):
                        s = arrive(u, j)
                        w = parts(s, KT)
                        for k in range(KT):
                            if isinstance(c, int) and c == 0 and which == 0:
                                pe.wait_ge(gather_lo, n * KT + k + 1)
                            ins = product(bank[2 * odd + which][:, 0:CH], cut(hT, everything, k, slice(0, P)),
                                          cut(w, everything, k, everything), k == 0, k == KT - 1)
                        ins.then_inc(used[s], 1)

                    def turn_hidden(c, odd):
                        pe.wait_ge(g_ready, n * NCH + NCH + c + 1)
                        for f in range(2):
                            ins = pe.transpose(bank[6][:, f * P:(f + 1) * P], gated_h[:, odd, 0, f * P:(f + 1) * P], ident)
                        ins.then_inc(g_turned, 1)

                    def down(u, j, c, odd, first_, last):
                        pe.wait_ge(g_lo, n * NCH + NCH + c + 1)
                        s = arrive(u, j)
                        w = parts(s, 2)
                        g = (ys_hi[:, odd, 0, :], ys_lo[:, odd, 0, :])
                        for half in range(2):
                            for f in range(2):
                                ins = product(bank[4 + half][:, :], cut(g, everything, slice(f * P, (f + 1) * P)),
                                              cut(w, everything, f, slice(half * 512, (half + 1) * 512)),
                                              first_ and f == 0, last and f == 1)
                        ins.then_inc(used[s], 1)

                    u = Units(MOE0, n * NCH)
                    hidden(u, 0, 0, 0, 0)
                    hidden(u, 1, 0, 0, 1)

                    def pair(i, first_):
                        v = Units(MOE0, n * NCH + i * 2)
                        for m in range(2):
                            c, odd = i * 2 + 1 + m, 1 - m
                            if first_ and m == 0:
                                pe.wait_ge(pick_taken, n + 1)
                            hidden(v, 2 + 3 * m, c, odd, 0)
                            turn_hidden(i * 2 + m, m)
                            hidden(v, 3 + 3 * m, c, odd, 1)
                            down(v, 4 + 3 * m, i * 2 + m, m, first_ and m == 0, False)

                    pair(0, True)
                    with pe.Fori(1, PAIRS) as i:
                        pair(i, False)
                    turn_hidden(NCH - 1, 0)
                    down(Units(MOE0, n * NCH), FFN_UNITS - 1, NCH - 1, 0, False, True)
                    for b in range(NB):
                        for half in range(2):
                            i = 2 * b + half
                            pe.wait_ge(y_taken, n * 2 + half + 1)
                            if b:
                                pe.wait_ge(added, n * 4 + half + 1)
                            pe.matmul(bank[6 + i % 2][:, :], pT[:, 0, b * P:(b + 1) * P],
                                      M[:, 0, half * 512:(half + 1) * 512], start=True, stop=True).then_inc(spread, 1)

                expert(0, True)
                with pe.Fori(1, NE) as e:
                    expert(e, False)
                pe.wait_ge(spill_known, 1)
                n_spill = pe.value_load(spill_i[0:1, 0:1], min_val=0, max_val=N_SPILL)
                for t in range(N_SPILL):
                    with pe.If(n_spill > t):
                        expert(NE + t, False)


def constants():
    i = np.arange(P)
    row, col = i[:, None], i[None, :]
    t = {
        "ident": row == col, "tri": row <= col, "tri_strict": row < col, "ones": np.ones((P, P)),
        "later": row > col, "suffix": -1.0 * (row >= col), "minus": -np.ones((P, P)), "mean": np.full((P, P), 1.0 / DB),
        "causal": np.where(col > row, -BIG, 0.0), "past": np.where(row < col, 0.0, -BIG),
        "keep": np.concatenate([row < col, np.ones((P, P)), row < col], axis=1),
        "iota": np.broadcast_to(col, (P, P)), "parity": np.stack([(i // GH) % 2 == 0, (i // GH) % 2 == 1], axis=1),
        "side": np.stack([i < GP, i >= GP], axis=1), "iota8": np.broadcast_to(np.arange(NE), (P, NE)),
    }
    out = np.zeros((P, N_CONST), np.float32)
    for name, (a, b) in CONST.items():
        out[:, a:b] = t[name]
    return out


def lay_out(a):
    def cols(v):
        return v.reshape(-1, P).T

    def rows(v):
        return np.broadcast_to(v, (P, v.size))

    def state(v):
        return v.reshape(ST, 2, GP).transpose(1, 2, 0).reshape(P, ST)

    params = []
    for l in range(2):
        t = {
            "g_mix": cols(a["g_mix"][l]), "g_ffn": cols(a["g_ffn"][l]), "b_forget": rows(a["b_forget"][l]),
            "lam_re": state(a["s5_lam_re"][l]), "lam_im": state(a["s5_lam_im"][l]),
            "log_dt": state(np.broadcast_to(a["s5_log_dt"][l][:, None], (NG, GP))),
            "s5_d": cols(a["s5_d"][l]), "conv_b": cols(a["conv_b"][l]), "ln_g": cols(a["conv_ln_g"][l]),
            "ln_b": cols(a["conv_ln_b"][l]),
            "conv_w": a["conv_w"][l].reshape(CONVW, CT, P).transpose(2, 1, 0).reshape(P, CT * CONVW),
            "w_glu": a["s5_w_glu"][l].reshape(CT, P, DB).transpose(1, 0, 2).reshape(P, CT * DB),
            "w_forget": a["w_in"][l][:, IN_F:IN_F + NH].reshape(KT, P, NH).transpose(1, 0, 2).reshape(P, KT * NH),
        }
        for n in ("fox_q", "fox_k", "sb_q", "sb_k"):
            t[n] = cols(np.tile(a[n + "_gain"][l], P // HD))
        for n in ("b_re", "b_im"):
            t[n] = a["s5_" + n][l].reshape(ST, 2, GP, GH).transpose(1, 2, 0, 3).reshape(P, ST * GH)
        for n in ("c_re", "c_im"):
            t[n] = a["s5_" + n][l].reshape(CT, P, GP).transpose(1, 0, 2).reshape(P, CT * GP)
        params += [t[n] for n in PARAM]
    router = [a["router_w"][0].reshape(KT, P, NE).transpose(1, 0, 2).reshape(P, KT * NE), rows(a["router_b"][0])]
    return np.concatenate(params, axis=1), np.concatenate(router, axis=1)


BIG_INPUTS = ["x", "w_in", "w_branch", "w_out", "ffn_w1", "ffn_w3", "ffn_w2", "moe_w1", "moe_w3", "moe_w2"]


def kernel(**inputs):
    import concourse.bacc as bacc
    from concourse.bass_utils import run_bass_kernel_spmd

    a = {k: np.ascontiguousarray(v) for k, v in inputs.items()}
    arrays = {n: a[n] for n in BIG_INPUTS}
    arrays["consts"] = constants()
    arrays["params"], arrays["router"] = (np.ascontiguousarray(t) for t in lay_out(a))
    nc = bacc.Bacc("TRN2", target_bir_lowering=False, num_devices=1, dynamic_dma_scratch_size=1024)
    aps = {n: nc.dram_tensor(n + "_dram", v.shape, mybir.dt.from_np(v.dtype), kind="ExternalInput").ap()
           for n, v in arrays.items()}
    out = nc.dram_tensor("out_dram", a["x"].shape, F32, kind="ExternalOutput").ap()
    build(nc, out=out, **aps)
    r = run_bass_kernel_spmd(nc, [{n + "_dram": v for n, v in arrays.items()}], core_ids=[0])
    return r.results[0]["out_dram"]
```

```python
from contextlib import ExitStack

import numpy as np

import concourse.bass as bass
from concourse import mybir

ALU = mybir.AluOpType
ACT = mybir.ActivationFunctionType
AX_X = mybir.AxisListType.X
F32 = mybir.dt.float32
F32R = mybir.dt.float32r
I32 = mybir.dt.int32
U32 = mybir.dt.uint32

P = 128
D = 1024
KT = D // P
SEQ = 256
NB = SEQ // P
DB = 256
CT = DB // P
HD = 64
NH = DB // HD
CONVW = 31
PAD = CONVW - 1
DFF = 2816
CH = 256
NCH = DFF // CH
NE = 8
EPS = 1e-6
BIG = 1e30
NG, GP, GH = 16, 64, 16
ST = NG // 2

IN_S5, IN_FOX, IN_F = 0, DB, 4 * DB
IN_CONV = IN_F + NH
IN_SB = IN_CONV + 2 * DB
IN_GATE = IN_SB + 3 * DB
D_PROJ = IN_GATE + 4 * D

UNIT = 2048
RING = 3
MIX_UNITS = 33
FFN_UNITS = 3 * NCH
assert MIX_UNITS % RING == 0 and FFN_UNITS % RING == 0

CONST = {}
_at = 0
for _name, _n in (("ident", P), ("tri", P), ("tri_strict", P), ("ones", P), ("later", P), ("suffix", P),
                  ("minus", P), ("mean", P), ("causal", P), ("past", P), ("keep", 3 * P), ("iota", P),
                  ("parity", 2), ("side", 2), ("iota8", NE)):
    CONST[_name] = (_at, _at + _n)
    _at += _n
N_CONST = _at

PARAM = {}
_at = 0
for _name, _n in (("g_mix", KT), ("g_ffn", KT), ("b_forget", NH), ("fox_q", 1), ("fox_k", 1), ("sb_q", 1),
                  ("sb_k", 1), ("lam_re", ST), ("lam_im", ST), ("log_dt", ST), ("b_re", ST * GH),
                  ("b_im", ST * GH), ("c_re", CT * GP), ("c_im", CT * GP), ("s5_d", CT),
                  ("conv_w", CT * CONVW), ("conv_b", CT), ("ln_g", CT), ("ln_b", CT), ("w_glu", CT * DB),
                  ("w_forget", KT * NH)):
    PARAM[_name] = (_at, _at + _n)
    _at += _n
N_PARAM = _at
N_ROUTER = KT * NE + NE

TWO_PI_1, TWO_PI_2 = 6.28125, 0.0019340515136719
TWO_PI_3 = 2 * np.pi - TWO_PI_1 - TWO_PI_2
ROUND = 1.5 * 2.0 ** 23
PI_F32 = 3.1415925


class Units:

    def __init__(self, base, steps=0):
        assert base % RING == 0
        self.base, self.steps = base // RING, steps

    def slot(self, j):
        return j % RING

    def earlier(self, j):
        return self.base + self.steps + j // RING

    def is_first(self, j):
        return isinstance(self.steps, int) and self.earlier(j) == 0


class Chain:

    def __init__(self, eng, sem):
        self.eng, self.sem, self.n, self.more = eng, sem, 0, 0

    def __call__(self, ins):
        self.n += 1
        ins.then_inc(self.sem, 1)
        self.eng.wait_ge(self.sem, self.more + self.n)

    def mark(self, ins):
        self.n += 1
        ins.then_inc(self.sem, 1)

    def settle(self):
        self.eng.wait_ge(self.sem, self.more + self.n)


def build(nc, x, consts, params, router, w_in, w_branch, w_out, ffn_w1, ffn_w3, ffn_w2, moe_w1, moe_w3, moe_w2,
          out):
    with ExitStack() as ctx:
        def sb(name, shape, dt=F32):
            return ctx.enter_context(nc.sbuf_tensor(name, shape, dt))

        def sem(name):
            return ctx.enter_context(nc.semaphore(name))

        bank = [ctx.enter_context(nc.psum_tensor(f"bank{i}", [P, 512], F32)) for i in range(8)]

        raw = sb("raw", [P, RING, UNIT])
        high = sb("high", [P, RING, UNIT], F32R)
        low = sb("low", [P, RING, UNIT], F32R)
        X = sb("X", [P, NB, D])
        H = sb("H", [P, NB, D])
        G2 = sb("G2", [P, NB, D])
        M = sb("M", [P, NB, D])
        hT_hi = sb("hT_hi", [P, KT, SEQ], F32R)
        hT_lo = sb("hT_lo", [P, KT, SEQ], F32R)
        C = sb("C", [P, N_CONST])
        PR = sb("PR", [P, 2, N_PARAM])
        RT = sb("RT", [P, N_ROUTER])
        smallw_hi = sb("smallw_hi", [P, 2 * KT * NH + KT * NE], F32R)
        smallw_lo = sb("smallw_lo", [P, 2 * KT * NH + KT * NE], F32R)
        stat = sb("stat", [P, 8])
        s5p = sb("s5p", [P, 20, ST])
        s5b = sb("s5b", [P, 2, ST, 2, GH])
        s5c = sb("s5c", [P, 2, CT, 2, GP])
        BT = sb("BT", [P, 2, CT, P])
        CTt = sb("CTt", [P, 2, DB])
        uT = sb("uT", [P, CT, SEQ])
        bu = sb("bu", [P, ST, 2, SEQ])
        tmp = sb("tmp", [P, 4, 2 * SEQ])
        silu = bu[:, 0:2, :, :]
        gated_h = bu[:, 2:4, :, :]
        upad = G2[:, 0, 0:CT * (PAD + SEQ)].rearrange("p (a c) -> p a c", a=CT)
        ca = sb("ca", [P, CT, SEQ])
        cs = sb("cs", [P, CT, SEQ])
        lnv = sb("lnv", [P, 3, SEQ])
        qk = H[:, 0, :].rearrange("p (w b c) -> p w b c", w=2, b=NB)
        sq = G2[:, 1, :].rearrange("p (w b c) -> p w b c", w=2, b=NB)
        nrm = sb("nrm", [P, 2, 2, NB * NH])
        lf = sb("lf", [P, 4, NB * NH])
        TL = M[:, :, :].rearrange("p a c -> p (a c)")[:, 0:NH * 3 * P].rearrange("p (h i c) -> p h i c", h=NH, i=3)
        sc = sb("sc", [P, 2, 3 * P])
        pT = sb("pT", [P, 2, 3 * P])
        mx = sb("mx", [P, 2, NH, 2])
        rs = sb("rs", [P, 2, NH, 2])
        route = sb("route", [P, 12, NB, NE])
        top_at = sb("top_at", [P, NB, NE], U32)
        spill = sb("spill", [P, 4, NE])
        spill_i = sb("spill_i", [1, 4], I32)
        ys_hi = sb("ys_hi", [P, 2, CT, SEQ], F32R)
        ys_lo = sb("ys_lo", [P, 2, CT, SEQ], F32R)

        with ExitStack() as mixers:
            def mixer_sb(name, shape):
                return mixers.enter_context(nc.sbuf_tensor(name, shape, F32))

            rot_c = mixer_sb("rot_c", [P, ST, SEQ])
            rot_s = mixer_sb("rot_s", [P, ST, SEQ])
            V = mixer_sb("V", [P, 2, NB, DB])
            qT = mixer_sb("qT", [P, 2, 2, CT, SEQ])
        h_parts = [sb(f"h_parts{i}", [P, NB, D], F32R) for i in range(2)]
        y_parts = [sb(f"y_parts{i}", [P, D], F32R) for i in range(2)]
        picks = sb("picks", [P, NB, P], F32R)
        back = sb("back", [P, NB * P], F32R)
        picks_back = G2[:, 0, 0:NB * P].rearrange("p (b c) -> p b c", b=NB)

        def const(name, a=0, b=None, rows=P):
            lo_, hi_ = CONST[name]
            return C[0:rows, lo_ + a:(hi_ if b is None else lo_ + b)]

        def par(l, name, a=0, b=None):
            lo_, hi_ = PARAM[name]
            return PR[:, l, lo_ + a:(hi_ if b is None else lo_ + b)]

        ident = const("ident")

        raw_ready = [sem(f"raw_ready{s}") for s in range(RING)]
        hi_ready = [sem(f"hi_ready{s}") for s in range(RING)]
        lo_ready = [sem(f"lo_ready{s}") for s in range(RING)]
        used = [sem(f"used{s}") for s in range(RING)]
        loaded = sem("loaded")
        stored = sem("stored")
        act_step = sem("act_step")
        dve_step = sem("dve_step")
        small_hi = sem("small_hi")
        small_lo = sem("small_lo")
        squared = sem("squared")
        mean_sq = sem("mean_sq")
        rms_root = sem("rms_root")
        normed = sem("normed")
        turned = sem("turned")
        turned_hi = sem("turned_hi")
        turned_lo = sem("turned_lo")
        s5_exp = sem("s5_exp")
        s5_arg = sem("s5_arg")
        s5_sin = sem("s5_sin")
        s5_spread = sem("s5_spread")
        s5_turned = sem("s5_turned")
        s5_lhs = sem("s5_lhs")
        s5_rot = sem("s5_rot")
        forget_ready = sem("forget_ready")
        forget_in = sem("forget_in")
        forget_ln = sem("forget_ln")
        forget_tri = sem("forget_tri")
        taken = sem("taken")
        bu_ready = sem("bu_ready")
        bu_taken = sem("bu_taken")
        conv_sum = sem("conv_sum")
        conv_mean = sem("conv_mean")
        conv_cent = sem("conv_cent")
        conv_sq = sem("conv_sq")
        conv_var = sem("conv_var")
        conv_vare = sem("conv_vare")
        conv_root = sem("conv_root")
        conv_lin = sem("conv_lin")
        conv_tanh = sem("conv_tanh")
        conv_out = sem("conv_out")
        qk_mean = sem("qk_mean")
        qk_root = sem("qk_root")
        qk_normed = sem("qk_normed")
        qk_turned = sem("qk_turned")
        qk_gained = sem("qk_gained")
        score = sem("score")
        row_max = sem("row_max")
        p_exp = sem("p_exp")
        p_norm = sem("p_norm")
        p_turned = sem("p_turned")
        p_taken = sem("p_taken")
        fox_out = sem("fox_out")
        z_ready = sem("z_ready")
        z_ln = sem("z_ln")
        z_soft = sem("z_soft")
        z_cum = sem("z_cum")
        a_exp = sem("a_exp")
        sb_out = sem("sb_out")
        s5_state = sem("s5_state")
        s5_y = sem("s5_y")
        gelu_in = sem("gelu_in")
        gelu_tanh = sem("gelu_tanh")
        gelu_out = sem("gelu_out")
        glu_ready = sem("glu_ready")
        glu_tanh = sem("glu_tanh")
        glu_out = sem("glu_out")
        ys_high = sem("ys_high")
        ys_low = sem("ys_low")
        gate_ready = sem("gate_ready")
        gate_tanh = sem("gate_tanh")
        branch = sem("branch")
        gated = sem("gated")
        merged = sem("merged")
        silu_ready = sem("silu_ready")
        g_ready = sem("g_ready")
        g_hi = sem("g_hi")
        g_lo = sem("g_lo")
        logits = sem("logits")
        top_gap = sem("top_gap")
        top_exp = sem("top_exp")
        chosen = sem("chosen")
        places = sem("places")
        routed = sem("routed")
        spill_known = sem("spill_known")
        picked = sem("picked")
        moe_raw = [sem(f"moe_raw{i}") for i in range(6)]
        moe_hi = [sem(f"moe_hi{i}") for i in range(6)]
        moe_lo = [sem(f"moe_lo{i}") for i in range(6)]
        moe_used = [sem(f"moe_used{i}") for i in range(6)]
        moe_silu = sem("moe_silu")
        moe_gated = sem("moe_gated")
        moe_turned = sem("moe_turned")
        moe_g_hi = sem("moe_g_hi")
        moe_g_lo = sem("moe_g_lo")
        picked_back = sem("picked_back")
        back_turned = sem("back_turned")
        side_done = sem("side_done")
        y_hi = sem("y_hi")
        y_lo = sem("y_lo")
        h_high = sem("h_high")
        h_low = sem("h_low")
        gathered = sem("gathered")
        gather_hi = sem("gather_hi")
        spread = sem("spread")
        finished = sem("finished")
        x_mixed = sem("x_mixed")
        block = ctx.enter_context(nc.Block())

        ORDER = (2, 1, 3, 0)
        COLS = [IN_CONV, IN_CONV + DB, IN_S5] + [IN_FOX + DB * i for i in range(3)] + [IN_SB + DB * i for i in range(3)]
        mix_src = []

        def k_rows(w, k0, nk, c0, n):
            return w.rearrange("(k p) c -> p k c", p=P)[:, k0:k0 + nk, c0:c0 + n]

        for l in range(2):
            src = [k_rows(w_in[l], 0, KT, c, DB) for c in COLS]
            for n in ORDER:
                for half in range(2):
                    for kh in range(2):
                        src.append(k_rows(w_in[l], 4 * kh, 4, IN_GATE + n * D + half * 512, 512))
                src.append(k_rows(w_branch[l, n], 0, CT, 0, D))
            src += [k_rows(w_out[l], 2 * i, 2, 0, D) for i in range(4)]
            assert len(src) == MIX_UNITS
            mix_src.append(src)

        def unit_view(t, s, nk):
            return t[:, s, :].rearrange("p (k c) -> p k c", k=nk)

        BASE = [0, MIX_UNITS + FFN_UNITS]
        DENSE0 = MIX_UNITS
        MIX_SPLITS = (2 * MIX_UNITS + FFN_UNITS) // RING

        PAIRS = (NCH - 1) // 2
        N_SPILL = 2 * SEQ // (P + 1)
        expert_gain = (1, "g_ffn")

        def wait_products(eng, u, j):
            eng.wait_ge(used[u.slot(j)], u.earlier(j) + 1)

        @block.sync
        def _(sp):
            sp.dma_start(C[:, :], consts).then_inc(loaded, 16)
            sp.dma_start(PR[:, :, :], params.rearrange("p (l n) -> p l n", l=2)).then_inc(loaded, 16)
            sp.dma_start(RT[:, :], router).then_inc(loaded, 16)
            sp.dma_start(X[:, :, :], x.rearrange("a (b p) d -> p (a b) d", p=P)).then_inc(loaded, 16)

            def load(u, j, src):
                s = u.slot(j)
                if not u.is_first(j):
                    sp.wait_ge(lo_ready[s], u.earlier(j))
                sp.dma_start(unit_view(raw, s, src.shape[1]), src).then_inc(raw_ready[s], 16)

            def load_ffn(base, steps, w1, w3, w2):
                w1, w3 = (w.rearrange("(k p) n -> p k n", p=P) for w in (w1, w3))
                w2 = w2.rearrange("(c p) n -> p c n", p=P)
                u = Units(base, steps)
                load(u, 0, w1[:, :, 0:CH])
                load(u, 1, w3[:, :, 0:CH])
                with sp.Fori(0, PAIRS) as i:
                    u = Units(base, steps + i * 2)
                    for m in range(2):
                        load(u, 2 + 3 * m, w1[:, :, bass.ds(i * (2 * CH) + (1 + m) * CH, CH)])
                        load(u, 3 + 3 * m, w3[:, :, bass.ds(i * (2 * CH) + (1 + m) * CH, CH)])
                        load(u, 4 + 3 * m, w2[:, bass.ds(i * 4 + 2 * m, 2), :])
                load(Units(base, steps), FFN_UNITS - 1, w2[:, 2 * NCH - 2:2 * NCH, :])

            def load_half(kind, half, g, src):
                if isinstance(g, int) and g == 0:
                    sp.wait_ge(lo_ready[kind], MIX_SPLITS)
                else:
                    sp.wait_ge(moe_lo[2 * kind + half], g)
                dst = raw[:, kind, half * UNIT // 2:(half + 1) * UNIT // 2]
                if kind < 2:
                    dst = dst.rearrange("p (k c) -> p k c", k=KT // 2)
                sp.dma_start(dst, src).then_inc(moe_raw[2 * kind + half], 16)

            def load_w1_w3(g, e, c0):
                for kind, w in enumerate((moe_w1, moe_w3)):
                    src = w[0, e].rearrange("(k p) n -> p k n", p=P)
                    for half in range(2):
                        load_half(kind, half, g, src[:, half * KT // 2:(half + 1) * KT // 2, bass.ds(c0, CH)])

            def load_w2(g, e, tile):
                src = moe_w2[0, e].rearrange("(c p) n -> p c n", p=P)
                for half in range(2):
                    load_half(2, half, g, src[:, bass.ds(tile + half, 1), :].rearrange("p a n -> p (a n)"))

            def load_chunks(n, e):
                with sp.Fori(0, NCH - 1) as i:
                    load_w1_w3(n * NCH + i + 1, e, i * CH + CH)
                    load_w2(n * NCH + i, e, i * 2)

            for l in range(2):
                u = Units(BASE[l])
                for j, src in enumerate(mix_src[l]):
                    load(u, j, src)
                if l == 0:
                    load_ffn(DENSE0, 0, ffn_w1[0], ffn_w3[0], ffn_w2[0])
            load_w1_w3(0, 0, 0)
            load_chunks(0, 0)
            with sp.Fori(1, NE) as e:
                load_w1_w3(e * NCH, e, 0)
                load_w2(e * NCH - 1, e - 1, 2 * NCH - 2)
                load_chunks(e, e)
            load_w2(NE * NCH - 1, NE - 1, 2 * NCH - 2)
            sp.wait_ge(spill_known, 1)
            n_spill = sp.value_load(spill_i[0:1, 0:1], min_val=0, max_val=N_SPILL)
            for t in range(N_SPILL):
                with sp.If(n_spill > t):
                    n = NE + t
                    e = sp.value_load(spill_i[0:1, 1 + t:2 + t], min_val=0, max_val=NE - 1)
                    load_w1_w3(n * NCH, e, 0)
                    load_chunks(n, e)
                    load_w2(n * NCH + NCH - 1, e, 2 * NCH - 2)
            sp.wait_ge(finished, 1)
            sp.dma_start(out.rearrange("a (b p) d -> p (a b) d", p=P), X[:, :, :]).then_inc(stored, 16)
            sp.wait_ge(stored, 16)

        @block.gpsimd
        def _(pool):
            def split_low(u, j):
                s = u.slot(j)
                pool.wait_ge(hi_ready[s], u.earlier(j) + 1)
                pool.tensor_tensor(low[:, s, :], raw[:, s, :], high[:, s, :].bitcast(F32),
                                   ALU.subtract).then_inc(lo_ready[s], 1)

            for l in range(2):
                with pool.Fori(0, MIX_UNITS // RING) as i:
                    for j in range(RING):
                        split_low(Units(BASE[l], i), j)
                if l == 0:
                    with pool.Fori(0, FFN_UNITS // RING) as i:
                        for j in range(RING):
                            split_low(Units(DENSE0, i), j)
            def split_half(kind, half, g):
                i, cols = 2 * kind + half, slice(half * UNIT // 2, (half + 1) * UNIT // 2)
                pool.wait_ge(moe_hi[i], g + 1)
                pool.tensor_tensor(low[:, kind, cols], raw[:, kind, cols], high[:, kind, cols].bitcast(F32),
                                   ALU.subtract).then_inc(moe_lo[i], 1)

            def split_turns(n, turns):
                for kind in range(2):
                    for half in range(2):
                        split_half(kind, half, n * NCH)
                with pool.Fori(0, turns * NCH) as i:
                    for half in range(2):
                        split_half(2, half, n * NCH + i)

            split_turns(0, NE)
            pool.wait_ge(spill_known, 1)
            n_spill = pool.value_load(spill_i[0:1, 0:1], min_val=0, max_val=N_SPILL)
            for t in range(N_SPILL):
                with pool.If(n_spill > t):
                    split_turns(NE + t, 1)

        @block.scalar
        def _(act):
            step = Chain(act, act_step)

            def split_high(u, j):
                s = u.slot(j)
                act.wait_ge(raw_ready[s], u.earlier(j) * 16 + 16)
                if not u.is_first(j):
                    act.wait_ge(used[s], u.earlier(j))
                act.activation(high[:, s, :], raw[:, s, :], ACT.Copy).then_inc(hi_ready[s], 1)

            def split_half(kind, half, g):
                i, cols = 2 * kind + half, slice(half * UNIT // 2, (half + 1) * UNIT // 2)
                act.wait_ge(moe_raw[i], g * 16 + 16)
                if isinstance(g, int) and g == 0:
                    act.wait_ge(used[kind], MIX_SPLITS)
                else:
                    act.wait_ge(moe_used[i], g)
                act.activation(high[:, kind, cols], raw[:, kind, cols], ACT.Copy).then_inc(moe_hi[i], 1)

            def norm_rows(r):
                if r:
                    act.wait_ge(x_mixed, 4 * r)
                for b in range(NB):
                    act.activation(H[:, b, :], X[:, b, :], ACT.Square, accum_out=stat[:, b:b + 1]).then_inc(squared, 1)
                act.wait_ge(mean_sq, r + 1)
                act.activation(stat[:, 4:6], stat[:, 2:4], ACT.Sqrt).then_inc(rms_root, 1)

            def turn_high(t, base, gain):
                for k in range(KT):
                    if k % 2 == 0:
                        act.wait_ge(turned, 4 * t + k // 2 + 1)
                    act.activation(hT_hi[:, k, :], bank[base + k // 2][:, (k % 2) * SEQ:(k % 2 + 1) * SEQ], ACT.Copy,
                                   scale=0.5 if gain is None else gain[:, k:k + 1]).then_inc(turned_hi, 1)

            def s5_angles(l):
                a = [s5p[:, i, :] for i in range(20)]
                act.activation(a[0], par(l, "log_dt"), ACT.Exp).then_inc(s5_exp, 1)
                act.wait_ge(s5_arg, 2 * l + 1)
                act.activation(a[1], a[1], ACT.Exp).then_inc(s5_exp, 1)
                act.wait_ge(s5_arg, 2 * l + 2)
                act.activation(a[4], a[3], ACT.Sin).then_inc(s5_sin, 1)
                act.activation(a[5], a[3], ACT.Sin, scale=0.5).then_inc(s5_sin, 1)

            def s5_operands(l):
                act.wait_ge(s5_turned, 2 * l + 1)
                act.activation(BT[:, :, :, :].rearrange("p a b c -> p (a b c)"), bank[6][:, :],
                               ACT.Copy).then_inc(s5_lhs, 1)
                act.wait_ge(s5_turned, 2 * l + 2)
                act.activation(CTt[:, 0, :], bank[7][:, 0:DB], ACT.Copy).then_inc(s5_lhs, 1)
                act.activation(CTt[:, 1, :], bank[7][:, DB:2 * DB], ACT.Copy, scale=-1.0).then_inc(s5_lhs, 1)

            act.wait_ge(loaded, 64)
            nf = KT * NH
            for l in range(2):
                act.activation(smallw_hi[:, l * nf:(l + 1) * nf], par(l, "w_forget"), ACT.Copy).then_inc(small_hi, 1)
            act.activation(smallw_hi[:, 2 * nf:], RT[:, 0:KT * NE], ACT.Copy).then_inc(small_hi, 1)

            for l in range(2):
                mix = Units(BASE[l])
                after = Units(DENSE0)
                if l == 0:
                    for j in range(RING):
                        split_high(mix, j)
                norm_rows(2 * l)
                if l == 0:
                    s5_angles(0)
                turn_high(3 * l, 0, par(l, "g_mix"))

                act.wait_ge(forget_in, l + 1)
                step(act.activation(lf[:, 1, :], lf[:, 0, :], ACT.Abs))
                step(act.activation(lf[:, 2, :], lf[:, 1, :], ACT.Exp, scale=-1.0))
                act.activation(lf[:, 3, :], lf[:, 2, :], ACT.Ln, bias=1.0).then_inc(forget_ln, 1)

                def halves(b):
                    return b[:, :].rearrange("p (a c) -> p a c", a=2)

                def take(i, dst, func=ACT.Copy, scale=1.0):
                    wait_products(act, mix, i)
                    act.activation(dst, halves(bank[i % 4]), func, scale=scale).then_inc(taken, 1)

                def take_bu(t):
                    act.wait_ge(bu_ready, ST * l + t + 1)
                    act.activation(bu[:, t, :, :], halves(bank[6 + t % 2]), ACT.Copy).then_inc(bu_taken, 1)

                def take_qk(kind, which):
                    if kind or l:
                        act.wait_ge(qk_turned, 2 * (2 * l + kind))
                        act.wait_ge(qk_mean, 2 * (2 * l + kind))
                    take(3 + 3 * kind + which, qk[:, which, :, :])
                    take(3 + 3 * kind + which, sq[:, which, :, :], ACT.Square)

                def root_qk(kind):
                    act.wait_ge(qk_mean, 2 * (2 * l + kind + 1))
                    act.activation(nrm[:, 1, :, :], nrm[:, 0, :, :], ACT.Sqrt).then_inc(qk_root, 1)

                def gain_qk(kind):
                    for which in range(2):
                        act.wait_ge(qk_turned, 2 * (2 * l + kind) + which + 1)
                        b = bank[(6, 7, 5, 4)[2 * kind + which]]
                        g = par(l, ("fox_q", "fox_k", "sb_q", "sb_k")[2 * kind + which])
                        act.activation(qT[:, kind, which, :, :], halves(b), ACT.Copy, scale=g).then_inc(qk_gained, 1)

                def gates(i):
                    n, half = i // 2, i % 2
                    buf = (G2, H)[n % 2]
                    if n >= 2 and half == 0:
                        if n == 2:
                            act.wait_ge(gated, 16 * l + 4)
                        else:
                            act.wait_ge(merged, 12 * l + 4)
                    for b in range(NB):
                        if b == 0:
                            act.wait_ge(gate_ready, 8 * l + i + 1)
                        else:
                            wait_products(act, mix, 10 + 5 * n + 2 * half)
                        act.activation(buf[:, b, half * 512:(half + 1) * 512], bank[2 * half + b][:, :], ACT.Tanh,
                                       scale=0.5).then_inc(gate_tanh, 1)

                def row_exp(h):
                    act.wait_ge(row_max, NH * l + h + 1)
                    if h >= 2:
                        act.wait_ge(p_turned, NH * l + h - 1)
                    act.activation(sc[:, h % 2, 0:P], bank[6 + h % 2][:, 0:P], ACT.Exp, bias=mx[:, 0, h, 0:1],
                                   accum_out=rs[:, 0, h, 0:1]).then_inc(p_exp, 1)
                    act.activation(sc[:, h % 2, P:3 * P], bank[6 + h % 2][:, P:3 * P], ACT.Exp, bias=mx[:, 0, h, 1:2],
                                   accum_out=rs[:, 0, h, 1:2]).then_inc(p_exp, 1)

                def take_p(h):
                    act.wait_ge(p_turned, NH * l + h + 1)
                    if h >= 2:
                        act.wait_ge(fox_out, NH * l + h - 1)
                    act.activation(pT[:, h % 2, :], bank[4][:, 0:3 * P], ACT.Copy).then_inc(p_taken, 1)

                def soft_ln(pair):
                    act.wait_ge(z_ready, NH * l + 2 * pair + 2)
                    for i in range(2):
                        step.mark(act.activation(sc[:, i, :], bank[6 + i][:, 0:3 * P], ACT.Abs))
                    step.settle()
                    step(act.activation(sc[:, :, :], sc[:, :, :], ACT.Exp, scale=-1.0))
                    act.activation(sc[:, :, :], sc[:, :, :], ACT.Ln, bias=1.0).then_inc(z_ln, 1)

                def a_weights(pair):
                    for i in range(2):
                        act.wait_ge(z_cum, NH * l + 2 * pair + i + 1)
                        if pair:
                            act.wait_ge(sb_out, NH * l + 2 * pair)
                        act.activation(pT[:, i, :], bank[6 + i][:, 0:3 * P], ACT.Exp).then_inc(a_exp, 1)

                def ys_split(n, src, ready, count, scale):
                    act.wait_ge(ready, count)
                    if n >= 2:
                        wait_products(act, mix, 13 + 5 * (n - 2))
                    act.activation(ys_hi[:, n % 2, :, :], src, ACT.Copy, scale=scale).then_inc(ys_high, 1)

                for u in range(MIX_UNITS):
                    if u + RING < MIX_UNITS:
                        split_high(mix, u + RING)
                    elif l == 0:
                        split_high(after, u + RING - MIX_UNITS)
                    elif u + RING - MIX_UNITS < 2:
                        for half in range(2):
                            split_half(u + RING - MIX_UNITS, half, 0)
                    if u == 0:
                        if l:
                            act.wait_ge(ys_low, 4 * l)
                        take(0, ca[:, :, :])
                    if u == 1:
                        take(1, cs[:, :, :], ACT.Tanh, 0.5)
                        s5_operands(l)
                    if u == 2:
                        take(2, uT[:, :, :])
                    if u in (3, 4):
                        take_qk(0, u - 3)
                    if u == 5:
                        take(5, V[:, 0, :, :])
                        root_qk(0)
                    if u in (3, 4, 5, 6):
                        take_bu(2 * (u - 3))
                        take_bu(2 * (u - 3) + 1)
                    if u == 7:
                        gain_qk(0)
                        take_qk(1, 0)
                        take_qk(1, 1)
                    if u == 8:
                        take(8, V[:, 1, :, :])
                        root_qk(1)
                        act.wait_ge(conv_cent, l + 1)
                        act.activation(cs[:, :, :], ca[:, :, :], ACT.Square).then_inc(conv_sq, 1)
                    if u == 9:
                        act.wait_ge(conv_vare, l + 1)
                        act.activation(lnv[:, 1, :], lnv[:, 0, :], ACT.Sqrt).then_inc(conv_root, 1)
                        row_exp(0)
                    if u == 10:
                        gates(0)
                        gain_qk(1)
                        row_exp(1)
                        act.wait_ge(conv_lin, l + 1)
                        act.activation(cs[:, :, :], ca[:, :, :], ACT.Tanh, scale=0.5).then_inc(conv_tanh, 1)
                        ys_split(0, ca[:, :, :], conv_out, l + 1, 0.5)
                    if u == 11:
                        row_exp(2)
                        take_p(0)
                    if u == 12:
                        gates(1)
                        row_exp(3)
                        take_p(1)
                    if u == 13:
                        take_p(2)
                    if u == 14:
                        take_p(3)
                        soft_ln(0)
                    if u == 15:
                        gates(2)
                        ys_split(1, halves(bank[5]), fox_out, NH * (l + 1), 1.0)
                    if u == 16:
                        a_weights(0)
                    if u == 17:
                        gates(3)
                        soft_ln(1)
                    if u == 19:
                        a_weights(1)
                    if u == 20:
                        gates(4)
                        ys_split(2, halves(bank[5]), sb_out, NH * (l + 1), 1.0)
                    if u == 22:
                        gates(5)
                    if u == 25:
                        gates(6)
                        act.wait_ge(gelu_in, l + 1)
                        act.activation(cs[:, :, :], halves(tmp[:, 1, :]), ACT.Tanh,
                                       scale=0.7978845608028654).then_inc(gelu_tanh, 1)
                    if u == 26:
                        act.wait_ge(glu_ready, l + 1)
                        act.activation(cs[:, :, :], halves(bank[6]), ACT.Tanh, scale=0.25).then_inc(glu_tanh, 1)
                        ys_split(3, ca[:, :, :], glu_out, l + 1, 0.25)
                    if u == 27:
                        gates(7)
                    if u == MIX_UNITS - 5:
                        turn_high(3 * l + 1, 4, None)
                norm_rows(2 * l + 1)
                turn_high(3 * l + 2, 0, par(l, "g_ffn"))

                if l == 0:
                    s5_angles(1)

                    def hidden(u, j, odd):
                        wait_products(act, u, j)
                        act.activation(silu[:, odd, :, :], halves(bank[2 * odd]), ACT.Silu).then_inc(silu_ready, 1)

                    def hidden_high(c, odd):
                        act.wait_ge(g_ready, c + 1)
                        act.activation(ys_hi[:, odd, :, :], gated_h[:, odd, :, :],
                                       ACT.Copy).then_inc(g_hi, 1)

                    split_high(Units(DENSE0), 3)
                    hidden(Units(DENSE0), 0, 0)
                    split_high(Units(DENSE0), 4)
                    hidden_high(0, 0)

                    def pair(i):
                        u = Units(DENSE0, i * 2)
                        for m in range(2):
                            split_high(u, 5 + 3 * m)
                            hidden(u, 2 + 3 * m, 1 - m)
                            split_high(u, 6 + 3 * m)
                            hidden_high(i * 2 + 1 + m, 1 - m)
                            split_high(u, 7 + 3 * m)

                    with act.Fori(0, PAIRS) as i:
                        pair(i)
                    split_high(Units(BASE[1]), 2)

            act.wait_ge(normed, 4 * NB)
            for b in range(NB):
                act.activation(h_parts[0][:, b, :], H[:, b, :], ACT.Copy).then_inc(h_high, 1)
            act.wait_ge(top_gap, 1)
            act.activation(route[:, 10, :, 0:1], route[:, 9, :, 0:1], ACT.Exp).then_inc(top_exp, 1)

            def gather_high(n, i, p):
                act.wait_ge(gathered, n * 2 + i + 1)
                for k in range(4 * i, 4 * i + 4):
                    ins = act.activation(hT_hi[:, k, p * P:(p + 1) * P], bank[7][:, k % 4 * P:(k % 4 + 1) * P], ACT.Copy,
                                         scale=par(1, "g_ffn", k, k + 1))
                ins.then_inc(gather_hi, 1)

            def take_back(n):
                act.wait_ge(back_turned, n + 1)
                act.activation(back[:, :], bank[7][:, 0:NB * P], ACT.Copy).then_inc(side_done, 1)

            def y_high(n):
                act.wait_ge(moe_used[5], n * NCH + NCH)
                for half in range(2):
                    cols = slice(half * 512, (half + 1) * 512)
                    act.activation(y_parts[0][:, cols], bank[4 + half][:, :], ACT.Copy).then_inc(y_hi, 1)

            def hidden_high(g, odd):
                act.wait_ge(moe_turned, g + 1)
                act.activation(ys_hi[:, odd, 0, :], bank[6][:, 0:CH], ACT.Copy).then_inc(moe_g_hi, 1)

            def turn_of(n, p, carry, more):
                def step(c, odd, last=False):
                    g = n * NCH + c
                    at = c if isinstance(c, int) else None
                    if at != 0 or carry:
                        for half in range(2):
                            split_half(2, half, g - 1)
                    if at == 1 and carry:
                        y_high(n - 1)
                    act.wait_ge(moe_used[1], g + 1)
                    act.activation(silu[:, odd, 0, :], bank[2 * odd][:, 0:CH], ACT.Silu).then_inc(moe_silu, 1)
                    if at != 0 or carry:
                        hidden_high(g - 1, 1 - odd)
                    if not last:
                        for half in range(2):
                            split_half(0, half, g + 1)
                    if at == 0 and carry:
                        take_back(n - 1)
                    if at in (1, 2) and more:
                        gather_high(n + 1, at - 1, 1 - p)
                    if not last:
                        for half in range(2):
                            split_half(1, half, g + 1)

                for c in range(3):
                    step(c, (p + c) % 2)

                def pair(i, last=False):
                    step(i * 2 + 3, 1 - p)
                    step(i * 2 + 4, p, last)

                with act.Fori(0, 4 if more else 3) as i:
                    pair(i)
                if not more:
                    pair(3, True)

            def finish(n, p):
                g = n * NCH + NCH - 1
                for half in range(2):
                    split_half(2, half, g)
                hidden_high(g, p)
                y_high(n)
                take_back(n)

            for i in range(2):
                gather_high(0, i, 0)
            turn_of(0, 0, False, True)
            with act.Fori(0, NE // 2 - 1) as i:
                turn_of(i * 2 + 1, 1, True, True)
                turn_of(i * 2 + 2, 0, True, True)
            turn_of(NE - 1, 1, True, False)
            finish(NE - 1, 1)
            act.wait_ge(spill_known, 1)
            n_spill = act.value_load(spill_i[0:1, 0:1], min_val=0, max_val=N_SPILL)
            for t in range(N_SPILL):
                with act.If(n_spill > t):
                    n, p = NE + t, t % 2
                    for kind in range(2):
                        for half in range(2):
                            split_half(kind, half, n * NCH)
                    for i in range(2):
                        gather_high(n, i, p)
                    turn_of(n, p, False, False)
                    finish(n, p)

        @block.vector
        def _(dve):
            step = Chain(dve, dve_step)
            tt, ts, stt = dve.tensor_tensor, dve.tensor_scalar, dve.scalar_tensor_tensor

            def norm_rows(r):
                dve.wait_ge(squared, 2 * r + 2)
                ts(stat[:, 2:4], stat[:, 0:2], 1.0 / D, EPS, ALU.mult, ALU.add).then_inc(mean_sq, 1)
                dve.wait_ge(rms_root, r + 1)
                step(dve.reciprocal(stat[:, 6:8], stat[:, 4:6]))
                for b in range(NB):
                    ts(H[:, b, :], X[:, b, :], stat[:, 6 + b:7 + b], None, ALU.mult).then_inc(normed, 1)

            def turn_low(t, base, gain):
                for k in range(KT):
                    dve.wait_ge(turned_hi, KT * t + k // 2 * 2 + 2)
                    stt(hT_lo[:, k, :], bank[base + k // 2][:, (k % 2) * SEQ:(k % 2 + 1) * SEQ],
                        0.5 if gain is None else gain[:, k:k + 1], hT_hi[:, k, :].bitcast(F32), ALU.mult,
                        ALU.subtract).then_inc(turned_lo, 1)

            s5a = [s5p[:, i, :] for i in range(20)]
            dt, mag, turn, arg, sin, hsin, t6, _, cos, are, aim, nre, den, kre, kim, t14, t15, t16, pc, ps = s5a

            def s5_angles(l):
                lre, lim = par(l, "lam_re"), par(l, "lam_im")
                dve.wait_ge(s5_exp, 2 * l + 1)
                tt(mag, lre, dt, ALU.mult).then_inc(s5_arg, 1)
                step(tt(turn, lim, dt, ALU.mult))
                step(ts(t6, turn, 1.0 / (2 * np.pi), ROUND, ALU.mult, ALU.add))
                step(ts(t6, t6, ROUND, None, ALU.subtract))
                step(stt(arg, t6, -TWO_PI_1, turn, ALU.mult, ALU.add))
                step(stt(arg, t6, -TWO_PI_2, arg, ALU.mult, ALU.add))
                step(stt(arg, t6, -TWO_PI_3, arg, ALU.mult, ALU.add))
                ts(arg, arg, PI_F32, -PI_F32, ALU.min, ALU.max).then_inc(s5_arg, 1)

            def s5_spread_of(l):
                lre, lim = par(l, "lam_re"), par(l, "lam_im")
                dve.wait_ge(s5_sin, 2 * l + 2)
                step(tt(cos, hsin, hsin, ALU.mult))
                step(ts(cos, cos, -2.0, 1.0, ALU.mult, ALU.add))
                step.mark(tt(are, mag, cos, ALU.mult))
                step.mark(tt(aim, mag, sin, ALU.mult))
                step.mark(tt(den, lre, lre, ALU.mult))
                step(tt(t14, lim, lim, ALU.mult))
                step.mark(ts(nre, are, 1.0, None, ALU.subtract))
                step(tt(den, den, t14, ALU.add))
                step.mark(dve.reciprocal(den, den))
                step.mark(tt(t14, nre, lre, ALU.mult))
                step.mark(tt(t15, aim, lim, ALU.mult))
                step.mark(tt(t16, aim, lre, ALU.mult))
                step(tt(kim, nre, lim, ALU.mult))
                step.mark(tt(t14, t14, t15, ALU.add))
                step(tt(t16, t16, kim, ALU.subtract))
                step.mark(tt(kre, t14, den, ALU.mult))
                step(tt(kim, t16, den, ALU.mult))
                b3 = [tmp[:, i, 0:ST * GH].rearrange("p (t h) -> p t h", h=GH) for i in range(4)]
                bre, bim = (par(l, n).rearrange("p (t h) -> p t h", h=GH) for n in ("b_re", "b_im"))
                kre3, kim3 = (k.unsqueeze(2).to_broadcast([P, ST, GH]) for k in (kre, kim))
                step.mark(tt(b3[0], bre, kre3, ALU.mult))
                step.mark(tt(b3[1], bim, kim3, ALU.mult))
                step.mark(tt(b3[2], bim, kre3, ALU.mult))
                step(tt(b3[3], bre, kim3, ALU.mult))
                step.mark(tt(b3[0], b3[0], b3[1], ALU.subtract))
                step(tt(b3[2], b3[2], b3[3], ALU.add))
                for ri in range(2):
                    for side in range(2):
                        step.mark(ts(s5b[:, ri, :, side, :], b3[2 * ri], const("side", side, side + 1), None, ALU.mult))
                    for side in range(2):
                        c3 = par(l, ("c_re", "c_im")[ri]).rearrange("p (a c) -> p a c", a=CT)
                        ins = ts(s5c[:, ri, :, side, :], c3, const("parity", side, side + 1), None, ALU.mult)
                        if ri == 0 or side == 0:
                            step.mark(ins)
                ins.then_inc(s5_spread, 1)
                step.settle()

            def s5_table(l, n, end):
                step.settle()
                if n == 1:
                    step.mark(dve.memset(rot_c[:, :, 0:1], 1.0))
                    step.mark(dve.memset(rot_s[:, :, 0:1], 0.0))
                    step.mark(dve.tensor_copy(pc, cos))
                    step(dve.tensor_copy(ps, sin))
                ta = tmp[:, 0:2, :].rearrange("p a c -> p (a c)")
                tb = tmp[:, 2:4, :].rearrange("p a c -> p (a c)")
                while n < end:
                    c0, s0, c1, s1 = rot_c[:, :, 0:n], rot_s[:, :, 0:n], rot_c[:, :, n:2 * n], rot_s[:, :, n:2 * n]
                    pcb, psb = (v.unsqueeze(2).to_broadcast([P, ST, n]) for v in (pc, ps))
                    t0, t1 = (t[:, 0:ST * n].rearrange("p (t n) -> p t n", t=ST) for t in (ta, tb))
                    step.mark(tt(t0, s0, psb, ALU.mult))
                    step.mark(tt(t1, c0, psb, ALU.mult))
                    step.mark(tt(c1, c0, pcb, ALU.mult))
                    step(tt(s1, s0, pcb, ALU.mult))
                    step.mark(tt(c1, c1, t0, ALU.subtract))
                    step.mark(tt(s1, s1, t1, ALU.add))
                    step.mark(tt(t14, pc, pc, ALU.mult))
                    step.mark(tt(t15, ps, ps, ALU.mult))
                    step(tt(t16, pc, ps, ALU.mult))
                    step.mark(tt(pc, t14, t15, ALU.subtract))
                    step(ts(ps, t16, 2.0, None, ALU.mult))
                    n *= 2

            def s5_scan(l, pair):
                t0 = 2 * pair
                dve.wait_ge(bu_taken, ST * l + t0 + 2)
                step.settle()
                if l or pair:
                    dve.wait_ge(s5_state, ST // 2 * l + pair)
                re, im = bu[:, t0:t0 + 2, 0, :], bu[:, t0:t0 + 2, 1, :]
                c, s = rot_c[:, t0:t0 + 2, :], rot_s[:, t0:t0 + 2, :]
                q = [tmp[:, i, :].rearrange("p (a c) -> p a c", a=2) for i in range(4)]
                step.mark(tt(q[0], c, re, ALU.mult))
                step.mark(tt(q[1], s, im, ALU.mult))
                step.mark(tt(q[2], c, im, ALU.mult))
                step(tt(q[3], s, re, ALU.mult))
                step.mark(tt(q[0], q[0], q[1], ALU.add))
                step(tt(q[2], q[2], q[3], ALU.subtract))
                for a in range(2):
                    mag = s5p[:, 1, t0 + a:t0 + a + 1].to_broadcast([P, SEQ])
                    for ri in range(2):
                        ins = dve.tensor_tensor_scan(bu[:, t0 + a, ri, :], mag, q[2 * ri][:, a, :], 0.0, ALU.mult, ALU.add)
                        step.mark(ins)
                step.settle()
                step.mark(tt(q[0], c, re, ALU.mult))
                step.mark(tt(q[1], s, im, ALU.mult))
                step.mark(tt(q[2], c, im, ALU.mult))
                step(tt(q[3], s, re, ALU.mult))
                step.mark(tt(re, q[0], q[1], ALU.subtract))
                tt(im, q[2], q[3], ALU.add).then_inc(s5_state, 1)

            def halves(b):
                return b[:, :].rearrange("p (a c) -> p a c", a=2)

            dve.wait_ge(loaded, 64)
            nf = KT * NH
            for l in range(2):
                dve.wait_ge(small_hi, l + 1)
                tt(smallw_lo[:, l * nf:(l + 1) * nf], par(l, "w_forget"), smallw_hi[:, l * nf:(l + 1) * nf].bitcast(F32),
                   ALU.subtract).then_inc(small_lo, 1)
            dve.wait_ge(small_hi, 3)
            tt(smallw_lo[:, 2 * nf:], RT[:, 0:KT * NE], smallw_hi[:, 2 * nf:].bitcast(F32), ALU.subtract).then_inc(small_lo, 1)

            for l in range(2):
                mix = Units(BASE[l])
                norm_rows(2 * l)
                if l == 0:
                    s5_angles(0)
                turn_low(3 * l, 0, par(l, "g_mix"))
                if l == 0:
                    s5_spread_of(0)

                dve.wait_ge(forget_ready, l + 1)
                f3 = lf[:, 0, :].rearrange("p (b h) -> p b h", b=NB)
                tt(f3, bank[4][:, 0:NB * NH].rearrange("p (b h) -> p b h", b=NB),
                   par(l, "b_forget").unsqueeze(1).to_broadcast([P, NB, NH]), ALU.add).then_inc(forget_in, 1)
                dve.wait_ge(forget_ln, l + 1)
                dve.wait_ge(forget_in, l + 1)
                step(stt(lf[:, 1, :], lf[:, 0, :], 0.0, lf[:, 3, :], ALU.min, ALU.subtract))
                for h in range(NH):
                    for i, (tab, b) in enumerate((("tri", 0), ("ones", 0), ("tri", 1))):
                        ins = ts(TL[:, h, i, :], const(tab), lf[:, 1, b * NH + h:b * NH + h + 1], None, ALU.mult)
                ins.then_inc(forget_tri, 1)

                dve.wait_ge(taken, 13 * l + 2)
                step.mark(dve.memset(upad[:, :, 0:PAD], 0.0))
                step(stt(upad[:, :, PAD:], cs[:, :, :], 1.0, ca[:, :, :], ALU.add, ALU.mult))
                for tap in range(CONVW):
                    for c in range(CT):
                        w = par(l, "conv_w", c * CONVW + tap, c * CONVW + tap + 1)
                        src = upad[:, c, tap:tap + SEQ]
                        if tap == 0:
                            step.mark(ts(ca[:, c, :], src, w, None, ALU.mult))
                        else:
                            step.mark(stt(ca[:, c, :], src, w, ca[:, c, :], ALU.mult, ALU.add))
                    step.settle()
                for c in range(CT):
                    ts(ca[:, c, :], ca[:, c, :], 0.5, par(l, "conv_b", c, c + 1), ALU.mult, ALU.add).then_inc(conv_sum, 1)

                def norm_qk(kind):
                    for which in range(2):
                        i = 3 + 3 * kind + which
                        dve.wait_ge(taken, 13 * l + (5, 7, 10, 12)[2 * kind + which])
                        step(dve.tensor_reduce(nrm[:, 0, which, :],
                                               sq[:, which, :, :].rearrange("p b (h d) -> p (b h) d", d=HD), AX_X, ALU.add))
                        f = 1.0 if which == 0 else 1.0 / HD
                        ts(nrm[:, 0, which, :], nrm[:, 0, which, :], f, f * HD * EPS, ALU.mult, ALU.add).then_inc(qk_mean, 1)
                    dve.wait_ge(qk_root, 2 * l + kind + 1)
                    dve.wait_ge(qk_mean, 2 * (2 * l + kind + 1))
                    step(dve.reciprocal(nrm[:, 0, :, :], nrm[:, 1, :, :]))
                    for which in range(2):
                        v = qk[:, which, :, :].rearrange("p b (h d) -> p (b h) d", d=HD)
                        tt(v, v, nrm[:, 0, which, :].unsqueeze(2).to_broadcast([P, NB * NH, HD]),
                           ALU.mult).then_inc(qk_normed, 1)

                def ys_split(n, src, scale):
                    dve.wait_ge(ys_high, 4 * l + n + 1)
                    stt(ys_lo[:, n % 2, :, :], src, scale, ys_hi[:, n % 2, :, :].bitcast(F32), ALU.mult,
                        ALU.subtract).then_inc(ys_low, 1)

                def row_max_of(h):
                    dve.wait_ge(score, NH * l + h + 1)
                    b = bank[6 + h % 2]
                    step.mark(dve.tensor_reduce(mx[:, 0, h, 0:1], b[:, 0:P], AX_X, ALU.max, negate=True))
                    dve.tensor_reduce(mx[:, 0, h, 1:2], b[:, P:3 * P], AX_X, ALU.max, negate=True).then_inc(row_max, 1)

                def row_norm(h):
                    dve.wait_ge(p_exp, 2 * (NH * l + h + 1))
                    step(dve.reciprocal(rs[:, 1, h, :], rs[:, 0, h, :]))
                    step.mark(ts(sc[:, h % 2, 0:P], sc[:, h % 2, 0:P], rs[:, 1, h, 0:1], None, ALU.mult))
                    ts(sc[:, h % 2, P:3 * P], sc[:, h % 2, P:3 * P], rs[:, 1, h, 1:2], None, ALU.mult).then_inc(p_norm, 1)

                def soft(pair):
                    dve.wait_ge(z_ln, 2 * l + pair + 1)
                    for i in range(2):
                        step(stt(sc[:, i, :], bank[6 + i][:, 0:3 * P], 0.0, sc[:, i, :], ALU.max, ALU.add))
                        tt(sc[:, i, :], sc[:, i, :], const("keep"), ALU.mult).then_inc(z_soft, 1)

                def apply_gates(n, half):
                    buf = (G2, H)[n % 2]
                    for b in range(NB):
                        cols = slice(half * 512, (half + 1) * 512)
                        if half and b:
                            wait_products(dve, mix, 13 + 5 * n)
                        else:
                            dve.wait_ge(branch, 12 * l + 3 * n + 2 * half + b + 1)
                        dve.wait_ge(gate_tanh, 16 * l + 4 * n + 2 * half + b + 1)
                        if n == 0:
                            stt(M[:, b, cols], buf[:, b, cols], 1.0, bank[2 * half + b][:, :], ALU.add,
                                ALU.mult).then_inc(gated, 1)
                        else:
                            stt(buf[:, b, cols], buf[:, b, cols], 1.0, bank[2 * half + b][:, :], ALU.add,
                                ALU.mult).then_inc(gated, 1)
                            dve.wait_ge(gated, 16 * l + 4 * n + 2 * half + b + 1)
                            if n >= 2:
                                dve.wait_ge(merged, 12 * l + 4 * (n - 2) + 2 * half + b + 1)
                            tt(M[:, b, cols], M[:, b, cols], buf[:, b, cols], ALU.add).then_inc(merged, 1)

                norm_qk(0)
                if l == 0:
                    s5_table(0, 1, SEQ)
                s5_scan(l, 0)
                dve.wait_ge(conv_mean, l + 1)
                dve.wait_ge(conv_sum, 2 * l + 2)
                tt(ca[:, :, :], ca[:, :, :], bank[4][:, 0:SEQ].unsqueeze(1).to_broadcast([P, CT, SEQ]),
                   ALU.subtract).then_inc(conv_cent, 1)
                norm_qk(1)
                dve.wait_ge(conv_var, l + 1)
                ts(lnv[:, 0, :], bank[4][:, SEQ:2 * SEQ], EPS, None, ALU.add).then_inc(conv_vare, 1)
                row_max_of(0)
                dve.wait_ge(conv_root, l + 1)
                step(dve.reciprocal(lnv[:, 2, :], lnv[:, 1, :]))
                dve.wait_ge(conv_cent, l + 1)
                step(tt(ca[:, :, :], ca[:, :, :], lnv[:, 2, :].unsqueeze(1).to_broadcast([P, CT, SEQ]), ALU.mult))
                for c in range(CT):
                    ins = ts(ca[:, c, :], ca[:, c, :], par(l, "ln_g", c, c + 1), par(l, "ln_b", c, c + 1), ALU.mult, ALU.add)
                    if c < CT - 1:
                        step.mark(ins)
                ins.then_inc(conv_lin, 1)
                row_norm(0)
                row_max_of(1)
                dve.wait_ge(conv_tanh, l + 1)
                stt(ca[:, :, :], cs[:, :, :], 1.0, ca[:, :, :], ALU.add, ALU.mult).then_inc(conv_out, 1)
                ys_split(0, ca[:, :, :], 0.5)
                row_norm(1)
                row_max_of(2)
                row_norm(2)
                row_max_of(3)
                row_norm(3)
                apply_gates(0, 0)
                apply_gates(0, 1)
                soft(0)
                ys_split(1, halves(bank[5]), 1.0)
                s5_scan(l, 1)
                soft(1)
                apply_gates(1, 0)
                apply_gates(1, 1)
                s5_scan(l, 2)
                ys_split(2, halves(bank[5]), 1.0)
                s5_scan(l, 3)
                apply_gates(2, 0)
                apply_gates(2, 1)
                dve.wait_ge(s5_y, l + 1)
                y3, g3, q3 = (halves(tmp[:, i, :]) for i in (0, 1, 2))
                dve.wait_ge(s5_state, ST // 2 * (l + 1))
                for c in range(CT):
                    step.mark(stt(y3[:, c, :], uT[:, c, :], par(l, "s5_d", c, c + 1), halves(bank[4])[:, c, :],
                                  ALU.mult, ALU.add))
                step.settle()
                step(tt(q3, y3, y3, ALU.mult))
                step(ts(q3, q3, 0.044715, 1.0, ALU.mult, ALU.add))
                tt(g3, q3, y3, ALU.mult).then_inc(gelu_in, 1)
                dve.wait_ge(gelu_tanh, l + 1)
                stt(q3, cs[:, :, :], 1.0, y3, ALU.add, ALU.mult).then_inc(gelu_out, 1)
                dve.wait_ge(glu_tanh, l + 1)
                dve.wait_ge(gelu_out, l + 1)
                stt(ca[:, :, :], cs[:, :, :], 1.0, q3, ALU.add, ALU.mult).then_inc(glu_out, 1)
                ys_split(3, ca[:, :, :], 0.25)
                apply_gates(3, 0)
                apply_gates(3, 1)
                turn_low(3 * l + 1, 4, None)

                def add_to_x(u, base):
                    wait_products(dve, u, MIX_UNITS - 1)
                    for half in range(2):
                        for b in range(NB):
                            xs = X[:, b, half * 512:(half + 1) * 512]
                            tt(xs, xs, bank[base + 2 * half + b][:, :], ALU.add).then_inc(x_mixed, 1)

                add_to_x(mix, 0)
                dve.wait_ge(x_mixed, 4 * (2 * l + 1))
                norm_rows(2 * l + 1)
                turn_low(3 * l + 2, 0, par(l, "g_ffn"))
                if l == 0:
                    def hidden(u, j, c, odd):
                        wait_products(dve, u, j)
                        dve.wait_ge(silu_ready, c + 1)
                        tt(gated_h[:, odd, :, :], silu[:, odd, :, :], halves(bank[2 * odd + 1]), ALU.mult).then_inc(g_ready, 1)
                        dve.wait_ge(g_hi, c + 1)
                        tt(ys_lo[:, odd, :, :], gated_h[:, odd, :, :], ys_hi[:, odd, :, :].bitcast(F32),
                           ALU.subtract).then_inc(g_lo, 1)

                    s5_angles(1)
                    hidden(Units(DENSE0), 1, 0, 0)
                    s5_spread_of(1)
                    s5_table(1, 1, 32)
                    hidden(Units(DENSE0), 3, 1, 1)
                    s5_table(1, 32, 128)
                    hidden(Units(DENSE0), 6, 2, 0)
                    s5_table(1, 128, SEQ)
                    with dve.Fori(1, PAIRS) as i:
                        for m in range(2):
                            hidden(Units(DENSE0, i * 2), 3 + 3 * m, i * 2 + 1 + m, 1 - m)
                    add_to_x(Units(DENSE0), 4)
                    dve.wait_ge(x_mixed, 8)

            r = [route[:, i, :, :] for i in range(12)]
            lg, top, at, one, two, sel, comb, place, w1, gap, e, spare = r
            dve.wait_ge(logits, 1)
            step(tt(lg, bank[4][:, 0:NB * NE].rearrange("p (b e) -> p b e", b=NB),
                    RT[:, KT * NE:].unsqueeze(1).to_broadcast([P, NB, NE]), ALU.add))
            for b in range(NB):
                step.mark(dve.max(top[:, b, :], lg[:, b, :]))
            step.settle()
            for b in range(NB):
                step.mark(dve.max_index(top_at[:, b, :], top[:, b, :], lg[:, b, :]))
            ts_ = tt(gap[:, :, 0:1], top[:, :, 1:2], top[:, :, 0:1], ALU.subtract)
            ts_.then_inc(top_gap, 1)
            step.settle()
            step(dve.tensor_copy(at, top_at[:, :, :]))
            for b in range(NB):
                step.mark(ts(one[:, b, :], const("iota8"), at[:, b, 0:1], None, ALU.is_equal))
                step.mark(ts(two[:, b, :], const("iota8"), at[:, b, 1:2], None, ALU.is_equal))
            step.settle()
            tt(sel, one, two, ALU.add).then_inc(chosen, 1)
            dve.wait_ge(top_exp, 1)
            step(ts(w1[:, :, 0:1], e[:, :, 0:1], 1.0, None, ALU.add))
            step(dve.reciprocal(w1[:, :, 0:1], w1[:, :, 0:1]))
            step(tt(w1[:, :, 1:2], w1[:, :, 0:1], e[:, :, 0:1], ALU.mult))
            for b in range(NB):
                step(ts(comb[:, b, :], one[:, b, :], w1[:, b, 0:1], None, ALU.mult))
                step(stt(comb[:, b, :], two[:, b, :], w1[:, b, 1:2], comb[:, b, :], ALU.mult, ALU.add))
            dve.wait_ge(places, 1)
            dve.wait_ge(chosen, 1)
            pb3 = bank[5][:, 0:NB * NE].rearrange("p (b e) -> p b e", b=NB)
            step(stt(place, pb3, 1.0, sel, ALU.add, ALU.mult))
            step(ts(place, place, 1.0, None, ALU.subtract))
            step(ts(spare, place, float(P), None, ALU.subtract))
            s = [spill[0:1, i, :] for i in range(4)]
            step(ts(s[0], bank[5][0:1, NB * NE:(NB + 1) * NE], float(P), None, ALU.is_gt))
            step(dve.tensor_tensor_scan(s[1], const("ones", 0, NE, rows=1), s[0], 0.0, ALU.mult, ALU.add))
            step(dve.tensor_copy(spill_i[0:1, 0:1], s[1][:, NE - 1:NE]))
            for t in range(N_SPILL):
                step(stt(s[2], s[1], float(t + 1), s[0], ALU.is_equal, ALU.mult))
                step(tt(s[2], s[2], const("iota8", rows=1), ALU.mult))
                step(dve.tensor_reduce(s[3][:, t:t + 1], s[2], AX_X, ALU.add))
            dve.tensor_copy(spill_i[0:1, 1:1 + N_SPILL], s[3][:, 0:N_SPILL]).then_inc(spill_known, 1)

            def split_half(kind, half, g):
                i, cols = 2 * kind + half, slice(half * UNIT // 2, (half + 1) * UNIT // 2)
                dve.wait_ge(moe_hi[i], g + 1)
                tt(low[:, kind, cols], raw[:, kind, cols], high[:, kind, cols].bitcast(F32),
                   ALU.subtract).then_inc(moe_lo[i], 1)

            def one_hot(dst, e, where, event):
                for b in range(NB):
                    ins = ts(dst[:, b, :], const("iota"), route[:, where, b, bass.ds(e, 1)], None, ALU.is_equal)
                ins.then_inc(event, 1)

            def gather_low(n, i, p):
                dve.wait_ge(gather_hi, n * 2 + i + 1)
                for k in range(4 * i, 4 * i + 4):
                    ins = stt(hT_lo[:, k, p * P:(p + 1) * P], bank[7][:, k % 4 * P:(k % 4 + 1) * P],
                              par(1, "g_ffn", k, k + 1), hT_hi[:, k, p * P:(p + 1) * P].bitcast(F32), ALU.mult,
                              ALU.subtract)
                ins.then_inc(side_done, 1)

            def y_low(n):
                for half in range(2):
                    cols = slice(half * 512, (half + 1) * 512)
                    dve.wait_ge(y_hi, n * 2 + half + 1)
                    tt(y_parts[1][:, cols], bank[4 + half][:, :], y_parts[0][:, cols].bitcast(F32),
                       ALU.subtract).then_inc(y_lo, 1)

            def add_back(n, i, e):
                dve.wait_ge(spread, n * 4 + i + 1)
                for b in range(NB):
                    xs = X[:, b, bass.ds(i * DB, DB)]
                    ins = stt(xs, bank[7][:, b * DB:(b + 1) * DB], route[:, 6, b, bass.ds(e, 1)], xs, ALU.mult, ALU.add)
                ins.then_inc(side_done, 1)

            def hidden_low(g, odd):
                dve.wait_ge(moe_g_hi, g + 1)
                tt(ys_lo[:, odd, 0, :], bank[6][:, 0:CH], ys_hi[:, odd, 0, :].bitcast(F32),
                   ALU.subtract).then_inc(moe_g_lo, 1)

            def turn_of(n, p, carry, more):
                def step(c, odd, job=None, last=False):
                    g = n * NCH + c
                    at = c if isinstance(c, int) else None
                    if at == 0 and more:
                        one_hot(picks, n + 1, 7, picked)
                    if at == 0 and carry:
                        one_hot(picks_back, n - 1, 7, picked_back)
                    if at == 1 and carry:
                        y_low(n - 1)
                    if at != 0 or carry:
                        hidden_low(g - 1, 1 - odd)
                    if not last:
                        for half in range(2):
                            split_half(0, half, g + 1)
                    dve.wait_ge(moe_used[3], g + 1)
                    dve.wait_ge(moe_silu, g + 1)
                    tt(gated_h[:, odd, 0, :], silu[:, odd, 0, :], bank[2 * odd + 1][:, 0:CH],
                       ALU.mult).then_inc(moe_gated, 1)
                    if job:
                        job()
                    if at in (1, 2) and more:
                        gather_low(n + 1, at - 1, 1 - p)
                    if not last:
                        for half in range(2):
                            split_half(1, half, g + 1)

                for c in range(3):
                    step(c, (p + c) % 2)

                def pair(i, last=False):
                    step(i * 2 + 3, 1 - p, (lambda: add_back(n - 1, i, n - 1)) if carry else None)
                    step(i * 2 + 4, p, None, last)

                with dve.Fori(0, 4 if more else 3) as i:
                    pair(i)
                if not more:
                    pair(3, True)

            def finish(n, p, e, where):
                g = n * NCH + NCH - 1
                one_hot(picks_back, e, where, picked_back)
                hidden_low(g, p)
                y_low(n)
                for i in range(4):
                    add_back(n, i, e)

            step.settle()
            dve.wait_ge(spill_known, 1)
            one_hot(picks, 0, 7, picked)
            for b in range(NB):
                dve.wait_ge(h_high, b + 1)
                tt(h_parts[1][:, b, :], H[:, b, :], h_parts[0][:, b, :].bitcast(F32), ALU.subtract).then_inc(h_low, 1)
            for i in range(2):
                gather_low(0, i, 0)
            turn_of(0, 0, False, True)
            with dve.Fori(0, NE // 2 - 1) as i:
                turn_of(i * 2 + 1, 1, True, True)
                turn_of(i * 2 + 2, 0, True, True)
            turn_of(NE - 1, 1, True, False)
            finish(NE - 1, 1, NE - 1, 7)
            n_spill = dve.value_load(spill_i[0:1, 0:1], min_val=0, max_val=N_SPILL)
            for t in range(N_SPILL):
                with dve.If(n_spill > t):
                    n, p = NE + t, t % 2
                    e = dve.value_load(spill_i[0:1, 1 + t:2 + t], min_val=0, max_val=NE - 1)
                    one_hot(picks, e, 11, picked)
                    for i in range(2):
                        gather_low(n, i, p)
                    turn_of(n, p, False, False)
                    finish(n, p, e, 11)
            dve.memset(stat[:, 0:1], 0.0).then_inc(finished, 1)

        @block.tensor
        def _(pe):
            def product(dst, w, m, start, stop):
                pe.matmul(dst, w[0], m[0], start=start, stop=False, skip_group_check=True)
                pe.matmul(dst, w[1], m[0], start=False, stop=False, skip_group_check=True)
                return pe.matmul(dst, w[0], m[1], start=False, stop=stop, skip_group_check=True)

            def parts(s, nk):
                return unit_view(high, s, nk), unit_view(low, s, nk)

            def cut(pair_, *ix):
                return tuple(t[ix] for t in pair_)

            def arrive(u, j):
                s = u.slot(j)
                pe.wait_ge(lo_ready[s], u.earlier(j) + 1)
                return s

            hT = (hT_hi, hT_lo)
            everything = slice(None)

            def turn(t, src, base):
                for i in range(KT // 2):
                    for kk in range(2):
                        for b in range(NB):
                            k = 2 * i + kk
                            ins = pe.transpose(bank[base + i][:, kk * SEQ + b * P:kk * SEQ + (b + 1) * P],
                                               src[:, b, k * P:(k + 1) * P], ident)
                    ins.then_inc(turned, 1)

            def channel_rows(u, j, dst):
                s = arrive(u, j)
                w = parts(s, KT)
                for c in range(2):
                    for k in range(KT):
                        ins = product(dst[:, c * SEQ:(c + 1) * SEQ], cut(w, everything, k, slice(c * P, (c + 1) * P)),
                                      cut(hT, everything, k, everything), k == 0, k == KT - 1)
                return ins, s

            def token_rows(u, j, dst):
                s = arrive(u, j)
                w = parts(s, KT)
                for b in range(NB):
                    for k in range(KT):
                        ins = product(dst[:, b * DB:(b + 1) * DB], cut(hT, everything, k, slice(b * P, (b + 1) * P)),
                                      cut(w, everything, k, everything), k == 0, k == KT - 1)
                return ins, s

            def wide_rows(u, j, nk, k0, last_k, lhs, dst, events=None, free=None):
                s = arrive(u, j)
                n = UNIT // nk // 512
                w = parts(s, nk)
                for half in range(n):
                    for b in range(NB):
                        if free:
                            free(half, b)
                        for k in range(nk):
                            ins = product(dst(half, b), cut(lhs, everything, k0 + k, slice(b * P, (b + 1) * P)),
                                          cut(w, everything, k, slice(half * 512, (half + 1) * 512)),
                                          k0 + k == 0, k0 + k == last_k)
                        last = half == n - 1 and b == NB - 1
                        if events and not last:
                            ins.then_inc(events, 1)
                return ins, s


            pe.wait_ge(loaded, 64)
            for l in range(2):
                U = Units(BASE[l])
                pe.wait_ge(normed, NB * (2 * l + 1))
                turn(3 * l, H, 0)
                pe.wait_ge(small_lo, l + 1)
                for b in range(NB):
                    for k in range(KT):
                        if b == 0:
                            pe.wait_ge(turned_lo, KT * 3 * l + k + 1)
                        cols = slice(l * KT * NH + k * NH, l * KT * NH + (k + 1) * NH)
                        ins = product(bank[4][:, b * NH:(b + 1) * NH], cut(hT, everything, k, slice(b * P, (b + 1) * P)),
                                      cut((smallw_hi, smallw_lo), everything, cols), k == 0, k == KT - 1)
                ins.then_inc(forget_ready, 1)

                def project(u):
                    if u >= 4:
                        pe.wait_ge(taken, 13 * l + (1, 2, 3, 5, 7)[u - 4])
                    ins, s = (channel_rows if u < 3 else token_rows)(U, u, bank[u % 4])
                    ins.then_inc(used[s], 1)

                def s5_operands():
                    pe.wait_ge(s5_spread, l + 1)
                    for ri in range(2):
                        for th in range(CT):
                            ins = pe.transpose(bank[6][:, (2 * ri + th) * P:(2 * ri + th + 1) * P],
                                               s5b[:, ri, 4 * th:4 * th + 4, :, :].rearrange("p t s h -> p (t s h)"), ident)
                    ins.then_inc(s5_turned, 1)
                    for ri in range(2):
                        for th in range(CT):
                            ins = pe.transpose(bank[7][:, (2 * ri + th) * P:(2 * ri + th + 1) * P],
                                               s5c[:, ri, th, :, :].rearrange("p s n -> p (s n)"), ident)
                    ins.then_inc(s5_turned, 1)

                def bu_of(t):
                    n, jj, th = ST * l + t, t % 4, t // 4
                    if t == 0:
                        pe.wait_ge(taken, 13 * l + 3)
                        pe.wait_ge(s5_lhs, 3 * (l + 1))
                    if t >= 2:
                        pe.wait_ge(bu_taken, n - 1)
                    rows = slice(32 * jj, 32 * jj + 32)
                    for ri in range(2):
                        ins = pe.matmul(bank[6 + t % 2][:, ri * SEQ:(ri + 1) * SEQ], BT[rows, ri, th, :], uT[rows, th, :],
                                        start=True, stop=True)
                    ins.then_inc(bu_ready, 1)

                def turn_qk(kind, which):
                    pe.wait_ge(qk_normed, 2 * (2 * l + kind) + which + 1)
                    i = 2 * kind + which
                    if i == 0:
                        pe.wait_ge(bu_taken, ST * (l + 1))
                    if i == 3:
                        pe.wait_ge(conv_vare, l + 1)
                    b5 = bank[(6, 7, 5, 4)[i]]
                    for hp in range(CT):
                        for b in range(NB):
                            ins = pe.transpose(b5[:, hp * SEQ + b * P:hp * SEQ + (b + 1) * P],
                                               qk[:, which, b, hp * P:(hp + 1) * P], ident)
                    ins.then_inc(qk_turned, 1)

                def qk_of(kind, h):
                    r0 = HD * (h % 2)
                    q, k = (qT[r0:r0 + HD, kind, which, h // 2, :] for which in range(2))
                    return q, k

                def fox_scores(h):
                    if h == 0:
                        pe.wait_ge(forget_tri, l + 1)
                        pe.wait_ge(qk_gained, 4 * l + 2)
                    if h >= 2:
                        pe.wait_ge(p_exp, 2 * (NH * l + h - 1))
                    q, k = qk_of(0, h)
                    b = bank[6 + h % 2]
                    mm = lambda o, a, c, st, sp_: pe.matmul(o, a, c, start=st, stop=sp_, skip_group_check=True)
                    mm(b[:, 0:P], q[:, 0:P], k[:, 0:P], True, False)
                    mm(b[:, 0:P], TL[:, h, 0, :], const("later"), False, False)
                    mm(b[:, 0:P], ident, const("causal"), False, True)
                    mm(b[:, P:3 * P], q[:, P:2 * P], k, True, False)
                    mm(b[:, P:2 * P], TL[:, h, 1, :], const("later"), False, False)
                    both = C[:, CONST["ones"][0]:CONST["later"][1]]
                    mm(b[:, P:3 * P], TL[:, h, 2, :], both, False, False)
                    mm(b[:, 2 * P:3 * P], ident, const("causal"), False, True).then_inc(score, 1)

                def turn_p(h):
                    pe.wait_ge(p_norm, NH * l + h + 1)
                    if h == 0:
                        pe.wait_ge(qk_gained, 4 * l + 4)
                    else:
                        pe.wait_ge(p_taken, NH * l + h)
                    for i in range(3):
                        ins = pe.transpose(bank[4][:, i * P:(i + 1) * P], sc[:, h % 2, i * P:(i + 1) * P], ident)
                    ins.then_inc(p_turned, 1)

                def attend(kind, h, ready, count, ev):
                    pe.wait_ge(ready, count)
                    if h == 0:
                        if kind == 0:
                            pe.wait_ge(qk_gained, 4 * l + 3)
                        else:
                            pe.wait_ge(ys_low, 4 * l + 2)
                    r0, hp = HD * (h % 2), h // 2
                    o = bank[5][r0:r0 + HD, hp * SEQ:(hp + 1) * SEQ]
                    v = [V[:, kind, b, h * HD:(h + 1) * HD] for b in range(NB)]
                    pe.matmul(o, v[0], pT[:, h % 2, 0:2 * P], start=True, stop=False, skip_group_check=True)
                    pe.matmul(o[:, P:2 * P], v[1], pT[:, h % 2, 2 * P:3 * P], start=False, stop=True,
                              skip_group_check=True).then_inc(ev, 1)

                def fox_attend(h):
                    attend(0, h, p_taken, NH * l + h + 1, fox_out)

                def sb_attend(h):
                    attend(1, h, a_exp, NH * l + h + 1, sb_out)

                def sb_scores(pair):
                    for i in range(2):
                        h = 2 * pair + i
                        if pair == 0:
                            pe.wait_ge(qk_gained, 4 * l + 4)
                            pe.wait_ge(p_exp, 2 * (NH * l + 3 + i))
                        else:
                            pe.wait_ge(a_exp, NH * l + i + 1)
                        q, k = qk_of(1, h)
                        pe.matmul(bank[6 + i][:, 0:2 * P], k[:, 0:P], q, start=True, stop=False, skip_group_check=True)
                        pe.matmul(bank[6 + i][:, 2 * P:3 * P], k[:, P:2 * P], q[:, P:2 * P], start=False, stop=True,
                                  skip_group_check=True).then_inc(z_ready, 1)

                def sb_sums(pair):
                    for i in range(2):
                        pe.wait_ge(z_soft, NH * l + 2 * pair + i + 1)
                        b, s = bank[6 + i], sc[:, i, :]
                        mm = lambda o, a, c: pe.matmul(o, a, c, start=False, stop=False, skip_group_check=True)
                        mm(b[:, 0:2 * P], const("suffix"), s[:, 0:2 * P])
                        mm(b[:, P:2 * P], const("minus"), s[:, 2 * P:3 * P])
                        mm(b[:, 2 * P:3 * P], const("suffix"), s[:, 2 * P:3 * P])
                        mm(b[:, 0:P], ident, const("past"))
                        mm(b[:, 2 * P:3 * P], ident, const("past")).then_inc(z_cum, 1)

                def conv_stat(which):
                    if which == 0:
                        pe.wait_ge(conv_sum, 2 * l + 2)
                        pe.wait_ge(forget_in, l + 1)
                    else:
                        pe.wait_ge(conv_sq, l + 1)
                    for c in range(CT):
                        ins = pe.matmul(bank[4][:, which * SEQ:(which + 1) * SEQ], const("mean"),
                                        (ca if which == 0 else cs)[:, c, :], start=(c == 0), stop=(c == CT - 1),
                                        skip_group_check=True)
                    ins.then_inc((conv_mean, conv_var)[which], 1)

                def s5_out(pair):
                    pe.wait_ge(s5_state, ST // 2 * l + pair + 1)
                    if pair == 0:
                        pe.wait_ge(p_taken, NH * (l + 1))
                    for t in (2 * pair, 2 * pair + 1):
                        jj, th = t % 4, t // 4
                        o = bank[4][32 * jj:32 * jj + 32, th * SEQ:(th + 1) * SEQ]
                        for ri in range(2):
                            ins = pe.matmul(o, CTt[:, ri, 32 * t:32 * t + 32], bu[:, t, ri, :], start=(ri == 0),
                                            stop=(ri == 1), skip_group_check=True)
                    if pair == 3:
                        ins.then_inc(s5_y, 1)

                def glu():
                    pe.wait_ge(gelu_out, l + 1)
                    pe.wait_ge(a_exp, NH * l + 3)
                    w = par(l, "w_glu").rearrange("p (k c) -> p k c", k=CT)
                    g = tmp[:, 2, :].rearrange("p (a c) -> p a c", a=CT)
                    for c in range(CT):
                        for k in range(CT):
                            ins = pe.matmul(bank[6][:, c * SEQ:(c + 1) * SEQ], w[:, k, c * P:(c + 1) * P], g[:, k, :],
                                            start=(k == 0), stop=(k == CT - 1), skip_group_check=True)
                    ins.then_inc(glu_ready, 1)

                def gates(n, half, kh):
                    if kh == 0:
                        if n == 0:
                            pe.wait_ge(taken, 13 * l + (13, 12)[half])
                    j = 9 + 5 * n + 2 * half + kh

                    def free(_, b):
                        if kh == 0 and n:
                            pe.wait_ge(gated, 16 * l + 4 * (n - 1) + 2 * half + b + 1)

                    ins, s = wide_rows(U, j, 4, 4 * kh, KT - 1, hT, lambda _, b: bank[2 * half + b][:, :],
                                       gate_ready if kh else None, free)
                    ins.then_inc(used[s], 1)

                def branch_rows(n):
                    pe.wait_ge(ys_low, 4 * l + n + 1)
                    ys = (ys_hi[:, n % 2, :, :], ys_lo[:, n % 2, :, :])
                    ins, s = wide_rows(U, 13 + 5 * n, CT, 0, CT - 1, ys, lambda half, b: bank[2 * half + b][:, :], branch,
                                       lambda half, b: pe.wait_ge(gate_tanh, 16 * l + 4 * n + 2 * half + b + 1))
                    ins.then_inc(used[s], 1)

                for u in range(9):
                    project(u)
                    if u == 1:
                        s5_operands()
                    if 3 <= u <= 6:
                        bu_of(2 * (u - 3))
                        bu_of(2 * (u - 3) + 1)
                    if u == 7:
                        turn_qk(0, 0)
                        turn_qk(0, 1)
                        conv_stat(0)
                gates(0, 0, 0)
                conv_stat(1)
                fox_scores(0)
                gates(0, 0, 1)
                turn_qk(1, 0)
                turn_qk(1, 1)
                fox_scores(1)
                gates(0, 1, 0)
                turn_p(0)
                fox_scores(2)
                gates(0, 1, 1)
                fox_attend(0)
                turn_p(1)
                fox_scores(3)
                branch_rows(0)
                fox_attend(1)
                turn_p(2)
                gates(1, 0, 0)
                fox_attend(2)
                turn_p(3)
                sb_scores(0)
                gates(1, 0, 1)
                fox_attend(3)
                gates(1, 1, 0)
                sb_sums(0)
                gates(1, 1, 1)
                sb_attend(0)
                sb_attend(1)
                sb_scores(1)
                branch_rows(1)
                gates(2, 0, 0)
                sb_sums(1)
                gates(2, 0, 1)
                sb_attend(2)
                sb_attend(3)
                gates(2, 1, 0)
                s5_out(0)
                gates(2, 1, 1)
                s5_out(1)
                branch_rows(2)
                gates(3, 0, 0)
                s5_out(2)
                s5_out(3)
                gates(3, 0, 1)
                gates(3, 1, 0)
                glu()
                gates(3, 1, 1)
                branch_rows(3)

                pe.wait_ge(merged, 12 * (l + 1))
                pe.wait_ge(glu_tanh, l + 1)
                turn(3 * l + 1, M, 4)
                for i in range(4):
                    def free(half, b, i=i):
                        if i == 0 and half == 0 and b == 0:
                            pe.wait_ge(turned_lo, KT * (3 * l + 2))
                    ins, s = wide_rows(U, 29 + i, 2, 2 * i, KT - 1, hT, lambda half, b: bank[2 * half + b][:, :], None, free)
                    ins.then_inc(used[s], 1)

                pe.wait_ge(normed, NB * (2 * l + 2))
                turn(3 * l + 2, H, 0)
                pe.wait_ge(turned_lo, KT * (3 * l + 3))
                if l == 0:
                    def hidden(u, j, c, odd, which):
                        ins, s = channel_rows(u, j, bank[2 * odd + which])
                        ins.then_inc(used[s], 1)

                    def down(u, j, c, odd, first, last):
                        pe.wait_ge(g_lo, c + 1)
                        s = arrive(u, j)
                        w = parts(s, 2)
                        g = (ys_hi[:, odd, :, :], ys_lo[:, odd, :, :])
                        for half in range(2):
                            for b in range(NB):
                                for f in range(2):
                                    ins = product(bank[4 + 2 * half + b][:, :], cut(g, everything, f, slice(b * P, (b + 1) * P)),
                                                  cut(w, everything, f, slice(half * 512, (half + 1) * 512)),
                                                  first and f == 0, last and f == 1)
                        ins.then_inc(used[s], 1)

                    u = Units(DENSE0)
                    hidden(u, 0, 0, 0, 0)
                    hidden(u, 1, 0, 0, 1)

                    def pair(i, first):
                        u = Units(DENSE0, i * 2)
                        for m in range(2):
                            c, odd = i * 2 + 1 + m, 1 - m
                            if not (first and m == 0):
                                pe.wait_ge(g_ready, c - 1)
                            hidden(u, 2 + 3 * m, c, odd, 0)
                            hidden(u, 3 + 3 * m, c, odd, 1)
                            down(u, 4 + 3 * m, i * 2 + m, m, first and m == 0, False)

                    pair(0, True)
                    with pe.Fori(1, PAIRS) as i:
                        pair(i, False)
                    down(Units(DENSE0), FFN_UNITS - 1, NCH - 1, 0, False, True)

            pe.wait_ge(small_lo, 3)
            for b in range(NB):
                for k in range(KT):
                    cols = slice(2 * KT * NH + k * NE, 2 * KT * NH + (k + 1) * NE)
                    ins = product(bank[4][:, b * NE:(b + 1) * NE], cut(hT, everything, k, slice(b * P, (b + 1) * P)),
                                  cut((smallw_hi, smallw_lo), everything, cols), k == 0, k == KT - 1)
            ins.then_inc(logits, 1)
            pe.wait_ge(chosen, 1)
            sel = route[:, 5, :, :]
            pe.matmul(bank[5][:, 0:NE], const("tri_strict"), sel[:, 0, :], start=True, stop=True)
            pe.matmul(bank[5][:, NE:2 * NE], const("tri_strict"), sel[:, 1, :], start=True, stop=False,
                      skip_group_check=True)
            pe.matmul(bank[5][:, NE:2 * NE], const("ones"), sel[:, 0, :], start=False, stop=True, skip_group_check=True)
            pe.matmul(bank[5][:, 2 * NE:3 * NE], const("ones"), sel[:, 0, :], start=True, stop=False,
                      skip_group_check=True)
            pe.matmul(bank[5][:, 2 * NE:3 * NE], const("ones"), sel[:, 1, :], start=False, stop=True,
                      skip_group_check=True).then_inc(places, 1)

            def gather(n, i, free):
                pe.wait_ge(picked, n + 1)
                if not (isinstance(free, int) and free == 0):
                    pe.wait_ge(side_done, free)
                for k in range(4 * i, 4 * i + 4):
                    for b in range(NB):
                        for part in range(2):
                            ins = pe.matmul(bank[7][:, k % 4 * P:(k % 4 + 1) * P], h_parts[part][:, b, k * P:(k + 1) * P],
                                            picks[:, b, :], start=(b + part == 0), stop=(b + part == NB),
                                            skip_group_check=True)
                ins.then_inc(gathered, 1)

            def turn_back(n, free):
                pe.wait_ge(picked_back, n + 1)
                pe.wait_ge(side_done, free)
                for b in range(NB):
                    ins = pe.transpose(bank[7][:, b * P:(b + 1) * P], picks_back[:, b, :], ident)
                ins.then_inc(back_turned, 1)

            def spread_rows(n, i, free):
                pe.wait_ge(y_lo, n * 2 + 2)
                pe.wait_ge(side_done, free)
                for b in range(NB):
                    for part in range(2):
                        ins = pe.matmul(bank[7][:, b * DB:(b + 1) * DB], back[:, b * P:(b + 1) * P],
                                        y_parts[part][:, bass.ds(i * DB, DB)], start=(part == 0), stop=(part == 1),
                                        skip_group_check=True)
                ins.then_inc(spread, 1)

            def hidden(g, odd, which, p):
                w = parts(which, KT)
                for k in range(KT):
                    if k % (KT // 2) == 0:
                        half = k // (KT // 2)
                        pe.wait_ge(moe_lo[2 * which + half], g + 1)
                    ins = product(bank[2 * odd + which][:, 0:CH], cut(hT, everything, k, slice(p * P, (p + 1) * P)),
                                  cut(w, everything, k, everything), k == 0, k == KT - 1)
                    if k % (KT // 2) == KT // 2 - 1:
                        ins.then_inc(moe_used[2 * which + half], 1)

            def turn_hidden(g, odd):
                pe.wait_ge(moe_gated, g + 1)
                for f in range(2):
                    ins = pe.transpose(bank[6][:, f * P:(f + 1) * P], gated_h[:, odd, 0, f * P:(f + 1) * P], ident)
                ins.then_inc(moe_turned, 1)

            def down(g, odd, first, last):
                pe.wait_ge(moe_g_lo, g + 1)
                w = parts(2, 2)
                h = (ys_hi[:, odd, 0, :], ys_lo[:, odd, 0, :])
                for f in range(2):
                    pe.wait_ge(moe_lo[4 + f], g + 1)
                    for half in range(2):
                        ins = product(bank[4 + half][:, :], cut(h, everything, slice(f * P, (f + 1) * P)),
                                      cut(w, everything, f, slice(half * 512, (half + 1) * 512)),
                                      first and f == 0, last and f == 1)
                    ins.then_inc(moe_used[4 + f], 1)

            def turn_of(n, p, carry, more, free):
                def step(c, odd, job=None):
                    g = n * NCH + c
                    at = c if isinstance(c, int) else None
                    if at == 0:
                        pe.wait_ge(side_done, free)
                    if not (isinstance(g, int) and g < 2):
                        pe.wait_ge(moe_gated, g - 1)
                    hidden(g, odd, 0, p)
                    if at != 0 or carry:
                        turn_hidden(g - 1, 1 - odd)
                    hidden(g, odd, 1, p)
                    if at == 0 and carry:
                        turn_back(n - 1, free)
                    if at in (1, 2) and more:
                        gather(n + 1, at - 1, free + carry + at - 1)
                    if job:
                        job()
                    if at == 1 and carry:
                        pe.wait_ge(y_lo, n * 2)
                    if at != 0 or carry:
                        down(g - 1, 1 - odd, at == 1, at == 0)

                for c in range(3):
                    step(c, (p + c) % 2)
                with pe.Fori(0, 4) as i:
                    step(i * 2 + 3, 1 - p, (lambda: spread_rows(n - 1, i, free + 1 + 2 * more + i)) if carry else None)
                    step(i * 2 + 4, p)

            def finish(n, p, free):
                g = n * NCH + NCH - 1
                turn_hidden(g, p)
                turn_back(n, free)
                down(g, p, False, True)
                for i in range(4):
                    spread_rows(n, i, free + 1 + i)

            pe.wait_ge(h_low, NB)
            for i in range(2):
                gather(0, i, i)
            turn_of(0, 0, False, True, 2)
            with pe.Fori(0, NE // 2 - 1) as i:
                for m in range(2):
                    n = i * 2 + 1 + m
                    turn_of(n, 1 - m, True, True, n * 7 - 3)
            turn_of(NE - 1, 1, True, False, (NE - 1) * 7 - 3)
            finish(NE - 1, 1, NE * 7 - 5)
            pe.wait_ge(spill_known, 1)
            n_spill = pe.value_load(spill_i[0:1, 0:1], min_val=0, max_val=N_SPILL)
            for t in range(N_SPILL):
                with pe.If(n_spill > t):
                    n, p = NE + t, t % 2
                    for i in range(2):
                        gather(n, i, n * 7 + i)
                    turn_of(n, p, False, False, n * 7 + 2)
                    finish(n, p, n * 7 + 2)


def constants():
    i = np.arange(P)
    row, col = i[:, None], i[None, :]
    t = {
        "ident": row == col, "tri": row <= col, "tri_strict": row < col, "ones": np.ones((P, P)),
        "later": row > col, "suffix": -1.0 * (row >= col), "minus": -np.ones((P, P)), "mean": np.full((P, P), 1.0 / DB),
        "causal": np.where(col > row, -BIG, 0.0), "past": np.where(row < col, 0.0, -BIG),
        "keep": np.concatenate([row < col, np.ones((P, P)), row < col], axis=1),
        "iota": np.broadcast_to(col, (P, P)), "parity": np.stack([(i // GH) % 2 == 0, (i // GH) % 2 == 1], axis=1),
        "side": np.stack([i < GP, i >= GP], axis=1), "iota8": np.broadcast_to(np.arange(NE), (P, NE)),
    }
    out = np.zeros((P, N_CONST), np.float32)
    for name, (a, b) in CONST.items():
        out[:, a:b] = t[name]
    return out


def lay_out(a):
    def cols(v):
        return v.reshape(-1, P).T

    def rows(v):
        return np.broadcast_to(v, (P, v.size))

    def state(v):
        return v.reshape(ST, 2, GP).transpose(1, 2, 0).reshape(P, ST)

    params = []
    for l in range(2):
        t = {
            "g_mix": cols(a["g_mix"][l]), "g_ffn": cols(a["g_ffn"][l]), "b_forget": rows(a["b_forget"][l]),
            "lam_re": state(a["s5_lam_re"][l]), "lam_im": state(a["s5_lam_im"][l]),
            "log_dt": state(np.broadcast_to(a["s5_log_dt"][l][:, None], (NG, GP))),
            "s5_d": cols(a["s5_d"][l]), "conv_b": cols(a["conv_b"][l]), "ln_g": cols(a["conv_ln_g"][l]),
            "ln_b": cols(a["conv_ln_b"][l]),
            "conv_w": a["conv_w"][l].reshape(CONVW, CT, P).transpose(2, 1, 0).reshape(P, CT * CONVW),
            "w_glu": a["s5_w_glu"][l].reshape(CT, P, DB).transpose(1, 0, 2).reshape(P, CT * DB),
            "w_forget": a["w_in"][l][:, IN_F:IN_F + NH].reshape(KT, P, NH).transpose(1, 0, 2).reshape(P, KT * NH),
        }
        for n in ("fox_q", "fox_k", "sb_q", "sb_k"):
            t[n] = cols(np.tile(a[n + "_gain"][l], P // HD))
        for n in ("b_re", "b_im"):
            t[n] = a["s5_" + n][l].reshape(ST, 2, GP, GH).transpose(1, 2, 0, 3).reshape(P, ST * GH)
        for n in ("c_re", "c_im"):
            t[n] = a["s5_" + n][l].reshape(CT, P, GP).transpose(1, 0, 2).reshape(P, CT * GP)
        params += [t[n] for n in PARAM]
    router = [a["router_w"][0].reshape(KT, P, NE).transpose(1, 0, 2).reshape(P, KT * NE), rows(a["router_b"][0])]
    return np.concatenate(params, axis=1), np.concatenate(router, axis=1)


BIG_INPUTS = ["x", "w_in", "w_branch", "w_out", "ffn_w1", "ffn_w3", "ffn_w2", "moe_w1", "moe_w3", "moe_w2"]


def kernel(**inputs):
    import concourse.bacc as bacc
    from concourse.bass_utils import run_bass_kernel_spmd

    a = {k: np.ascontiguousarray(v) for k, v in inputs.items()}
    arrays = {n: a[n] for n in BIG_INPUTS}
    arrays["consts"] = constants()
    arrays["params"], arrays["router"] = (np.ascontiguousarray(t) for t in lay_out(a))
    nc = bacc.Bacc("TRN2", target_bir_lowering=False, num_devices=1, dynamic_dma_scratch_size=1024)
    aps = {n: nc.dram_tensor(n + "_dram", v.shape, mybir.dt.from_np(v.dtype), kind="ExternalInput").ap()
           for n, v in arrays.items()}
    out = nc.dram_tensor("out_dram", a["x"].shape, F32, kind="ExternalOutput").ap()
    build(nc, out=out, **aps)
    r = run_bass_kernel_spmd(nc, [{n + "_dram": v for n, v in arrays.items()}], core_ids=[0])
    return r.results[0]["out_dram"]
```

```python
from contextlib import ExitStack

import numpy as np

import concourse.bass as bass
from concourse import mybir

ALU = mybir.AluOpType
ACT = mybir.ActivationFunctionType
AX_X = mybir.AxisListType.X
F32 = mybir.dt.float32
F32R = mybir.dt.float32r
I32 = mybir.dt.int32
U32 = mybir.dt.uint32

P = 128
D = 1024
KT = D // P
SEQ = 256
NB = SEQ // P
DB = 256
CT = DB // P
HD = 64
NH = DB // HD
CONVW = 31
PAD = CONVW - 1
DFF = 2816
CH = 256
NCH = DFF // CH
NE = 8
EPS = 1e-6
BIG = 1e30
NG, GP, GH = 16, 64, 16
ST = NG // 2

IN_S5, IN_FOX, IN_F = 0, DB, 4 * DB
IN_CONV = IN_F + NH
IN_SB = IN_CONV + 2 * DB
IN_GATE = IN_SB + 3 * DB
D_PROJ = IN_GATE + 4 * D

UNIT = 2048
RING = 3
MIX_UNITS = 33
FFN_UNITS = 3 * NCH
assert MIX_UNITS % RING == 0 and FFN_UNITS % RING == 0

CONST = {}
_at = 0
for _name, _n in (("ident", P), ("power", 1), ("tri", P), ("tri_strict", P), ("ones", P), ("later", P), ("suffix", P),
                  ("minus", P), ("mean", P), ("keep", 3 * P), ("iota", P), ("parity", 2), ("side", 2), ("iota8", NE),
                  ("causal", P), ("past", P)):
    CONST[_name] = (_at, _at + _n)
    _at += _n
N_CONST = _at
N_STAY = CONST["causal"][0]

PARAM = {}
_at = 0
for _name, _n in (("g_mix", KT), ("g_ffn", KT), ("b_forget", NH), ("fox_q", 1), ("fox_k", 1), ("sb_q", 1),
                  ("sb_k", 1), ("lam_re", ST), ("lam_im", ST), ("log_dt", ST), ("b_re", ST * GH),
                  ("b_im", ST * GH), ("c_re", CT * GP), ("c_im", CT * GP), ("s5_d", CT),
                  ("conv_w", CT * CONVW), ("conv_b", CT), ("ln_g", CT), ("ln_b", CT), ("w_glu", CT * DB),
                  ("w_forget", KT * NH)):
    PARAM[_name] = (_at, _at + _n)
    _at += _n
N_PARAM = _at
N_ROUTER = KT * NE + NE

TWO_PI_1, TWO_PI_2 = 6.28125, 0.0019340515136719
TWO_PI_3 = 2 * np.pi - TWO_PI_1 - TWO_PI_2
ROUND = 1.5 * 2.0 ** 23
PI_F32 = 3.1415925


class Units:

    def __init__(self, base, steps=0):
        assert base % RING == 0
        self.base, self.steps = base // RING, steps

    def slot(self, j):
        return j % RING

    def earlier(self, j):
        return self.base + self.steps + j // RING

    def is_first(self, j):
        return isinstance(self.steps, int) and self.earlier(j) == 0


class Chain:

    def __init__(self, eng, sem):
        self.eng, self.sem, self.n = eng, sem, 0

    def __call__(self, ins):
        self.n += 1
        ins.then_inc(self.sem, 1)
        self.eng.wait_ge(self.sem, self.n)

    def mark(self, ins):
        self.n += 1
        ins.then_inc(self.sem, 1)

    def settle(self):
        self.eng.wait_ge(self.sem, self.n)


def build(nc, x, consts, params, router, w_in, w_branch, w_out, ffn_w1, ffn_w3, ffn_w2, moe_w1, moe_w3, moe_w2,
          out):
    with ExitStack() as ctx:
        def sb(name, shape, dt=F32):
            return ctx.enter_context(nc.sbuf_tensor(name, shape, dt))

        def sem(name):
            return ctx.enter_context(nc.semaphore(name))

        bank = [ctx.enter_context(nc.psum_tensor(f"bank{i}", [P, 512], F32)) for i in range(8)]

        raw = sb("raw", [P, RING, UNIT])
        high = sb("high", [P, RING, UNIT], F32R)
        low = sb("low", [P, RING, UNIT], F32R)
        X = sb("X", [P, NB, D])
        H = sb("H", [P, NB, D])
        G2 = sb("G2", [P, NB, D])
        hT_hi = sb("hT_hi", [P, KT, SEQ], F32R)
        hT_lo = sb("hT_lo", [P, KT, SEQ], F32R)
        C = sb("C", [P, N_STAY])
        PR = sb("PR", [P, 2, N_PARAM])
        RT = sb("RT", [P, N_ROUTER])
        smallw_hi = sb("smallw_hi", [P, 2 * KT * NH + KT * NE], F32R)
        smallw_lo = sb("smallw_lo", [P, 2 * KT * NH + KT * NE], F32R)
        masks = sb("masks", [P, 3 * P], F32R)
        stat = sb("stat", [P, 8])
        s5p = sb("s5p", [P, 20, ST])
        s5b = sb("s5b", [P, 2, ST, 2, GH])
        s5c = sb("s5c", [P, 2, CT, 2, GP])
        BT = sb("BT", [P, 2, CT, P])
        CTt = sb("CTt", [P, 2, DB])
        bu = sb("bu", [P, ST, 2, SEQ])
        silu = bu[:, 0:2, :, :]
        gated_h = bu[:, 2:4, :, :]
        upad = G2[:, 0, 0:CT * (PAD + SEQ)].rearrange("p (a c) -> p a c", a=CT)
        qk = H[:, 0, :].rearrange("p (w b c) -> p w b c", w=2, b=NB)
        sq = G2[:, 1, :].rearrange("p (w b c) -> p w b c", w=2, b=NB)
        nrm = sb("nrm", [P, 2, 2, NB * NH])
        pT = sb("pT", [P, 2, 3 * P])
        lg_rows = pT[:, 1, 0:SEQ]
        lf = sb("lf", [P, 4, NB * NH])
        sc = sb("sc", [P, 2, 3 * P])
        mx = sb("mx", [P, 2, NH, 2])
        rs = sb("rs", [P, 2, NH, 2])
        route = sb("route", [P, 12, NB, NE])
        top_at = sb("top_at", [P, NB, NE], U32)
        spill = sb("spill", [P, 4, NE])
        spill_i = sb("spill_i", [1, 4], I32)
        ys_hi = sb("ys_hi", [P, 2, CT, SEQ], F32R)
        ys_lo = sb("ys_lo", [P, 2, CT, SEQ], F32R)

        with ExitStack() as mixers:
            def mixer_sb(name, shape):
                return mixers.enter_context(nc.sbuf_tensor(name, shape, F32))

            rot_c = mixer_sb("rot_c", [P, ST, SEQ])
            rot_s = mixer_sb("rot_s", [P, ST, SEQ])
            V = mixer_sb("V", [P, 2, NB, DB])
            qT = mixer_sb("qT", [P, 2, 2, CT, SEQ])
            uT = mixer_sb("uT", [P, CT, SEQ])
            tmp = mixer_sb("tmp", [P, 4, 2 * SEQ])
            ca = mixer_sb("ca", [P, CT, SEQ])
            cs = mixer_sb("cs", [P, CT, SEQ])
            lnv = mixer_sb("lnv", [P, 2, SEQ])
            M = mixer_sb("M", [P, NB, D])
            TL = M[:, :, :].rearrange("p a c -> p (a c)")[:, 0:NH * 3 * P].rearrange("p (h i c) -> p h i c", h=NH, i=3)
        h_parts = [sb(f"h_parts{i}", [P, NB, D], F32R) for i in range(2)]
        y_parts = [sb(f"y_parts{i}", [P, D], F32R) for i in range(2)]
        picks = sb("picks", [P, NB, P], F32R)
        back = sb("back", [P, NB * P], F32R)
        raw_odd = sb("raw_odd", [P, RING, UNIT])
        picks_back = G2[:, 0, 0:NB * P].rearrange("p (b c) -> p b c", b=NB)

        def const(name, a=0, b=None, rows=P):
            lo_, hi_ = CONST[name]
            return C[0:rows, lo_ + a:(hi_ if b is None else lo_ + b)]

        def par(l, name, a=0, b=None):
            lo_, hi_ = PARAM[name]
            return PR[:, l, lo_ + a:(hi_ if b is None else lo_ + b)]

        ident = const("ident")

        raw_ready = [sem(f"raw_ready{s}") for s in range(RING)]
        hi_ready = [sem(f"hi_ready{s}") for s in range(RING)]
        lo_ready = [sem(f"lo_ready{s}") for s in range(RING)]
        used = [sem(f"used{s}") for s in range(RING)]
        x_loaded = [sem(f"x_loaded{b}") for b in range(NB)]
        ident_loaded = sem("ident_loaded")
        consts_loaded = sem("consts_loaded")
        params_loaded = [sem(f"params_loaded{l}") for l in range(2)]
        router_loaded = sem("router_loaded")
        masks_loaded = sem("masks_loaded")
        masks_ready = sem("masks_ready")
        stored = sem("stored")
        act_step = sem("act_step")
        dve_step = sem("dve_step")
        small_hi = sem("small_hi")
        small_lo = sem("small_lo")
        squared = sem("squared")
        pool_step = sem("pool_step")
        rms_root = sem("rms_root")
        last_rows = sem("last_rows")
        normed = sem("normed")
        turned = sem("turned")
        turned_hi = sem("turned_hi")
        turned_lo = sem("turned_lo")
        s5_exp = sem("s5_exp")
        s5_arg = sem("s5_arg")
        s5_sin = sem("s5_sin")
        s5_spread = sem("s5_spread")
        s5_turned = sem("s5_turned")
        s5_lhs = sem("s5_lhs")
        small_logits = sem("small_logits")
        small_rows = sem("small_rows")
        small_turned = sem("small_turned")
        forget_in = sem("forget_in")
        forget_ln = sem("forget_ln")
        forget_tri = sem("forget_tri")
        taken = sem("taken")
        bu_ready = sem("bu_ready")
        bu_taken = sem("bu_taken")
        conv_sum = sem("conv_sum")
        conv_mean = sem("conv_mean")
        conv_cent = sem("conv_cent")
        conv_sq = sem("conv_sq")
        conv_var = sem("conv_var")
        conv_vare = sem("conv_vare")
        conv_root = sem("conv_root")
        conv_lin = sem("conv_lin")
        conv_tanh = sem("conv_tanh")
        conv_out = sem("conv_out")
        qk_mean = sem("qk_mean")
        qk_root = sem("qk_root")
        qk_normed = sem("qk_normed")
        qk_turned = sem("qk_turned")
        qk_gained = sem("qk_gained")
        score = sem("score")
        row_max = sem("row_max")
        p_exp = sem("p_exp")
        p_norm = sem("p_norm")
        p_turned = sem("p_turned")
        p_taken = sem("p_taken")
        fox_out = sem("fox_out")
        z_ready = sem("z_ready")
        z_ln = sem("z_ln")
        z_soft = sem("z_soft")
        z_cum = sem("z_cum")
        a_exp = sem("a_exp")
        sb_out = sem("sb_out")
        s5_state = sem("s5_state")
        s5_y = sem("s5_y")
        gelu_in = sem("gelu_in")
        gelu_tanh = sem("gelu_tanh")
        gelu_out = sem("gelu_out")
        glu_ready = sem("glu_ready")
        glu_tanh = sem("glu_tanh")
        glu_out = sem("glu_out")
        ys_high = sem("ys_high")
        ys_low = sem("ys_low")
        gate_ready = sem("gate_ready")
        gate_tanh = sem("gate_tanh")
        branch = sem("branch")
        gated = sem("gated")
        merged = sem("merged")
        silu_ready = sem("silu_ready")
        g_ready = sem("g_ready")
        g_hi = sem("g_hi")
        g_lo = sem("g_lo")
        top_gap = sem("top_gap")
        top_exp = sem("top_exp")
        chosen = sem("chosen")
        places = sem("places")
        spill_known = sem("spill_known")
        picked = sem("picked")
        moe_raw = [[sem(f"moe_raw{odd}{i}") for i in range(6)] for odd in range(2)]
        moe_hi = [sem(f"moe_hi{i}") for i in range(6)]
        moe_lo = [sem(f"moe_lo{i}") for i in range(6)]
        moe_used = [sem(f"moe_used{i}") for i in range(6)]
        moe_silu = sem("moe_silu")
        moe_gated = sem("moe_gated")
        moe_turned = sem("moe_turned")
        moe_g_hi = sem("moe_g_hi")
        moe_g_lo = sem("moe_g_lo")
        picked_back = sem("picked_back")
        back_turned = sem("back_turned")
        side_done = sem("side_done")
        y_hi = sem("y_hi")
        y_lo = sem("y_lo")
        h_high = sem("h_high")
        h_low = sem("h_low")
        gathered = sem("gathered")
        gather_hi = sem("gather_hi")
        spread = sem("spread")
        finished = sem("finished")
        x_mixed = sem("x_mixed")
        block = ctx.enter_context(nc.Block())

        ORDER = (2, 1, 3, 0)
        COLS = [IN_CONV, IN_CONV + DB, IN_S5] + [IN_FOX + DB * i for i in range(3)] + [IN_SB + DB * i for i in range(3)]
        mix_src = []

        def k_rows(w, k0, nk, c0, n):
            return w.rearrange("(k p) c -> p k c", p=P)[:, k0:k0 + nk, c0:c0 + n]

        for l in range(2):
            src = [k_rows(w_in[l], 0, KT, c, DB) for c in COLS]
            for n in ORDER:
                for half in range(2):
                    for kh in range(2):
                        src.append(k_rows(w_in[l], 4 * kh, 4, IN_GATE + n * D + half * 512, 512))
                src.append(k_rows(w_branch[l, n], 0, CT, 0, D))
            src += [k_rows(w_out[l], 2 * i, 2, 0, D) for i in range(4)]
            assert len(src) == MIX_UNITS
            mix_src.append(src)

        def unit_view(t, s, nk):
            return t[:, s, :].rearrange("p (k c) -> p k c", k=nk)

        BASE = [0, MIX_UNITS + FFN_UNITS]
        DENSE0 = MIX_UNITS
        MIX_SPLITS = (2 * MIX_UNITS + FFN_UNITS) // RING

        PAIRS = (NCH - 1) // 2
        N_SPILL = 2 * SEQ // (P + 1)

        FFN_TURN_BANK = (4, 0)
        END_BANK = (7, 0, 1, 2)
        PROJ_BANK = (0, 1, 2, 3, 0, 1, 2, 3, 5)
        SMALL = [slice(l * KT * NH, (l + 1) * KT * NH) for l in range(2)] + [slice(2 * KT * NH, 2 * KT * NH + KT * NE)]

        def wait_products(eng, u, j):
            eng.wait_ge(used[u.slot(j)], u.earlier(j) + 1)

        @block.sync
        def _(sp):
            for b in range(NB):
                sp.dma_start(X[:, b, :], x[0, b * P:(b + 1) * P, :]).then_inc(x_loaded[b], 16)
            sp.dma_start(C[:, 0:P + 1], consts[:, 0:P + 1]).then_inc(ident_loaded, 16)

            def load(u, j, src):
                s = u.slot(j)
                if not u.is_first(j):
                    sp.wait_ge(lo_ready[s], u.earlier(j))
                sp.dma_start(unit_view(raw, s, src.shape[1]), src).then_inc(raw_ready[s], 16)

            def load_ffn(base, steps, w1, w3, w2):
                w1, w3 = (w.rearrange("(k p) n -> p k n", p=P) for w in (w1, w3))
                w2 = w2.rearrange("(c p) n -> p c n", p=P)
                u = Units(base, steps)
                load(u, 0, w1[:, :, 0:CH])
                load(u, 1, w3[:, :, 0:CH])
                with sp.Fori(0, PAIRS) as i:
                    u = Units(base, steps + i * 2)
                    for m in range(2):
                        load(u, 2 + 3 * m, w1[:, :, bass.ds(i * (2 * CH) + (1 + m) * CH, CH)])
                        load(u, 3 + 3 * m, w3[:, :, bass.ds(i * (2 * CH) + (1 + m) * CH, CH)])
                        load(u, 4 + 3 * m, w2[:, bass.ds(i * 4 + 2 * m, 2), :])
                load(Units(base, steps), FFN_UNITS - 1, w2[:, 2 * NCH - 2:2 * NCH, :])

            def load_chunk(n, e, c, odd, first=None):
                g = n * NCH + c
                w1, w3 = (w[0, e].rearrange("(k p) n -> p k n", p=P) for w in (moe_w1, moe_w3))
                w2 = moe_w2[0, e].rearrange("(c p) n -> p c n", p=P)
                for kind in range(3):
                    for half in range(2):
                        if first == 0:
                            sp.wait_ge(lo_ready[kind], MIX_SPLITS)
                        elif first == 1:
                            sp.wait_ge(x_mixed, 12)
                        else:
                            sp.wait_ge(moe_lo[2 * kind + half], g - 1)
                        dst = (raw, raw_odd)[odd][:, kind, half * UNIT // 2:(half + 1) * UNIT // 2]
                        if kind < 2:
                            dst = dst.rearrange("p (k c) -> p k c", k=KT // 2)
                            src = (w1, w3)[kind][:, half * KT // 2:(half + 1) * KT // 2, bass.ds(c * CH, CH)]
                        else:
                            src = w2[:, bass.ds(c * 2 + half, 1), :].rearrange("p a n -> p (a n)")
                        sp.dma_start(dst, src).then_inc(moe_raw[odd][2 * kind + half], 16)

            def load_turn(n, e, p):
                if isinstance(n, int) and n == 0:
                    load_chunk(0, e, 0, 0, 0)
                    load_chunk(0, e, 1, 1, 1)
                    load_chunk(0, e, 2, 0)
                    start = 1
                else:
                    load_chunk(n, e, 0, p)
                    start = 0
                with sp.Fori(start, PAIRS) as i:
                    load_chunk(n, e, i * 2 + 1, 1 - p)
                    load_chunk(n, e, i * 2 + 2, p)

            for l in range(2):
                u = Units(BASE[l])
                for j, src in enumerate(mix_src[l]):
                    load(u, j, src)
                    if l == 0 and j == 0:
                        sp.dma_start(PR[:, 0, :], params[:, 0:N_PARAM]).then_inc(params_loaded[0], 16)
                    if l == 0 and j == 1:
                        sp.dma_start(C[:, P + 1:], consts[:, P + 1:N_STAY]).then_inc(consts_loaded, 16)
                        sp.dma_start(M[:, 0, 0:2 * P], consts[:, N_STAY:]).then_inc(masks_loaded, 16)
                    if l == 0 and j == 2:
                        sp.dma_start(PR[:, 1, :], params[:, N_PARAM:]).then_inc(params_loaded[1], 16)
                        sp.dma_start(RT[:, :], router).then_inc(router_loaded, 16)
                if l == 0:
                    load_ffn(DENSE0, 0, ffn_w1[0], ffn_w3[0], ffn_w2[0])
            load_turn(0, 0, 0)
            with sp.Fori(0, NE // 2 - 1) as i:
                load_turn(i * 2 + 1, i * 2 + 1, 1)
                load_turn(i * 2 + 2, i * 2 + 2, 0)
            load_turn(NE - 1, NE - 1, 1)
            for i in range(4):
                sp.wait_ge(side_done, NE * 7 - 3 + i)
                cols = slice(i * DB, (i + 1) * DB)
                sp.dma_start(out.rearrange("a (b p) d -> p (a b) d", p=P)[:, :, cols], X[:, :, cols]).then_inc(stored, 16)
            sp.wait_ge(stored, 16 * 4)
            sp.wait_ge(spill_known, 1)
            n_spill = sp.value_load(spill_i[0:1, 0:1], min_val=0, max_val=N_SPILL)
            for t in range(N_SPILL):
                with sp.If(n_spill > t):
                    n = NE + t
                    e = sp.value_load(spill_i[0:1, 1 + t:2 + t], min_val=0, max_val=NE - 1)
                    load_turn(n, e, t % 2)
            with sp.If(n_spill > 0):
                sp.wait_ge(finished, 1)
                sp.dma_start(out.rearrange("a (b p) d -> p (a b) d", p=P), X[:, :, :]).then_inc(stored, 16)
                sp.wait_ge(stored, 16 * 5)

        @block.gpsimd
        def _(pool):
            def split_low(u, j):
                s = u.slot(j)
                pool.wait_ge(hi_ready[s], u.earlier(j) + 1)
                pool.tensor_tensor(low[:, s, :], raw[:, s, :], high[:, s, :].bitcast(F32),
                                   ALU.subtract).then_inc(lo_ready[s], 1)

            step = Chain(pool, pool_step)

            def norm_root(r):
                for b in range(NB):
                    pool.wait_ge(squared, 4 * r + 2 * b + 1)
                    step(pool.tensor_scalar(stat[:, 4 + b:5 + b], stat[:, 2 * b:2 * b + 1], D * EPS, None, ALU.add))
                    pool.wait_ge(squared, 4 * r + 2 * b + 2)
                    total, factor = stat[:, 4 + b:5 + b], stat[:, 6 + b:7 + b]
                    step(pool.tensor_tensor(total, total, stat[:, 2 * b + 1:2 * b + 2], ALU.add))
                    pool.tensor_tensor(factor, total, const("power"), ALU.pow).then_inc(rms_root, 1)

            pool.wait_ge(ident_loaded, 16)

            def split_rounds(a, b):
                with pool.Fori(0, b - a) as i:
                    for j in range(RING):
                        split_low(Units(a * RING, i), j)

            norm_root(0)
            rounds = 0
            for r in range(3):
                end = (MIX_UNITS, MIX_UNITS + FFN_UNITS, 2 * MIX_UNITS + FFN_UNITS)[r] // RING
                split_rounds(rounds, end)
                if r < 2:
                    for j in range(RING):
                        if j == RING - 1:
                            norm_root(r + 1)
                        split_low(Units(end * RING), j)
                rounds = end + 1

            def split_half(kind, half, g, odd):
                i, cols = 2 * kind + half, slice(half * UNIT // 2, (half + 1) * UNIT // 2)
                pool.wait_ge(moe_hi[i], g + 1)
                pool.tensor_tensor(low[:, kind, cols], (raw, raw_odd)[odd][:, kind, cols], high[:, kind, cols].bitcast(F32),
                                   ALU.subtract).then_inc(moe_lo[i], 1)

            def split_first(n):
                for kind in range(2):
                    for half in range(2):
                        split_half(kind, half, n * NCH, n % 2)

            def split_turns(n, turns):
                with pool.Fori(0, turns * NCH // 2) as i:
                    for m in range(2):
                        for half in range(2):
                            split_half(2, half, n * NCH + i * 2 + m, (n + m) % 2)
                if turns * NCH % 2:
                    for half in range(2):
                        split_half(2, half, (n + turns) * NCH - 1, n % 2)

            split_first(0)
            norm_root(3)
            split_turns(0, NE)
            pool.wait_ge(spill_known, 1)
            n_spill = pool.value_load(spill_i[0:1, 0:1], min_val=0, max_val=N_SPILL)
            for t in range(N_SPILL):
                with pool.If(n_spill > t):
                    split_first(NE + t)
                    split_turns(NE + t, 1)

        @block.scalar
        def _(act):
            step = Chain(act, act_step)

            def split_high(u, j):
                s = u.slot(j)
                act.wait_ge(raw_ready[s], u.earlier(j) * 16 + 16)
                if not u.is_first(j):
                    act.wait_ge(used[s], u.earlier(j))
                act.activation(high[:, s, :], raw[:, s, :], ACT.Copy).then_inc(hi_ready[s], 1)

            def split_half(kind, half, g, odd):
                i, cols = 2 * kind + half, slice(half * UNIT // 2, (half + 1) * UNIT // 2)
                act.wait_ge(moe_raw[odd][i], g * 8 + (16 - 8 * odd))
                if isinstance(g, int) and g == 0:
                    act.wait_ge(used[kind], MIX_SPLITS)
                else:
                    act.wait_ge(moe_used[i], g)
                act.activation(high[:, kind, cols], (raw, raw_odd)[odd][:, kind, cols], ACT.Copy).then_inc(moe_hi[i], 1)

            def square_rows(r):
                for b in range(NB):
                    for half in range(2):
                        if r:
                            act.wait_ge(x_mixed, 4 * (r - 1) + 2 * b + half + 1)
                        elif half == 0:
                            act.wait_ge(x_loaded[b], 16)
                        cols = slice(half * 512, (half + 1) * 512)
                        act.activation(H[:, b, cols], X[:, b, cols], ACT.Square,
                                       accum_out=stat[:, 2 * b + half:2 * b + half + 1]).then_inc(squared, 1)

            def turn_high(t, base, gain):
                for k in range(KT):
                    if k % 2 == 0:
                        act.wait_ge(turned, 4 * t + k // 2 + 1)
                    act.activation(hT_hi[:, k, :], bank[base + k // 2][:, (k % 2) * SEQ:(k % 2 + 1) * SEQ], ACT.Copy,
                                   scale=0.5 if gain is None else gain[:, k:k + 1]).then_inc(turned_hi, 1)

            def s5_angles(l):
                a = [s5p[:, i, :] for i in range(20)]
                act.activation(a[0], par(l, "log_dt"), ACT.Exp).then_inc(s5_exp, 1)
                act.wait_ge(s5_arg, 2 * l + 1)
                act.activation(a[1], a[1], ACT.Exp).then_inc(s5_exp, 1)
                act.wait_ge(s5_arg, 2 * l + 2)
                act.activation(a[4], a[3], ACT.Sin).then_inc(s5_sin, 1)
                act.activation(a[5], a[3], ACT.Sin, scale=0.5).then_inc(s5_sin, 1)

            def s5_operands(l):
                act.wait_ge(s5_turned, 2 * l + 1)
                act.activation(BT[:, :, :, :].rearrange("p a b c -> p (a b c)"), bank[6][:, :],
                               ACT.Copy).then_inc(s5_lhs, 1)
                act.wait_ge(s5_turned, 2 * l + 2)
                act.activation(CTt[:, 0, :], bank[7][:, 0:DB], ACT.Copy).then_inc(s5_lhs, 1)
                act.activation(CTt[:, 1, :], bank[7][:, DB:2 * DB], ACT.Copy, scale=-1.0).then_inc(s5_lhs, 1)

            def split_small(l):
                act.wait_ge(router_loaded if l == 2 else params_loaded[l], 16)
                src = RT[:, 0:KT * NE] if l == 2 else par(l, "w_forget")
                act.activation(smallw_hi[:, SMALL[l]], src, ACT.Copy).then_inc(small_hi, 1)

            for l in range(2):
                mix = Units(BASE[l])
                after = Units(DENSE0)
                square_rows(2 * l)
                if l == 1:
                    split_high(mix, 2)
                if l == 0:
                    split_high(mix, 0)
                    split_small(0)
                turn_high(3 * l, 0, par(l, "g_mix"))
                if l == 0:
                    split_high(mix, 1)
                    split_high(mix, 2)
                    split_small(1)
                    split_small(2)
                    act.wait_ge(masks_loaded, 16)
                    act.activation(masks[:, 0:P], ident, ACT.Copy).then_inc(masks_ready, 1)
                    act.activation(masks[:, P:3 * P], M[:, 0, 0:2 * P], ACT.Copy).then_inc(masks_ready, 1)

                act.wait_ge(small_logits, l + 1)
                act.activation(lg_rows[0:NH, :], bank[4][0:NH, 0:SEQ], ACT.Copy).then_inc(small_rows, 1)
                act.wait_ge(forget_in, l + 1)
                step(act.activation(lf[:, 1, :], lf[:, 0, :], ACT.Abs))
                step(act.activation(lf[:, 2, :], lf[:, 1, :], ACT.Exp, scale=-1.0))
                act.activation(lf[:, 3, :], lf[:, 2, :], ACT.Ln, bias=1.0).then_inc(forget_ln, 1)
                if l == 0:
                    s5_angles(0)

                def halves(b):
                    return b[:, :].rearrange("p (a c) -> p a c", a=2)

                def take(i, dst, func=ACT.Copy, scale=1.0):
                    wait_products(act, mix, i)
                    act.activation(dst, halves(bank[PROJ_BANK[i]]), func, scale=scale).then_inc(taken, 1)

                def take_bu(t):
                    act.wait_ge(bu_ready, ST * l + t + 1)
                    act.activation(bu[:, t, :, :], halves(bank[6 + t % 2]), ACT.Copy).then_inc(bu_taken, 1)

                def take_qk(kind, which):
                    if kind or l:
                        act.wait_ge(qk_turned, 2 * (2 * l + kind))
                        act.wait_ge(qk_mean, 2 * (2 * l + kind))
                    take(3 + 3 * kind + which, qk[:, which, :, :])
                    take(3 + 3 * kind + which, sq[:, which, :, :], ACT.Square)

                def root_qk(kind):
                    act.wait_ge(qk_mean, 2 * (2 * l + kind + 1))
                    act.activation(nrm[:, 1, :, :], nrm[:, 0, :, :], ACT.Sqrt).then_inc(qk_root, 1)

                def gain_qk(kind):
                    for which in range(2):
                        act.wait_ge(qk_turned, 2 * (2 * l + kind) + which + 1)
                        b = bank[(6, 7, 5, 4)[2 * kind + which]]
                        g = par(l, ("fox_q", "fox_k", "sb_q", "sb_k")[2 * kind + which])
                        act.activation(qT[:, kind, which, :, :], halves(b), ACT.Copy, scale=g).then_inc(qk_gained, 1)

                def gates(i):
                    n, half = i // 2, i % 2
                    buf = (G2, H)[n % 2]
                    if n >= 2 and half == 0:
                        if n == 2:
                            act.wait_ge(gated, 16 * l + 4)
                        else:
                            act.wait_ge(merged, 12 * l + 4)
                    for b in range(NB):
                        if b == 0:
                            act.wait_ge(gate_ready, 8 * l + i + 1)
                        else:
                            wait_products(act, mix, 10 + 5 * n + 2 * half)
                        act.activation(buf[:, b, half * 512:(half + 1) * 512], bank[2 * half + b][:, :], ACT.Tanh,
                                       scale=0.5).then_inc(gate_tanh, 1)

                def row_exp(h):
                    act.wait_ge(row_max, NH * l + h + 1)
                    if h >= 2:
                        act.wait_ge(p_turned, NH * l + h - 1)
                    act.activation(sc[:, h % 2, 0:P], bank[6 + h % 2][:, 0:P], ACT.Exp, bias=mx[:, 0, h, 0:1],
                                   accum_out=rs[:, 0, h, 0:1]).then_inc(p_exp, 1)
                    act.activation(sc[:, h % 2, P:3 * P], bank[6 + h % 2][:, P:3 * P], ACT.Exp, bias=mx[:, 0, h, 1:2],
                                   accum_out=rs[:, 0, h, 1:2]).then_inc(p_exp, 1)

                def take_p(h):
                    act.wait_ge(p_turned, NH * l + h + 1)
                    if h >= 2:
                        act.wait_ge(fox_out, NH * l + h - 1)
                    act.activation(pT[:, h % 2, :], bank[4][:, 0:3 * P], ACT.Copy).then_inc(p_taken, 1)

                def soft_ln(pair):
                    act.wait_ge(z_ready, NH * l + 2 * pair + 2)
                    for i in range(2):
                        step.mark(act.activation(sc[:, i, :], bank[6 + i][:, 0:3 * P], ACT.Abs))
                    step.settle()
                    step(act.activation(sc[:, :, :], sc[:, :, :], ACT.Exp, scale=-1.0))
                    act.activation(sc[:, :, :], sc[:, :, :], ACT.Ln, bias=1.0).then_inc(z_ln, 1)

                def a_weights(pair):
                    for i in range(2):
                        act.wait_ge(z_cum, NH * l + 2 * pair + i + 1)
                        if pair:
                            act.wait_ge(sb_out, NH * l + 2 * pair)
                        act.activation(pT[:, i, :], bank[6 + i][:, 0:3 * P], ACT.Exp).then_inc(a_exp, 1)

                def ys_split(n, src, ready, count, scale):
                    act.wait_ge(ready, count)
                    if n >= 2:
                        wait_products(act, mix, 13 + 5 * (n - 2))
                    act.activation(ys_hi[:, n % 2, :, :], src, ACT.Copy, scale=scale).then_inc(ys_high, 1)

                for u in range(MIX_UNITS):
                    if u + RING < MIX_UNITS:
                        split_high(mix, u + RING)
                    elif u == MIX_UNITS - 1:
                        pass
                    elif l == 0:
                        split_high(after, u + RING - MIX_UNITS)
                    elif u + RING - MIX_UNITS < 2:
                        for half in range(2):
                            split_half(u + RING - MIX_UNITS, half, 0, 0)
                    if u == 0:
                        if l:
                            act.wait_ge(ys_low, 4 * l)
                        take(0, ca[:, :, :])
                    if u == 1:
                        take(1, cs[:, :, :], ACT.Tanh, 0.5)
                    if u == 2:
                        take(2, uT[:, :, :])
                        s5_operands(l)
                    if u in (3, 4):
                        take_qk(0, u - 3)
                    if u == 5:
                        take(5, V[:, 0, :, :])
                    if u in (3, 4, 5, 6):
                        take_bu(2 * (u - 3))
                        take_bu(2 * (u - 3) + 1)
                    if u == 8:
                        take(8, V[:, 1, :, :])
                        root_qk(0)
                    if u == 9:
                        gain_qk(0)
                        take_qk(1, 0)
                        take_qk(1, 1)
                        act.wait_ge(conv_cent, l + 1)
                        act.activation(cs[:, :, :], ca[:, :, :], ACT.Square).then_inc(conv_sq, 1)
                        root_qk(1)
                    if u == 10:
                        act.wait_ge(conv_vare, l + 1)
                        act.activation(lnv[:, 1, :], lnv[:, 0, :], ACT.Sqrt).then_inc(conv_root, 1)
                        gates(0)
                        row_exp(0)
                    if u == 11:
                        gain_qk(1)
                        row_exp(1)
                        act.wait_ge(conv_lin, l + 1)
                        act.activation(cs[:, :, :], ca[:, :, :], ACT.Tanh, scale=0.5).then_inc(conv_tanh, 1)
                        ys_split(0, ca[:, :, :], conv_out, l + 1, 0.5)
                    if u == 12:
                        gates(1)
                        take_p(0)
                        row_exp(2)
                    if u == 13:
                        take_p(1)
                        row_exp(3)
                    if u == 14:
                        take_p(2)
                    if u == 15:
                        gates(2)
                        take_p(3)
                        soft_ln(0)
                    if u == 16:
                        ys_split(1, halves(bank[5]), fox_out, NH * (l + 1), 1.0)
                        a_weights(0)
                    if u == 17:
                        gates(3)
                        soft_ln(1)
                    if u == 19:
                        a_weights(1)
                    if u == 20:
                        gates(4)
                        ys_split(2, halves(bank[5]), sb_out, NH * (l + 1), 1.0)
                    if u == 22:
                        gates(5)
                    if u == 25:
                        gates(6)
                        act.wait_ge(gelu_in, l + 1)
                        act.activation(cs[:, :, :], halves(tmp[:, 1, :]), ACT.Tanh,
                                       scale=0.7978845608028654).then_inc(gelu_tanh, 1)
                    if u == 26:
                        act.wait_ge(glu_ready, l + 1)
                        act.activation(cs[:, :, :], halves(bank[6]), ACT.Tanh, scale=0.25).then_inc(glu_tanh, 1)
                        ys_split(3, ca[:, :, :], glu_out, l + 1, 0.25)
                    if u == 27:
                        gates(7)
                    if u == MIX_UNITS - 5:
                        turn_high(3 * l + 1, 4, None)
                square_rows(2 * l + 1)
                if l == 0:
                    split_high(after, 2)
                turn_high(3 * l + 2, FFN_TURN_BANK[l], par(l, "g_ffn"))

                if l == 0:
                    s5_angles(1)

                    def hidden(u, j, odd):
                        wait_products(act, u, j)
                        act.activation(silu[:, odd, :, :], halves(bank[2 * odd]), ACT.Silu).then_inc(silu_ready, 1)

                    def hidden_high(c, odd):
                        act.wait_ge(g_ready, c + 1)
                        act.activation(ys_hi[:, odd, :, :], gated_h[:, odd, :, :],
                                       ACT.Copy).then_inc(g_hi, 1)

                    split_high(Units(DENSE0), 3)
                    hidden(Units(DENSE0), 0, 0)
                    split_high(Units(DENSE0), 4)
                    hidden_high(0, 0)

                    def pair(i):
                        u = Units(DENSE0, i * 2)
                        for m in range(2):
                            split_high(u, 5 + 3 * m)
                            hidden(u, 2 + 3 * m, 1 - m)
                            split_high(u, 6 + 3 * m)
                            hidden_high(i * 2 + 1 + m, 1 - m)
                            split_high(u, 7 + 3 * m)

                    with act.Fori(0, PAIRS) as i:
                        pair(i)

            for b in range(NB):
                act.activation(h_parts[0][:, b, :], H[:, b, :], ACT.Copy).then_inc(h_high, 1)
            act.wait_ge(small_logits, 3)
            act.activation(lg_rows[0:NE, :], bank[4][0:NE, 0:SEQ], ACT.Copy).then_inc(small_rows, 1)
            for half in range(2):
                split_half(2, half, 0, 0)
            act.wait_ge(top_gap, 1)
            act.activation(route[:, 10, :, 0:1], route[:, 9, :, 0:1], ACT.Exp).then_inc(top_exp, 1)

            def gather_high(n, i, p, at=7):
                act.wait_ge(gathered, n * 2 + i + 1)
                for k in range(4 * i, 4 * i + 4):
                    ins = act.activation(hT_hi[:, k, p * P:(p + 1) * P], bank[at][:, k % 4 * P:(k % 4 + 1) * P], ACT.Copy,
                                         scale=par(1, "g_ffn", k, k + 1))
                ins.then_inc(gather_hi, 1)

            def take_back(n):
                act.wait_ge(back_turned, n + 1)
                act.activation(back[:, :], bank[7][:, 0:NB * P], ACT.Copy).then_inc(side_done, 1)

            def y_high(n):
                act.wait_ge(moe_used[5], n * NCH + NCH)
                for half in range(2):
                    cols = slice(half * 512, (half + 1) * 512)
                    act.activation(y_parts[0][:, cols], bank[4 + half][:, :], ACT.Copy).then_inc(y_hi, 1)

            def hidden_high(g, odd):
                act.wait_ge(moe_turned, g + 1)
                act.activation(ys_hi[:, odd, 0, :], bank[6][:, 0:CH], ACT.Copy).then_inc(moe_g_hi, 1)

            def turn_of(n, p, carry, more):
                def step(c, odd, last=False):
                    g = n * NCH + c
                    at = c if isinstance(c, int) else None
                    if (at != 0 or carry) and not (isinstance(g, int) and g == 1):
                        for half in range(2):
                            split_half(2, half, g - 1, 1 - odd)
                    if at == 1 and carry:
                        y_high(n - 1)
                    act.wait_ge(moe_used[1], g + 1)
                    act.activation(silu[:, odd, 0, :], bank[2 * odd][:, 0:CH], ACT.Silu).then_inc(moe_silu, 1)
                    if at != 0 or carry:
                        hidden_high(g - 1, 1 - odd)
                    if not last:
                        for half in range(2):
                            split_half(0, half, g + 1, 1 - odd)
                    if at == 0 and carry:
                        take_back(n - 1)
                    if at in (1, 2) and more:
                        gather_high(n + 1, at - 1, 1 - p)
                    if not last:
                        for half in range(2):
                            split_half(1, half, g + 1, 1 - odd)

                for c in range(3):
                    step(c, (p + c) % 2)

                def pair(i, last=False):
                    step(i * 2 + 3, 1 - p)
                    step(i * 2 + 4, p, last)

                with act.Fori(0, 4 if more else 3) as i:
                    pair(i)
                if not more:
                    pair(3, True)

            def finish(n, p):
                g = n * NCH + NCH - 1
                for half in range(2):
                    split_half(2, half, g, p)
                hidden_high(g, p)
                y_high(n)
                take_back(n)

            for i in range(2):
                gather_high(0, i, 0, 7 - i)
            turn_of(0, 0, False, True)
            with act.Fori(0, NE // 2 - 1) as i:
                turn_of(i * 2 + 1, 1, True, True)
                turn_of(i * 2 + 2, 0, True, True)
            turn_of(NE - 1, 1, True, False)
            finish(NE - 1, 1)
            act.wait_ge(spill_known, 1)
            n_spill = act.value_load(spill_i[0:1, 0:1], min_val=0, max_val=N_SPILL)
            for t in range(N_SPILL):
                with act.If(n_spill > t):
                    n, p = NE + t, t % 2
                    for kind in range(2):
                        for half in range(2):
                            split_half(kind, half, n * NCH, p)
                    for i in range(2):
                        gather_high(n, i, p, 7 - i)
                    turn_of(n, p, False, False)
                    finish(n, p)

        @block.vector
        def _(dve):
            step = Chain(dve, dve_step)
            tt, ts, stt = dve.tensor_tensor, dve.tensor_scalar, dve.scalar_tensor_tensor

            def scale_rows(r):
                for b in range(NB):
                    dve.wait_ge(rms_root, 2 * r + b + 1)
                    ts(H[:, b, :], X[:, b, :], stat[:, 6 + b:7 + b], float(D) ** 0.5, ALU.mult, ALU.mult).then_inc(normed, 1)

            def turn_low(t, base, gain):
                for k in range(KT):
                    dve.wait_ge(turned_hi, KT * t + k // 2 * 2 + 2)
                    stt(hT_lo[:, k, :], bank[base + k // 2][:, (k % 2) * SEQ:(k % 2 + 1) * SEQ],
                        0.5 if gain is None else gain[:, k:k + 1], hT_hi[:, k, :].bitcast(F32), ALU.mult,
                        ALU.subtract).then_inc(turned_lo, 1)

            s5a = [s5p[:, i, :] for i in range(20)]
            dt, mag, turn, arg, sin, hsin, t6, _, cos, are, aim, nre, den, kre, kim, t14, t15, t16, pc, ps = s5a

            def s5_angles(l):
                lre, lim = par(l, "lam_re"), par(l, "lam_im")
                dve.wait_ge(s5_exp, 2 * l + 1)
                tt(mag, lre, dt, ALU.mult).then_inc(s5_arg, 1)
                step(tt(turn, lim, dt, ALU.mult))
                step(ts(t6, turn, 1.0 / (2 * np.pi), ROUND, ALU.mult, ALU.add))
                step(ts(t6, t6, ROUND, None, ALU.subtract))
                step(stt(arg, t6, -TWO_PI_1, turn, ALU.mult, ALU.add))
                step(stt(arg, t6, -TWO_PI_2, arg, ALU.mult, ALU.add))
                step(stt(arg, t6, -TWO_PI_3, arg, ALU.mult, ALU.add))
                ts(arg, arg, PI_F32, -PI_F32, ALU.min, ALU.max).then_inc(s5_arg, 1)

            def s5_spread_of(l):
                lre, lim = par(l, "lam_re"), par(l, "lam_im")
                dve.wait_ge(s5_sin, 2 * l + 2)
                step(tt(cos, hsin, hsin, ALU.mult))
                step(ts(cos, cos, -2.0, 1.0, ALU.mult, ALU.add))
                step.mark(tt(are, mag, cos, ALU.mult))
                step.mark(tt(aim, mag, sin, ALU.mult))
                step.mark(tt(den, lre, lre, ALU.mult))
                step(tt(t14, lim, lim, ALU.mult))
                step.mark(ts(nre, are, 1.0, None, ALU.subtract))
                step(tt(den, den, t14, ALU.add))
                step.mark(dve.reciprocal(den, den))
                step.mark(tt(t14, nre, lre, ALU.mult))
                step.mark(tt(t15, aim, lim, ALU.mult))
                step.mark(tt(t16, aim, lre, ALU.mult))
                step(tt(kim, nre, lim, ALU.mult))
                step.mark(tt(t14, t14, t15, ALU.add))
                step(tt(t16, t16, kim, ALU.subtract))
                step.mark(tt(kre, t14, den, ALU.mult))
                step(tt(kim, t16, den, ALU.mult))
                b3 = [tmp[:, i, 0:ST * GH].rearrange("p (t h) -> p t h", h=GH) for i in range(4)]
                bre, bim = (par(l, n).rearrange("p (t h) -> p t h", h=GH) for n in ("b_re", "b_im"))
                kre3, kim3 = (k.unsqueeze(2).to_broadcast([P, ST, GH]) for k in (kre, kim))
                step.mark(tt(b3[0], bre, kre3, ALU.mult))
                step.mark(tt(b3[1], bim, kim3, ALU.mult))
                step.mark(tt(b3[2], bim, kre3, ALU.mult))
                step(tt(b3[3], bre, kim3, ALU.mult))
                step.mark(tt(b3[0], b3[0], b3[1], ALU.subtract))
                step(tt(b3[2], b3[2], b3[3], ALU.add))
                for ri in range(2):
                    for side in range(2):
                        step.mark(ts(s5b[:, ri, :, side, :], b3[2 * ri], const("side", side, side + 1), None, ALU.mult))
                    for side in range(2):
                        c3 = par(l, ("c_re", "c_im")[ri]).rearrange("p (a c) -> p a c", a=CT)
                        ins = ts(s5c[:, ri, :, side, :], c3, const("parity", side, side + 1), None, ALU.mult)
                        if ri == 0 or side == 0:
                            step.mark(ins)
                ins.then_inc(s5_spread, 1)
                step.settle()

            def s5_table_start():
                step.settle()
                step.mark(dve.memset(rot_c[:, :, 0:1], 1.0))
                step.mark(dve.memset(rot_s[:, :, 0:1], 0.0))
                step.mark(dve.tensor_copy(pc, cos))
                step(dve.tensor_copy(ps, sin))

            def s5_double(n, t0=0, t1=ST):
                step.settle()
                c0, s0, c1, s1 = (v[:, t0:t1, at:at + n] for at in (0, n) for v in (rot_c, rot_s))
                pcb, psb = (v[:, t0:t1].unsqueeze(2).to_broadcast([P, t1 - t0, n]) for v in (pc, ps))
                x0, x1 = (tmp[:, i:i + 2, :].rearrange("p a c -> p (a c)")[:, 0:(t1 - t0) * n]
                          .rearrange("p (t n) -> p t n", n=n) for i in (0, 2))
                step.mark(tt(x0, s0, psb, ALU.mult))
                step.mark(tt(x1, c0, psb, ALU.mult))
                step.mark(tt(c1, c0, pcb, ALU.mult))
                step(tt(s1, s0, pcb, ALU.mult))
                step.mark(tt(c1, c1, x0, ALU.subtract))
                step.mark(tt(s1, s1, x1, ALU.add))
                if t1 == ST:
                    step.mark(tt(t14, pc, pc, ALU.mult))
                    step.mark(tt(t15, ps, ps, ALU.mult))
                    step(tt(t16, pc, ps, ALU.mult))
                    step.mark(tt(pc, t14, t15, ALU.subtract))
                    step(ts(ps, t16, 2.0, None, ALU.mult))

            def s5_scan(l, pair):
                t0 = 2 * pair
                dve.wait_ge(bu_taken, ST * l + t0 + 2)
                step.settle()
                if l or pair:
                    dve.wait_ge(s5_state, ST // 2 * l + pair)
                re, im = bu[:, t0:t0 + 2, 0, :], bu[:, t0:t0 + 2, 1, :]
                c, s = rot_c[:, t0:t0 + 2, :], rot_s[:, t0:t0 + 2, :]
                q = [tmp[:, i, :].rearrange("p (a c) -> p a c", a=2) for i in range(4)]
                step.mark(tt(q[0], c, re, ALU.mult))
                step.mark(tt(q[1], s, im, ALU.mult))
                step.mark(tt(q[2], c, im, ALU.mult))
                step(tt(q[3], s, re, ALU.mult))
                step.mark(tt(q[0], q[0], q[1], ALU.add))
                step(tt(q[2], q[2], q[3], ALU.subtract))
                for a in range(2):
                    mag = s5p[:, 1, t0 + a:t0 + a + 1].to_broadcast([P, SEQ])
                    for ri in range(2):
                        ins = dve.tensor_tensor_scan(bu[:, t0 + a, ri, :], mag, q[2 * ri][:, a, :], 0.0, ALU.mult, ALU.add)
                        step.mark(ins)
                step.settle()
                step.mark(tt(q[0], c, re, ALU.mult))
                step.mark(tt(q[1], s, im, ALU.mult))
                step.mark(tt(q[2], c, im, ALU.mult))
                step(tt(q[3], s, re, ALU.mult))
                step.mark(tt(re, q[0], q[1], ALU.subtract))
                tt(im, q[2], q[3], ALU.add).then_inc(s5_state, 1)

            def halves(b):
                return b[:, :].rearrange("p (a c) -> p a c", a=2)

            def split_small(l):
                dve.wait_ge(small_hi, l + 1)
                src = RT[:, 0:KT * NE] if l == 2 else par(l, "w_forget")
                tt(smallw_lo[:, SMALL[l]], src, smallw_hi[:, SMALL[l]].bitcast(F32), ALU.subtract).then_inc(small_lo, 1)

            dve.wait_ge(ident_loaded, 16)
            for l in range(2):
                mix = Units(BASE[l])
                scale_rows(2 * l)
                if l == 0:
                    split_small(0)
                turn_low(3 * l, 0, par(l, "g_mix"))
                dve.wait_ge(small_turned, l + 1)
                f3 = lf[:, 0, :].rearrange("p (b h) -> p b h", b=NB)
                tt(f3, bank[4][:, 0:NB * NH].rearrange("p (b h) -> p b h", b=NB),
                   par(l, "b_forget").unsqueeze(1).to_broadcast([P, NB, NH]), ALU.add).then_inc(forget_in, 1)
                if l == 0:
                    dve.wait_ge(consts_loaded, 16)
                    s5_angles(0)
                    s5_spread_of(0)
                    s5_table_start()
                    for k in range(6):
                        s5_double(2 ** k)
                    split_small(1)
                    split_small(2)
                dve.wait_ge(forget_ln, l + 1)
                dve.wait_ge(forget_in, l + 1)
                step(stt(lf[:, 1, :], lf[:, 0, :], 0.0, lf[:, 3, :], ALU.min, ALU.subtract))
                if l == 0:
                    dve.wait_ge(masks_ready, 2)
                for h in range(NH):
                    for i, (tab, b) in enumerate((("tri", 0), ("ones", 0), ("tri", 1))):
                        ins = ts(TL[:, h, i, :], const(tab), lf[:, 1, b * NH + h:b * NH + h + 1], None, ALU.mult)
                ins.then_inc(forget_tri, 1)

                dve.wait_ge(taken, 13 * l + 2)
                step.mark(dve.memset(upad[:, :, 0:PAD], 0.0))
                step(stt(upad[:, :, PAD:], cs[:, :, :], 1.0, ca[:, :, :], ALU.add, ALU.mult))
                for tap in range(CONVW):
                    for c in range(CT):
                        w = par(l, "conv_w", c * CONVW + tap, c * CONVW + tap + 1)
                        src = upad[:, c, tap:tap + SEQ]
                        if tap == 0:
                            step.mark(ts(ca[:, c, :], src, w, None, ALU.mult))
                        else:
                            step.mark(stt(ca[:, c, :], src, w, ca[:, c, :], ALU.mult, ALU.add))
                    step.settle()
                for c in range(CT):
                    ts(ca[:, c, :], ca[:, c, :], 0.5, par(l, "conv_b", c, c + 1), ALU.mult, ALU.add).then_inc(conv_sum, 1)

                def norm_qk(kind):
                    for which in range(2):
                        dve.wait_ge(taken, 13 * l + (5, 7, 11, 13)[2 * kind + which])
                        step(dve.tensor_reduce(nrm[:, 0, which, :],
                                               sq[:, which, :, :].rearrange("p b (h d) -> p (b h) d", d=HD), AX_X, ALU.add))
                        f = 1.0 if which == 0 else 1.0 / HD
                        ts(nrm[:, 0, which, :], nrm[:, 0, which, :], f, f * HD * EPS, ALU.mult, ALU.add).then_inc(qk_mean, 1)
                    dve.wait_ge(qk_root, 2 * l + kind + 1)
                    dve.wait_ge(qk_mean, 2 * (2 * l + kind + 1))
                    step(dve.reciprocal(nrm[:, 0, :, :], nrm[:, 1, :, :]))
                    for which in range(2):
                        v = qk[:, which, :, :].rearrange("p b (h d) -> p (b h) d", d=HD)
                        tt(v, v, nrm[:, 0, which, :].unsqueeze(2).to_broadcast([P, NB * NH, HD]),
                           ALU.mult).then_inc(qk_normed, 1)

                def ys_split(n, src, scale):
                    dve.wait_ge(ys_high, 4 * l + n + 1)
                    stt(ys_lo[:, n % 2, :, :], src, scale, ys_hi[:, n % 2, :, :].bitcast(F32), ALU.mult,
                        ALU.subtract).then_inc(ys_low, 1)

                def row_max_of(h):
                    dve.wait_ge(score, NH * l + h + 1)
                    b = bank[6 + h % 2]
                    step.mark(dve.tensor_reduce(mx[:, 0, h, 0:1], b[:, 0:P], AX_X, ALU.max, negate=True))
                    dve.tensor_reduce(mx[:, 0, h, 1:2], b[:, P:3 * P], AX_X, ALU.max, negate=True).then_inc(row_max, 1)

                def row_norm(h):
                    dve.wait_ge(p_exp, 2 * (NH * l + h + 1))
                    step(dve.reciprocal(rs[:, 1, h, :], rs[:, 0, h, :]))
                    step.mark(ts(sc[:, h % 2, 0:P], sc[:, h % 2, 0:P], rs[:, 1, h, 0:1], None, ALU.mult))
                    ts(sc[:, h % 2, P:3 * P], sc[:, h % 2, P:3 * P], rs[:, 1, h, 1:2], None, ALU.mult).then_inc(p_norm, 1)

                def soft(pair):
                    dve.wait_ge(z_ln, 2 * l + pair + 1)
                    for i in range(2):
                        step(stt(sc[:, i, :], bank[6 + i][:, 0:3 * P], 0.0, sc[:, i, :], ALU.max, ALU.add))
                        tt(sc[:, i, :], sc[:, i, :], const("keep"), ALU.mult).then_inc(z_soft, 1)

                def apply_gates(n, half):
                    buf = (G2, H)[n % 2]
                    for b in range(NB):
                        cols = slice(half * 512, (half + 1) * 512)
                        if half and b:
                            wait_products(dve, mix, 13 + 5 * n)
                        else:
                            dve.wait_ge(branch, 12 * l + 3 * n + 2 * half + b + 1)
                        dve.wait_ge(gate_tanh, 16 * l + 4 * n + 2 * half + b + 1)
                        if n == 0:
                            stt(M[:, b, cols], buf[:, b, cols], 1.0, bank[2 * half + b][:, :], ALU.add,
                                ALU.mult).then_inc(gated, 1)
                        else:
                            stt(buf[:, b, cols], buf[:, b, cols], 1.0, bank[2 * half + b][:, :], ALU.add,
                                ALU.mult).then_inc(gated, 1)
                            dve.wait_ge(gated, 16 * l + 4 * n + 2 * half + b + 1)
                            if n >= 2:
                                dve.wait_ge(merged, 12 * l + 4 * (n - 2) + 2 * half + b + 1)
                            tt(M[:, b, cols], M[:, b, cols], buf[:, b, cols], ALU.add).then_inc(merged, 1)

                norm_qk(0)
                dve.wait_ge(conv_mean, l + 1)
                dve.wait_ge(conv_sum, 2 * l + 2)
                tt(ca[:, :, :], ca[:, :, :], bank[4][:, 0:SEQ].unsqueeze(1).to_broadcast([P, CT, SEQ]),
                   ALU.subtract).then_inc(conv_cent, 1)
                if l == 0:
                    s5_double(64)
                norm_qk(1)
                dve.wait_ge(conv_var, l + 1)
                ts(lnv[:, 0, :], bank[4][:, SEQ:2 * SEQ], EPS, None, ALU.add).then_inc(conv_vare, 1)
                row_max_of(0)
                dve.wait_ge(conv_root, l + 1)
                step(dve.reciprocal(lnv[:, 0, :], lnv[:, 1, :]))
                dve.wait_ge(conv_cent, l + 1)
                step(tt(ca[:, :, :], ca[:, :, :], lnv[:, 0, :].unsqueeze(1).to_broadcast([P, CT, SEQ]), ALU.mult))
                for c in range(CT):
                    ins = ts(ca[:, c, :], ca[:, c, :], par(l, "ln_g", c, c + 1), par(l, "ln_b", c, c + 1), ALU.mult, ALU.add)
                    if c < CT - 1:
                        step.mark(ins)
                ins.then_inc(conv_lin, 1)
                row_norm(0)
                if l == 0:
                    s5_double(128, 0, ST // 2)
                row_max_of(1)
                dve.wait_ge(conv_tanh, l + 1)
                stt(ca[:, :, :], cs[:, :, :], 1.0, ca[:, :, :], ALU.add, ALU.mult).then_inc(conv_out, 1)
                ys_split(0, ca[:, :, :], 0.5)
                row_norm(1)
                row_max_of(2)
                row_norm(2)
                if l == 0:
                    s5_double(128, ST // 2, ST)
                row_max_of(3)
                apply_gates(0, 0)
                row_norm(3)
                apply_gates(0, 1)
                s5_scan(l, 0)
                soft(0)
                ys_split(1, halves(bank[5]), 1.0)
                s5_scan(l, 1)
                apply_gates(1, 0)
                soft(1)
                apply_gates(1, 1)
                s5_scan(l, 2)
                ys_split(2, halves(bank[5]), 1.0)
                s5_scan(l, 3)
                apply_gates(2, 0)
                apply_gates(2, 1)
                dve.wait_ge(s5_y, l + 1)
                y3, g3, q3 = (halves(tmp[:, i, :]) for i in (0, 1, 2))
                dve.wait_ge(s5_state, ST // 2 * (l + 1))
                for c in range(CT):
                    step.mark(stt(y3[:, c, :], uT[:, c, :], par(l, "s5_d", c, c + 1), halves(bank[4])[:, c, :],
                                  ALU.mult, ALU.add))
                step.settle()
                step(tt(q3, y3, y3, ALU.mult))
                step(ts(q3, q3, 0.044715, 1.0, ALU.mult, ALU.add))
                tt(g3, q3, y3, ALU.mult).then_inc(gelu_in, 1)
                dve.wait_ge(gelu_tanh, l + 1)
                stt(q3, cs[:, :, :], 1.0, y3, ALU.add, ALU.mult).then_inc(gelu_out, 1)
                dve.wait_ge(glu_tanh, l + 1)
                dve.wait_ge(gelu_out, l + 1)
                stt(ca[:, :, :], cs[:, :, :], 1.0, q3, ALU.add, ALU.mult).then_inc(glu_out, 1)
                ys_split(3, ca[:, :, :], 0.25)
                apply_gates(3, 0)
                apply_gates(3, 1)
                turn_low(3 * l + 1, 4, None)

                def add_to_x(r, u, base):
                    for b in range(NB):
                        for half in range(2):
                            i = 2 * b + half
                            if i < 3:
                                dve.wait_ge(last_rows, 3 * r + i + 1)
                            else:
                                wait_products(dve, u, MIX_UNITS - 1)
                            xs = X[:, b, half * 512:(half + 1) * 512]
                            tt(xs, xs, bank[base + 2 * half + b][:, :], ALU.add).then_inc(x_mixed, 1)

                add_to_x(2 * l, mix, 0)
                scale_rows(2 * l + 1)
                turn_low(3 * l + 2, FFN_TURN_BANK[l], par(l, "g_ffn"))
                if l == 0:
                    def hidden(u, j, c, odd):
                        wait_products(dve, u, j)
                        dve.wait_ge(silu_ready, c + 1)
                        tt(gated_h[:, odd, :, :], silu[:, odd, :, :], halves(bank[2 * odd + 1]), ALU.mult).then_inc(g_ready, 1)
                        dve.wait_ge(g_hi, c + 1)
                        tt(ys_lo[:, odd, :, :], gated_h[:, odd, :, :], ys_hi[:, odd, :, :].bitcast(F32),
                           ALU.subtract).then_inc(g_lo, 1)

                    s5_angles(1)
                    hidden(Units(DENSE0), 1, 0, 0)
                    s5_spread_of(1)
                    s5_table_start()
                    for k in range(5):
                        s5_double(2 ** k)
                    hidden(Units(DENSE0), 3, 1, 1)
                    s5_double(32)
                    s5_double(64)
                    hidden(Units(DENSE0), 6, 2, 0)
                    s5_double(128)
                    with dve.Fori(1, PAIRS) as i:
                        for m in range(2):
                            hidden(Units(DENSE0, i * 2), 3 + 3 * m, i * 2 + 1 + m, 1 - m)
                    add_to_x(1, Units(DENSE0), 4)

            r = [route[:, i, :, :] for i in range(12)]
            lg, top, at, one, two, sel, comb, place, w1, gap, e, spare = r
            for b in range(NB):
                dve.wait_ge(h_high, b + 1)
                tt(h_parts[1][:, b, :], H[:, b, :], h_parts[0][:, b, :].bitcast(F32), ALU.subtract).then_inc(h_low, 1)
            dve.wait_ge(small_turned, 3)
            step(tt(lg, bank[4][:, 0:NB * NE].rearrange("p (b e) -> p b e", b=NB),
                    RT[:, KT * NE:].unsqueeze(1).to_broadcast([P, NB, NE]), ALU.add))
            for b in range(NB):
                step.mark(dve.max(top[:, b, :], lg[:, b, :]))
            step.settle()
            for b in range(NB):
                step.mark(dve.max_index(top_at[:, b, :], top[:, b, :], lg[:, b, :]))
            ts_ = tt(gap[:, :, 0:1], top[:, :, 1:2], top[:, :, 0:1], ALU.subtract)
            ts_.then_inc(top_gap, 1)
            step.settle()
            step(dve.tensor_copy(at, top_at[:, :, :]))
            for b in range(NB):
                step.mark(ts(one[:, b, :], const("iota8"), at[:, b, 0:1], None, ALU.is_equal))
                step.mark(ts(two[:, b, :], const("iota8"), at[:, b, 1:2], None, ALU.is_equal))
            step.settle()
            tt(sel, one, two, ALU.add).then_inc(chosen, 1)
            dve.wait_ge(places, 1)
            dve.wait_ge(chosen, 1)
            pb3 = bank[5][:, 0:NB * NE].rearrange("p (b e) -> p b e", b=NB)
            step(stt(place, pb3, 1.0, sel, ALU.add, ALU.mult))
            step(ts(place, place, 1.0, None, ALU.subtract))
            step(ts(spare, place, float(P), None, ALU.subtract))

            def one_hot(dst, e, where, event):
                for b in range(NB):
                    ins = ts(dst[:, b, :], const("iota"), route[:, where, b, bass.ds(e, 1)], None, ALU.is_equal)
                ins.then_inc(event, 1)

            one_hot(picks, 0, 7, picked)

            dve.wait_ge(top_exp, 1)
            step(ts(w1[:, :, 0:1], e[:, :, 0:1], 1.0, None, ALU.add))
            step(dve.reciprocal(w1[:, :, 0:1], w1[:, :, 0:1]))
            step(tt(w1[:, :, 1:2], w1[:, :, 0:1], e[:, :, 0:1], ALU.mult))
            for b in range(NB):
                step(ts(comb[:, b, :], one[:, b, :], w1[:, b, 0:1], None, ALU.mult))
                step(stt(comb[:, b, :], two[:, b, :], w1[:, b, 1:2], comb[:, b, :], ALU.mult, ALU.add))
            s = [spill[0:1, i, :] for i in range(4)]
            step(ts(s[0], bank[5][0:1, NB * NE:(NB + 1) * NE], float(P), None, ALU.is_gt))
            step(dve.tensor_tensor_scan(s[1], const("ones", 0, NE, rows=1), s[0], 0.0, ALU.mult, ALU.add))
            step(dve.tensor_copy(spill_i[0:1, 0:1], s[1][:, NE - 1:NE]))
            for t in range(N_SPILL):
                step(stt(s[2], s[1], float(t + 1), s[0], ALU.is_equal, ALU.mult))
                step(tt(s[2], s[2], const("iota8", rows=1), ALU.mult))
                step(dve.tensor_reduce(s[3][:, t:t + 1], s[2], AX_X, ALU.add))
            dve.tensor_copy(spill_i[0:1, 1:1 + N_SPILL], s[3][:, 0:N_SPILL]).then_inc(spill_known, 1)

            def split_half(kind, half, g, odd):
                i, cols = 2 * kind + half, slice(half * UNIT // 2, (half + 1) * UNIT // 2)
                dve.wait_ge(moe_hi[i], g + 1)
                tt(low[:, kind, cols], (raw, raw_odd)[odd][:, kind, cols], high[:, kind, cols].bitcast(F32),
                   ALU.subtract).then_inc(moe_lo[i], 1)

            def gather_low(n, i, p, at=7):
                dve.wait_ge(gather_hi, n * 2 + i + 1)
                for k in range(4 * i, 4 * i + 4):
                    ins = stt(hT_lo[:, k, p * P:(p + 1) * P], bank[at][:, k % 4 * P:(k % 4 + 1) * P],
                              par(1, "g_ffn", k, k + 1), hT_hi[:, k, p * P:(p + 1) * P].bitcast(F32), ALU.mult,
                              ALU.subtract)
                ins.then_inc(side_done, 1)

            def y_low(n):
                for half in range(2):
                    cols = slice(half * 512, (half + 1) * 512)
                    dve.wait_ge(y_hi, n * 2 + half + 1)
                    tt(y_parts[1][:, cols], bank[4 + half][:, :], y_parts[0][:, cols].bitcast(F32),
                       ALU.subtract).then_inc(y_lo, 1)

            def add_back(n, i, e, at=7):
                dve.wait_ge(spread, n * 4 + i + 1)
                for b in range(NB):
                    xs = X[:, b, bass.ds(i * DB, DB)]
                    ins = stt(xs, bank[at][:, b * DB:(b + 1) * DB], route[:, 6, b, bass.ds(e, 1)], xs, ALU.mult, ALU.add)
                ins.then_inc(side_done, 1)

            def hidden_low(g, odd):
                dve.wait_ge(moe_g_hi, g + 1)
                tt(ys_lo[:, odd, 0, :], bank[6][:, 0:CH], ys_hi[:, odd, 0, :].bitcast(F32),
                   ALU.subtract).then_inc(moe_g_lo, 1)

            def turn_of(n, p, carry, more):
                def step(c, odd, job=None, last=False):
                    g = n * NCH + c
                    at = c if isinstance(c, int) else None
                    if at == 0 and more:
                        one_hot(picks, n + 1, 7, picked)
                    if at == 0 and carry:
                        one_hot(picks_back, n - 1, 7, picked_back)
                    if at == 1 and carry:
                        y_low(n - 1)
                    if at != 0 or carry:
                        hidden_low(g - 1, 1 - odd)
                    if not last:
                        for half in range(2):
                            split_half(0, half, g + 1, 1 - odd)
                    dve.wait_ge(moe_used[3], g + 1)
                    dve.wait_ge(moe_silu, g + 1)
                    tt(gated_h[:, odd, 0, :], silu[:, odd, 0, :], bank[2 * odd + 1][:, 0:CH],
                       ALU.mult).then_inc(moe_gated, 1)
                    if job:
                        job()
                    if at in (1, 2) and more:
                        gather_low(n + 1, at - 1, 1 - p)
                    if not last:
                        for half in range(2):
                            split_half(1, half, g + 1, 1 - odd)

                for c in range(3):
                    step(c, (p + c) % 2)

                def pair(i, last=False):
                    step(i * 2 + 3, 1 - p, (lambda: add_back(n - 1, i, n - 1)) if carry else None)
                    step(i * 2 + 4, p, None, last)

                with dve.Fori(0, 4 if more else 3) as i:
                    pair(i)
                if not more:
                    pair(3, True)

            def finish(n, p, e, where):
                g = n * NCH + NCH - 1
                one_hot(picks_back, e, where, picked_back)
                hidden_low(g, p)
                y_low(n)
                for i in range(4):
                    add_back(n, i, e, END_BANK[i])

            step.settle()
            for i in range(2):
                gather_low(0, i, 0, 7 - i)
            turn_of(0, 0, False, True)
            with dve.Fori(0, NE // 2 - 1) as i:
                turn_of(i * 2 + 1, 1, True, True)
                turn_of(i * 2 + 2, 0, True, True)
            turn_of(NE - 1, 1, True, False)
            finish(NE - 1, 1, NE - 1, 7)
            n_spill = dve.value_load(spill_i[0:1, 0:1], min_val=0, max_val=N_SPILL)
            for t in range(N_SPILL):
                with dve.If(n_spill > t):
                    n, p = NE + t, t % 2
                    e = dve.value_load(spill_i[0:1, 1 + t:2 + t], min_val=0, max_val=NE - 1)
                    dve.wait_ge(stored, 16 * 4)
                    one_hot(picks, e, 11, picked)
                    for i in range(2):
                        gather_low(n, i, p, 7 - i)
                    turn_of(n, p, False, False)
                    finish(n, p, e, 11)
            dve.memset(stat[:, 0:1], 0.0).then_inc(finished, 1)

        @block.tensor
        def _(pe):
            def product(dst, w, m, start, stop):
                pe.matmul(dst, w[0], m[0], start=start, stop=False, skip_group_check=True)
                pe.matmul(dst, w[1], m[0], start=False, stop=False, skip_group_check=True)
                return pe.matmul(dst, w[0], m[1], start=False, stop=stop, skip_group_check=True)

            def parts(s, nk):
                return unit_view(high, s, nk), unit_view(low, s, nk)

            def cut(pair_, *ix):
                return tuple(t[ix] for t in pair_)

            def arrive(u, j):
                s = u.slot(j)
                pe.wait_ge(lo_ready[s], u.earlier(j) + 1)
                return s

            hT = (hT_hi, hT_lo)
            everything = slice(None)

            def turn_tile(src, base, k, b):
                return pe.transpose(bank[base + k // 2][:, k % 2 * SEQ + b * P:k % 2 * SEQ + (b + 1) * P],
                                    src[:, b, k * P:(k + 1) * P], ident)

            def turn_normed(r, base):
                for b in range(NB):
                    pe.wait_ge(normed, NB * r + b + 1)
                    for k in range(KT):
                        ins = turn_tile(H, base, k, b)
                        if b and k % 2:
                            ins.then_inc(turned, 1)

            def turn_merged(half):
                for k in range(half * KT // 2, (half + 1) * KT // 2):
                    for b in range(NB):
                        ins = turn_tile(M, 4, k, b)
                    if k % 2:
                        ins.then_inc(turned, 1)

            def small_product(l, n, t):
                for k in range(KT):
                    pe.wait_ge(turned_lo, KT * t + k + 1)
                    if k == 0:
                        pe.wait_ge(small_lo, l + 1)
                    cols = slice(SMALL[l].start + k * n, SMALL[l].start + (k + 1) * n)
                    ins = product(bank[4][0:n, 0:SEQ], cut((smallw_hi, smallw_lo), everything, cols),
                                  cut(hT, everything, k, everything), k == 0, k == KT - 1)
                ins.then_inc(small_logits, 1)

            def turn_small(l, n):
                pe.wait_ge(small_rows, l + 1)
                for b in range(NB):
                    ins = pe.transpose(bank[4][:, b * n:(b + 1) * n], lg_rows[0:n, b * P:(b + 1) * P], ident[0:n, 0:n])
                ins.then_inc(small_turned, 1)

            def channel_rows(u, j, dst, fresh=None):
                s = arrive(u, j)
                w = parts(s, KT)
                for c in range(2):
                    for k in range(KT):
                        if fresh is not None and c == 0:
                            pe.wait_ge(turned_lo, KT * fresh + k + 1)
                        ins = product(dst[:, c * SEQ:(c + 1) * SEQ], cut(w, everything, k, slice(c * P, (c + 1) * P)),
                                      cut(hT, everything, k, everything), k == 0, k == KT - 1)
                return ins, s

            def token_rows(u, j, dst):
                s = arrive(u, j)
                w = parts(s, KT)
                for b in range(NB):
                    for k in range(KT):
                        ins = product(dst[:, b * DB:(b + 1) * DB], cut(hT, everything, k, slice(b * P, (b + 1) * P)),
                                      cut(w, everything, k, everything), k == 0, k == KT - 1)
                return ins, s

            def wide_rows(u, j, nk, k0, last_k, lhs, dst, events=None, free=None):
                s = arrive(u, j)
                n = UNIT // nk // 512
                w = parts(s, nk)
                for half in range(n):
                    for b in range(NB):
                        if free:
                            free(half, b)
                        for k in range(nk):
                            ins = product(dst(half, b), cut(lhs, everything, k0 + k, slice(b * P, (b + 1) * P)),
                                          cut(w, everything, k, slice(half * 512, (half + 1) * 512)),
                                          k0 + k == 0, k0 + k == last_k)
                        last = half == n - 1 and b == NB - 1
                        if events and not last:
                            ins.then_inc(events, 1)
                return ins, s

            def last_wide_rows(u, j, k0, lhs, base, free=None):
                s = arrive(u, j)
                w = parts(s, 2)
                if free:
                    free(0, 0)
                for b in range(NB):
                    for half in range(2):
                        for k in range(2):
                            ins = product(bank[base + 2 * half + b][:, :],
                                          cut(lhs, everything, k0 + k, slice(b * P, (b + 1) * P)),
                                          cut(w, everything, k, slice(half * 512, (half + 1) * 512)), False, k == 1)
                        if b + half < 2:
                            ins.then_inc(last_rows, 1)
                return ins, s

            pe.wait_ge(ident_loaded, 16)
            for l in range(2):
                U = Units(BASE[l])
                turn_normed(2 * l, 0)
                small_product(l, NH, 3 * l)

                def project(u):
                    if 4 <= u < 8:
                        pe.wait_ge(taken, 13 * l + (1, 2, 3, 5)[u - 4])
                    ins, s = (channel_rows if u < 3 else token_rows)(U, u, bank[PROJ_BANK[u]])
                    ins.then_inc(used[s], 1)

                def s5_operands():
                    pe.wait_ge(s5_spread, l + 1)
                    for ri in range(2):
                        for th in range(CT):
                            ins = pe.transpose(bank[6][:, (2 * ri + th) * P:(2 * ri + th + 1) * P],
                                               s5b[:, ri, 4 * th:4 * th + 4, :, :].rearrange("p t s h -> p (t s h)"), ident)
                    ins.then_inc(s5_turned, 1)
                    for ri in range(2):
                        for th in range(CT):
                            ins = pe.transpose(bank[7][:, (2 * ri + th) * P:(2 * ri + th + 1) * P],
                                               s5c[:, ri, th, :, :].rearrange("p s n -> p (s n)"), ident)
                    ins.then_inc(s5_turned, 1)

                def bu_of(t):
                    n, jj, th = ST * l + t, t % 4, t // 4
                    if t == 0:
                        pe.wait_ge(taken, 13 * l + 3)
                        pe.wait_ge(s5_lhs, 3 * (l + 1))
                    if t >= 2:
                        pe.wait_ge(bu_taken, n - 1)
                    rows = slice(32 * jj, 32 * jj + 32)
                    for ri in range(2):
                        ins = pe.matmul(bank[6 + t % 2][:, ri * SEQ:(ri + 1) * SEQ], BT[rows, ri, th, :], uT[rows, th, :],
                                        start=True, stop=True)
                    ins.then_inc(bu_ready, 1)

                def turn_qk(kind, which):
                    pe.wait_ge(qk_normed, 2 * (2 * l + kind) + which + 1)
                    i = 2 * kind + which
                    if i == 0:
                        pe.wait_ge(bu_taken, ST * (l + 1))
                    if i == 2:
                        pe.wait_ge(taken, 13 * l + 9)
                    if i == 3:
                        pe.wait_ge(conv_vare, l + 1)
                    b5 = bank[(6, 7, 5, 4)[i]]
                    for hp in range(CT):
                        for b in range(NB):
                            ins = pe.transpose(b5[:, hp * SEQ + b * P:hp * SEQ + (b + 1) * P],
                                               qk[:, which, b, hp * P:(hp + 1) * P], ident)
                    ins.then_inc(qk_turned, 1)

                def qk_of(kind, h):
                    r0 = HD * (h % 2)
                    q, k = (qT[r0:r0 + HD, kind, which, h // 2, :] for which in range(2))
                    return q, k

                def fox_scores(h):
                    if h == 0:
                        pe.wait_ge(masks_ready, 2)
                        pe.wait_ge(forget_tri, l + 1)
                        pe.wait_ge(qk_gained, 4 * l + 2)
                    if h >= 2:
                        pe.wait_ge(p_exp, 2 * (NH * l + h - 1))
                    q, k = qk_of(0, h)
                    b = bank[6 + h % 2]
                    mm = lambda o, a, c, st, sp_: pe.matmul(o, a, c, start=st, stop=sp_, skip_group_check=True)
                    mm(b[:, 0:P], q[:, 0:P], k[:, 0:P], True, False)
                    mm(b[:, 0:P], TL[:, h, 0, :], const("later"), False, False)
                    mm(b[:, 0:P], masks[:, 0:P], masks[:, P:2 * P], False, True)
                    mm(b[:, P:3 * P], q[:, P:2 * P], k, True, False)
                    mm(b[:, P:2 * P], TL[:, h, 1, :], const("later"), False, False)
                    both = C[:, CONST["ones"][0]:CONST["later"][1]]
                    mm(b[:, P:3 * P], TL[:, h, 2, :], both, False, False)
                    mm(b[:, 2 * P:3 * P], masks[:, 0:P], masks[:, P:2 * P], False, True).then_inc(score, 1)

                def turn_p(h):
                    pe.wait_ge(p_norm, NH * l + h + 1)
                    if h == 0:
                        pe.wait_ge(qk_gained, 4 * l + 4)
                    else:
                        pe.wait_ge(p_taken, NH * l + h)
                    for i in range(3):
                        ins = pe.transpose(bank[4][:, i * P:(i + 1) * P], sc[:, h % 2, i * P:(i + 1) * P], ident)
                    ins.then_inc(p_turned, 1)

                def attend(kind, h, ready, count, ev):
                    pe.wait_ge(ready, count)
                    if h == 0:
                        if kind == 0:
                            pe.wait_ge(qk_gained, 4 * l + 3)
                        else:
                            pe.wait_ge(ys_low, 4 * l + 2)
                    r0, hp = HD * (h % 2), h // 2
                    o = bank[5][r0:r0 + HD, hp * SEQ:(hp + 1) * SEQ]
                    v = [V[:, kind, b, h * HD:(h + 1) * HD] for b in range(NB)]
                    pe.matmul(o, v[0], pT[:, h % 2, 0:2 * P], start=True, stop=False, skip_group_check=True)
                    pe.matmul(o[:, P:2 * P], v[1], pT[:, h % 2, 2 * P:3 * P], start=False, stop=True,
                              skip_group_check=True).then_inc(ev, 1)

                def fox_attend(h):
                    attend(0, h, p_taken, NH * l + h + 1, fox_out)

                def sb_attend(h):
                    attend(1, h, a_exp, NH * l + h + 1, sb_out)

                def sb_scores(pair):
                    for i in range(2):
                        h = 2 * pair + i
                        if pair == 0:
                            pe.wait_ge(qk_gained, 4 * l + 4)
                            pe.wait_ge(p_exp, 2 * (NH * l + 3 + i))
                        else:
                            pe.wait_ge(a_exp, NH * l + i + 1)
                        q, k = qk_of(1, h)
                        pe.matmul(bank[6 + i][:, 0:2 * P], k[:, 0:P], q, start=True, stop=False, skip_group_check=True)
                        pe.matmul(bank[6 + i][:, 2 * P:3 * P], k[:, P:2 * P], q[:, P:2 * P], start=False, stop=True,
                                  skip_group_check=True).then_inc(z_ready, 1)

                def sb_sums(pair):
                    for i in range(2):
                        pe.wait_ge(z_soft, NH * l + 2 * pair + i + 1)
                        b, s = bank[6 + i], sc[:, i, :]
                        mm = lambda o, a, c: pe.matmul(o, a, c, start=False, stop=False, skip_group_check=True)
                        mm(b[:, 0:2 * P], const("suffix"), s[:, 0:2 * P])
                        mm(b[:, P:2 * P], const("minus"), s[:, 2 * P:3 * P])
                        mm(b[:, 2 * P:3 * P], const("suffix"), s[:, 2 * P:3 * P])
                        mm(b[:, 0:P], masks[:, 0:P], masks[:, 2 * P:3 * P])
                        mm(b[:, 2 * P:3 * P], masks[:, 0:P], masks[:, 2 * P:3 * P]).then_inc(z_cum, 1)

                def conv_stat(which):
                    if which == 0:
                        pe.wait_ge(conv_sum, 2 * l + 2)
                        pe.wait_ge(forget_in, l + 1)
                    else:
                        pe.wait_ge(conv_sq, l + 1)
                    for c in range(CT):
                        ins = pe.matmul(bank[4][:, which * SEQ:(which + 1) * SEQ], const("mean"),
                                        (ca if which == 0 else cs)[:, c, :], start=(c == 0), stop=(c == CT - 1),
                                        skip_group_check=True)
                    ins.then_inc((conv_mean, conv_var)[which], 1)

                def s5_out(pair):
                    pe.wait_ge(s5_state, ST // 2 * l + pair + 1)
                    if pair == 0:
                        pe.wait_ge(p_taken, NH * (l + 1))
                    for t in (2 * pair, 2 * pair + 1):
                        jj, th = t % 4, t // 4
                        o = bank[4][32 * jj:32 * jj + 32, th * SEQ:(th + 1) * SEQ]
                        for ri in range(2):
                            ins = pe.matmul(o, CTt[:, ri, 32 * t:32 * t + 32], bu[:, t, ri, :], start=(ri == 0),
                                            stop=(ri == 1), skip_group_check=True)
                    if pair == 3:
                        ins.then_inc(s5_y, 1)

                def glu():
                    pe.wait_ge(gelu_out, l + 1)
                    pe.wait_ge(a_exp, NH * l + 3)
                    w = par(l, "w_glu").rearrange("p (k c) -> p k c", k=CT)
                    g = tmp[:, 2, :].rearrange("p (a c) -> p a c", a=CT)
                    for c in range(CT):
                        for k in range(CT):
                            ins = pe.matmul(bank[6][:, c * SEQ:(c + 1) * SEQ], w[:, k, c * P:(c + 1) * P], g[:, k, :],
                                            start=(k == 0), stop=(k == CT - 1), skip_group_check=True)
                    ins.then_inc(glu_ready, 1)

                def gates(n, half, kh):
                    if kh == 0:
                        if n == 0:
                            pe.wait_ge(taken, 13 * l + (8, 13)[half])
                    j = 9 + 5 * n + 2 * half + kh

                    def free(_, b):
                        if kh == 0 and n:
                            pe.wait_ge(gated, 16 * l + 4 * (n - 1) + 2 * half + b + 1)

                    ins, s = wide_rows(U, j, 4, 4 * kh, KT - 1, hT, lambda _, b: bank[2 * half + b][:, :],
                                       gate_ready if kh else None, free)
                    ins.then_inc(used[s], 1)

                def branch_rows(n):
                    pe.wait_ge(ys_low, 4 * l + n + 1)
                    ys = (ys_hi[:, n % 2, :, :], ys_lo[:, n % 2, :, :])
                    ins, s = wide_rows(U, 13 + 5 * n, CT, 0, CT - 1, ys, lambda half, b: bank[2 * half + b][:, :], branch,
                                       lambda half, b: pe.wait_ge(gate_tanh, 16 * l + 4 * n + 2 * half + b + 1))
                    ins.then_inc(used[s], 1)

                for u in range(9):
                    project(u)
                    if u == 0:
                        turn_small(l, NH)
                    if u == 2:
                        s5_operands()
                    if 3 <= u <= 6:
                        bu_of(2 * (u - 3))
                        bu_of(2 * (u - 3) + 1)
                gates(0, 0, 0)
                turn_qk(0, 0)
                turn_qk(0, 1)
                conv_stat(0)
                gates(0, 0, 1)
                conv_stat(1)
                fox_scores(0)
                gates(0, 1, 0)
                turn_qk(1, 0)
                turn_qk(1, 1)
                fox_scores(1)
                gates(0, 1, 1)
                turn_p(0)
                fox_scores(2)
                fox_scores(3)
                branch_rows(0)
                fox_attend(0)
                turn_p(1)
                gates(1, 0, 0)
                fox_attend(1)
                turn_p(2)
                gates(1, 0, 1)
                fox_attend(2)
                turn_p(3)
                sb_scores(0)
                gates(1, 1, 0)
                fox_attend(3)
                sb_sums(0)
                gates(1, 1, 1)
                sb_attend(0)
                sb_attend(1)
                sb_scores(1)
                branch_rows(1)
                gates(2, 0, 0)
                sb_sums(1)
                gates(2, 0, 1)
                sb_attend(2)
                sb_attend(3)
                gates(2, 1, 0)
                s5_out(0)
                gates(2, 1, 1)
                s5_out(1)
                branch_rows(2)
                gates(3, 0, 0)
                s5_out(2)
                s5_out(3)
                gates(3, 0, 1)
                gates(3, 1, 0)
                glu()
                gates(3, 1, 1)
                branch_rows(3)

                pe.wait_ge(glu_tanh, l + 1)
                for half in range(2):
                    pe.wait_ge(merged, 12 * l + 10 + 2 * half)
                    turn_merged(half)
                for i in range(4):
                    def free(half, b, i=i):
                        if half == 0 and b == 0:
                            pe.wait_ge(turned_lo, KT * (3 * l + 1) + 2 * i + 2)
                    if i < 3:
                        ins, s = wide_rows(U, 29 + i, 2, 2 * i, KT - 1, hT, lambda half, b: bank[2 * half + b][:, :],
                                           None, free)
                    else:
                        ins, s = last_wide_rows(U, 29 + i, 2 * i, hT, 0, free)
                    ins.then_inc(used[s], 1)

                turn_normed(2 * l + 1, FFN_TURN_BANK[l])
                if l == 0:
                    def hidden(u, j, c, odd, which):
                        fresh = 2 if isinstance(c, int) and c + which == 0 else None
                        ins, s = channel_rows(u, j, bank[2 * odd + which], fresh)
                        ins.then_inc(used[s], 1)

                    def down(u, j, c, odd, first, last):
                        pe.wait_ge(g_lo, c + 1)
                        s = arrive(u, j)
                        w = parts(s, 2)
                        g = (ys_hi[:, odd, :, :], ys_lo[:, odd, :, :])
                        if last:
                            ins, s = last_wide_rows(u, j, 0, g, 4)
                            ins.then_inc(used[s], 1)
                            return
                        for half in range(2):
                            for b in range(NB):
                                for f in range(2):
                                    ins = product(bank[4 + 2 * half + b][:, :],
                                                  cut(g, everything, f, slice(b * P, (b + 1) * P)),
                                                  cut(w, everything, f, slice(half * 512, (half + 1) * 512)),
                                                  first and f == 0, last and f == 1)
                        ins.then_inc(used[s], 1)

                    u = Units(DENSE0)
                    hidden(u, 0, 0, 0, 0)
                    hidden(u, 1, 0, 0, 1)

                    def pair(i, first):
                        u = Units(DENSE0, i * 2)
                        for m in range(2):
                            c, odd = i * 2 + 1 + m, 1 - m
                            if not (first and m == 0):
                                pe.wait_ge(g_ready, c - 1)
                            hidden(u, 2 + 3 * m, c, odd, 0)
                            hidden(u, 3 + 3 * m, c, odd, 1)
                            down(u, 4 + 3 * m, i * 2 + m, m, first and m == 0, False)

                    pair(0, True)
                    with pe.Fori(1, PAIRS) as i:
                        pair(i, False)
                    down(Units(DENSE0), FFN_UNITS - 1, NCH - 1, 0, False, True)

            small_product(2, NE, 5)
            turn_small(2, NE)
            pe.wait_ge(chosen, 1)
            sel = route[:, 5, :, :]
            pe.matmul(bank[5][:, 0:NE], const("tri_strict"), sel[:, 0, :], start=True, stop=True)
            pe.matmul(bank[5][:, NE:2 * NE], const("tri_strict"), sel[:, 1, :], start=True, stop=False,
                      skip_group_check=True)
            pe.matmul(bank[5][:, NE:2 * NE], const("ones"), sel[:, 0, :], start=False, stop=True, skip_group_check=True)
            pe.matmul(bank[5][:, 2 * NE:3 * NE], const("ones"), sel[:, 0, :], start=True, stop=False,
                      skip_group_check=True)
            pe.matmul(bank[5][:, 2 * NE:3 * NE], const("ones"), sel[:, 1, :], start=False, stop=True,
                      skip_group_check=True).then_inc(places, 1)

            def gather(n, i, free, to=7):
                pe.wait_ge(picked, n + 1)
                if free is not None:
                    pe.wait_ge(side_done, free)
                for k in range(4 * i, 4 * i + 4):
                    for b in range(NB):
                        for part in range(2):
                            ins = pe.matmul(bank[to][:, k % 4 * P:(k % 4 + 1) * P], h_parts[part][:, b, k * P:(k + 1) * P],
                                            picks[:, b, :], start=(b + part == 0), stop=(b + part == NB),
                                            skip_group_check=True)
                ins.then_inc(gathered, 1)

            def turn_back(n, free):
                pe.wait_ge(picked_back, n + 1)
                pe.wait_ge(side_done, free)
                for b in range(NB):
                    ins = pe.transpose(bank[7][:, b * P:(b + 1) * P], picks_back[:, b, :], ident)
                ins.then_inc(back_turned, 1)

            def spread_rows(n, i, free, to=7):
                pe.wait_ge(y_lo, n * 2 + 2)
                pe.wait_ge(side_done, free)
                for b in range(NB):
                    for part in range(2):
                        ins = pe.matmul(bank[to][:, b * DB:(b + 1) * DB], back[:, b * P:(b + 1) * P],
                                        y_parts[part][:, bass.ds(i * DB, DB)], start=(part == 0), stop=(part == 1),
                                        skip_group_check=True)
                ins.then_inc(spread, 1)

            def hidden(g, odd, which, p, rows=None):
                w = parts(which, KT)
                for k in range(KT):
                    if k % (KT // 2) == 0:
                        half = k // (KT // 2)
                        pe.wait_ge(moe_lo[2 * which + half], g + 1)
                        if half and rows:
                            pe.wait_ge(side_done, rows)
                    ins = product(bank[2 * odd + which][:, 0:CH], cut(hT, everything, k, slice(p * P, (p + 1) * P)),
                                  cut(w, everything, k, everything), k == 0, k == KT - 1)
                    if k % (KT // 2) == KT // 2 - 1:
                        ins.then_inc(moe_used[2 * which + half], 1)

            def turn_hidden(g, odd):
                pe.wait_ge(moe_gated, g + 1)
                for f in range(2):
                    ins = pe.transpose(bank[6][:, f * P:(f + 1) * P], gated_h[:, odd, 0, f * P:(f + 1) * P], ident)
                ins.then_inc(moe_turned, 1)

            def down(g, odd, first, last):
                pe.wait_ge(moe_g_lo, g + 1)
                w = parts(2, 2)
                h = (ys_hi[:, odd, 0, :], ys_lo[:, odd, 0, :])
                for f in range(2):
                    pe.wait_ge(moe_lo[4 + f], g + 1)
                    for half in range(2):
                        ins = product(bank[4 + half][:, :], cut(h, everything, slice(f * P, (f + 1) * P)),
                                      cut(w, everything, f, slice(half * 512, (half + 1) * 512)),
                                      first and f == 0, last and f == 1)
                    ins.then_inc(moe_used[4 + f], 1)

            def turn_of(n, p, carry, more, free):
                def step(c, odd, job=None):
                    g = n * NCH + c
                    at = c if isinstance(c, int) else None
                    if at == 0:
                        pe.wait_ge(side_done, free if carry else free - 1)
                    if not (isinstance(g, int) and g < 2):
                        pe.wait_ge(moe_gated, g - 1)
                    hidden(g, odd, 0, p, free if at == 0 and not carry else None)
                    if at != 0 or carry:
                        turn_hidden(g - 1, 1 - odd)
                    hidden(g, odd, 1, p)
                    if at == 0 and carry:
                        turn_back(n - 1, free)
                    if at in (1, 2) and more:
                        gather(n + 1, at - 1, free + carry + at - 1)
                    if job:
                        job()
                    if at == 1 and carry:
                        pe.wait_ge(y_lo, n * 2)
                    if at != 0 or carry:
                        down(g - 1, 1 - odd, at == 1, at == 0)

                for c in range(3):
                    step(c, (p + c) % 2)
                with pe.Fori(0, 4) as i:
                    step(i * 2 + 3, 1 - p, (lambda: spread_rows(n - 1, i, free + 1 + 2 * more + i)) if carry else None)
                    step(i * 2 + 4, p)

            def finish(n, p, free):
                g = n * NCH + NCH - 1
                turn_hidden(g, p)
                turn_back(n, free)
                down(g, p, False, True)
                for i in range(4):
                    spread_rows(n, i, free + 1, END_BANK[i])

            pe.wait_ge(h_low, NB)
            for i in range(2):
                gather(0, i, None, 7 - i)
            turn_of(0, 0, False, True, 2)
            with pe.Fori(0, NE // 2 - 1) as i:
                for m in range(2):
                    n = i * 2 + 1 + m
                    turn_of(n, 1 - m, True, True, n * 7 - 3)
            turn_of(NE - 1, 1, True, False, (NE - 1) * 7 - 3)
            finish(NE - 1, 1, NE * 7 - 5)
            pe.wait_ge(spill_known, 1)
            n_spill = pe.value_load(spill_i[0:1, 0:1], min_val=0, max_val=N_SPILL)
            for t in range(N_SPILL):
                with pe.If(n_spill > t):
                    n, p = NE + t, t % 2
                    for i in range(2):
                        gather(n, i, n * 7, 7 - i)
                    turn_of(n, p, False, False, n * 7 + 2)
                    finish(n, p, n * 7 + 2)


def constants():
    i = np.arange(P)
    row, col = i[:, None], i[None, :]
    t = {
        "ident": row == col, "power": np.full((P, 1), -0.5), "tri": row <= col, "tri_strict": row < col, "ones": np.ones((P, P)),
        "later": row > col, "suffix": -1.0 * (row >= col), "minus": -np.ones((P, P)), "mean": np.full((P, P), 1.0 / DB),
        "causal": np.where(col > row, -BIG, 0.0), "past": np.where(row < col, 0.0, -BIG),
        "keep": np.concatenate([row < col, np.ones((P, P)), row < col], axis=1),
        "iota": np.broadcast_to(col, (P, P)), "parity": np.stack([(i // GH) % 2 == 0, (i // GH) % 2 == 1], axis=1),
        "side": np.stack([i < GP, i >= GP], axis=1), "iota8": np.broadcast_to(np.arange(NE), (P, NE)),
    }
    out = np.zeros((P, N_CONST), np.float32)
    for name, (a, b) in CONST.items():
        out[:, a:b] = t[name]
    return out


def lay_out(a):
    def cols(v):
        return v.reshape(-1, P).T

    def rows(v):
        return np.broadcast_to(v, (P, v.size))

    def state(v):
        return v.reshape(ST, 2, GP).transpose(1, 2, 0).reshape(P, ST)

    params = []
    for l in range(2):
        t = {
            "g_mix": cols(a["g_mix"][l]), "g_ffn": cols(a["g_ffn"][l]), "b_forget": rows(a["b_forget"][l]),
            "lam_re": state(a["s5_lam_re"][l]), "lam_im": state(a["s5_lam_im"][l]),
            "log_dt": state(np.broadcast_to(a["s5_log_dt"][l][:, None], (NG, GP))),
            "s5_d": cols(a["s5_d"][l]), "conv_b": cols(a["conv_b"][l]), "ln_g": cols(a["conv_ln_g"][l]),
            "ln_b": cols(a["conv_ln_b"][l]),
            "conv_w": a["conv_w"][l].reshape(CONVW, CT, P).transpose(2, 1, 0).reshape(P, CT * CONVW),
            "w_glu": a["s5_w_glu"][l].reshape(CT, P, DB).transpose(1, 0, 2).reshape(P, CT * DB),
            "w_forget": a["w_in"][l][:, IN_F:IN_F + NH].reshape(KT, P, NH).transpose(1, 0, 2).reshape(P, KT * NH),
        }
        for n in ("fox_q", "fox_k", "sb_q", "sb_k"):
            t[n] = cols(np.tile(a[n + "_gain"][l], P // HD))
        for n in ("b_re", "b_im"):
            t[n] = a["s5_" + n][l].reshape(ST, 2, GP, GH).transpose(1, 2, 0, 3).reshape(P, ST * GH)
        for n in ("c_re", "c_im"):
            t[n] = a["s5_" + n][l].reshape(CT, P, GP).transpose(1, 0, 2).reshape(P, CT * GP)
        params += [t[n] for n in PARAM]
    router = [a["router_w"][0].reshape(KT, P, NE).transpose(1, 0, 2).reshape(P, KT * NE), rows(a["router_b"][0])]
    return np.concatenate(params, axis=1), np.concatenate(router, axis=1)


BIG_INPUTS = ["x", "w_in", "w_branch", "w_out", "ffn_w1", "ffn_w3", "ffn_w2", "moe_w1", "moe_w3", "moe_w2"]


def kernel(**inputs):
    import concourse.bacc as bacc
    from concourse.bass_utils import run_bass_kernel_spmd

    a = {k: np.ascontiguousarray(v) for k, v in inputs.items()}
    arrays = {n: a[n] for n in BIG_INPUTS}
    arrays["consts"] = constants()
    arrays["params"], arrays["router"] = (np.ascontiguousarray(t) for t in lay_out(a))
    nc = bacc.Bacc("TRN2", target_bir_lowering=False, num_devices=1, dynamic_dma_scratch_size=1024)
    aps = {n: nc.dram_tensor(n + "_dram", v.shape, mybir.dt.from_np(v.dtype), kind="ExternalInput").ap()
           for n, v in arrays.items()}
    out = nc.dram_tensor("out_dram", a["x"].shape, F32, kind="ExternalOutput").ap()
    build(nc, out=out, **aps)
    r = run_bass_kernel_spmd(nc, [{n + "_dram": v for n, v in arrays.items()}], core_ids=[0])
    return r.results[0]["out_dram"]
```
